# Optimizing a Trainium2 kernel written in Bass

```python
import math
import jax, jax.numpy as jnp
from jax import lax
import numpy as np

D_MODEL = 1024
BATCH = 1
SEQ = 1024
DEPTH = 2

CHUNK = 64
Q_BLOCK = 128
A_WIDTH = D_MODEL // 2
CONV_WIDTH = 31
B_WIDTH = D_MODEL // 2
LRU_BLOCKS = 8
LRU_BLOCK_DIM = B_WIDTH // LRU_BLOCKS
LRU_CONV_WIDTH = 4
LRU_C = 8.0
IN_WIDTH = 2 * A_WIDTH + 2 * B_WIDTH
DIFF_HEADS = D_MODEL // 128
DIFF_HEAD_DIM = 64
DIFF_V_DIM = 2 * DIFF_HEAD_DIM
QK_WIDTH = DIFF_HEADS * 2 * DIFF_HEAD_DIM
V_WIDTH = DIFF_HEADS * DIFF_V_DIM
ROPE_THETA = 10000.0
D_FF = ((8 * D_MODEL // 3 + 255) // 256) * 256
LN_EPS = 1e-5
DN_ALPHA = (2 * DEPTH) ** 0.25
DN_BETA = (8 * DEPTH) ** -0.25
N_EVEN = (DEPTH + 1) // 2
N_ODD = DEPTH // 2
NEG_INF = -1e30


def layer_norm(x, g, b):
    xf = x.astype(jnp.float32)
    mu = jnp.mean(xf, axis=-1, keepdims=True)
    var = jnp.mean(jnp.square(xf - mu), axis=-1, keepdims=True)
    return ((xf - mu) * lax.rsqrt(var + LN_EPS)).astype(x.dtype) * g + b

def rms_norm(x, g):
    xf = x.astype(jnp.float32)
    return (xf * lax.rsqrt(jnp.mean(jnp.square(xf), axis=-1, keepdims=True) + LN_EPS)).astype(x.dtype) * g

def causal_depthwise_conv(x, w, b):
    k, c = w.shape
    y = lax.conv_general_dilated(x, w[:, None, :].astype(x.dtype), window_strides=(1,),
                                 padding=[(k - 1, 0)], dimension_numbers=('NWC', 'WIO', 'NWC'),
                                 feature_group_count=c)
    return y + b

def _linear_recurrence_combine(c1, c2):
    a1, u1 = c1
    a2, u2 = c2
    return a1 * a2, a2 * u1 + u2

def rg_lru(x, w_a, b_a, w_x, b_x, lam):
    bsz, seq, width = x.shape
    xb = x.reshape(bsz, seq, LRU_BLOCKS, LRU_BLOCK_DIM)
    gate_r = jax.nn.sigmoid((jnp.einsum('bsgi,gij->bsgj', xb, w_a).reshape(bsz, seq, width) + b_a).astype(jnp.float32))
    gate_i = jax.nn.sigmoid((jnp.einsum('bsgi,gij->bsgj', xb, w_x).reshape(bsz, seq, width) + b_x).astype(jnp.float32))
    log_a = -LRU_C * gate_r * jax.nn.softplus(-lam.astype(jnp.float32))
    a = jnp.exp(log_a)
    u = jnp.sqrt(-jnp.expm1(2.0 * log_a)) * (gate_i * x.astype(jnp.float32))
    _, h = lax.associative_scan(_linear_recurrence_combine, (a, u), axis=1)
    return h.astype(x.dtype)

def conv_lru_mixer(x, w_in, b_in, conv_w, conv_b, cnorm_g, cnorm_b, lru_conv_w, lru_conv_b,
                   w_a, b_a, w_x, b_x, lru_lambda, w_out):
    h = x @ w_in + b_in
    a_val = h[..., :A_WIDTH]
    a_gate = h[..., A_WIDTH:2 * A_WIDTH]
    b_gate = h[..., 2 * A_WIDTH:2 * A_WIDTH + B_WIDTH]
    b_rec = h[..., 2 * A_WIDTH + B_WIDTH:]
    ya = jax.nn.silu(layer_norm(causal_depthwise_conv(a_val * jax.nn.sigmoid(a_gate), conv_w, conv_b),
                                cnorm_g, cnorm_b))
    yb = rg_lru(causal_depthwise_conv(b_rec, lru_conv_w, lru_conv_b), w_a, b_a, w_x, b_x, lru_lambda) \
        * jax.nn.gelu(b_gate)
    return jnp.concatenate([ya, yb], axis=-1) @ w_out

def rotate_half(t):
    half = t.shape[-1] // 2
    return jnp.concatenate([-t[..., half:], t[..., :half]], axis=-1)

def diff_attention_mixer(x, w_qkv, lq1, lk1, lq2, lk2, subln_g, w_out, lambda_init):
    bsz, seq, _ = x.shape
    qkv = x @ w_qkv
    q = qkv[..., :QK_WIDTH].reshape(bsz, seq, DIFF_HEADS, 2, DIFF_HEAD_DIM)
    k = qkv[..., QK_WIDTH:2 * QK_WIDTH].reshape(bsz, seq, DIFF_HEADS, 2, DIFF_HEAD_DIM)
    v = qkv[..., 2 * QK_WIDTH:].reshape(bsz, seq, DIFF_HEADS, DIFF_V_DIM)
    pos = jnp.arange(seq, dtype=jnp.float32)
    inv_freq = ROPE_THETA ** (-jnp.arange(0, DIFF_HEAD_DIM, 2, dtype=jnp.float32) / DIFF_HEAD_DIM)
    ang = pos[:, None] * inv_freq[None, :]
    ang = jnp.concatenate([ang, ang], axis=-1)
    cos = jnp.cos(ang).astype(x.dtype)[:, None, None, :]
    sin = jnp.sin(ang).astype(x.dtype)[:, None, None, :]
    q = (q * cos + rotate_half(q) * sin) * (DIFF_HEAD_DIM ** -0.5)
    k = k * cos + rotate_half(k) * sin
    q = q.transpose(0, 2, 3, 1, 4)
    k = k.transpose(0, 2, 3, 1, 4)
    v = v.transpose(0, 2, 1, 3)
    lam = (jnp.exp(jnp.sum(lq1.astype(jnp.float32) * lk1.astype(jnp.float32)))
           - jnp.exp(jnp.sum(lq2.astype(jnp.float32) * lk2.astype(jnp.float32))) + lambda_init)
    chunk_id = jnp.arange(seq) // CHUNK
    outs = []
    for qb in range(seq // Q_BLOCK):
        s0, s1 = qb * Q_BLOCK, (qb + 1) * Q_BLOCK
        scores = jnp.einsum('bhmqd,bhmkd->bhmqk', q[:, :, :, s0:s1], k[:, :, :, :s1],
                            preferred_element_type=jnp.float32)
        mask = chunk_id[s0:s1, None] >= chunk_id[None, :s1]
        p = jax.nn.softmax(jnp.where(mask, scores, NEG_INF), axis=-1)
        attn = p[:, :, 0] - lam * p[:, :, 1]
        outs.append(jnp.einsum('bhqk,bhkd->bhqd', attn.astype(v.dtype), v[:, :, :s1]))
    o = jnp.concatenate(outs, axis=2)
    o = rms_norm(o, subln_g) * (1.0 - lambda_init)
    o = o.transpose(0, 2, 1, 3).reshape(bsz, seq, V_WIDTH)
    return o @ w_out

def swiglu(x, w_gate, w_up, w_down):
    return (jax.nn.silu(x @ w_gate) * (x @ w_up)) @ w_down

def first_inputs(seed: int = 0) -> dict:
    key = jax.random.key(seed)
    ks = iter(jax.random.split(key, 40))
    f32 = jnp.float32

    def nrm(shape, scale):
        return scale * jax.random.normal(next(ks), shape, f32)

    def gain(shape):
        return 1.0 + nrm(shape, 0.02)

    a_pow = jax.random.uniform(next(ks), (N_EVEN, B_WIDTH), f32, minval=0.9, maxval=0.999)
    a0 = a_pow ** (1.0 / LRU_C)
    lru_lambda = jnp.log(a0) - jnp.log1p(-a0)
    return {
        'x': nrm((BATCH, SEQ, D_MODEL), 1.0),
        'even_w_in': nrm((N_EVEN, D_MODEL, IN_WIDTH), D_MODEL ** -0.5),
        'even_b_in': nrm((N_EVEN, IN_WIDTH), 0.01),
        'even_conv_w': nrm((N_EVEN, CONV_WIDTH, A_WIDTH), CONV_WIDTH ** -0.5),
        'even_conv_b': nrm((N_EVEN, A_WIDTH), 0.01),
        'even_cnorm_g': gain((N_EVEN, A_WIDTH)),
        'even_cnorm_b': nrm((N_EVEN, A_WIDTH), 0.01),
        'even_lru_conv_w': nrm((N_EVEN, LRU_CONV_WIDTH, B_WIDTH), LRU_CONV_WIDTH ** -0.5),
        'even_lru_conv_b': nrm((N_EVEN, B_WIDTH), 0.01),
        'even_w_a': nrm((N_EVEN, LRU_BLOCKS, LRU_BLOCK_DIM, LRU_BLOCK_DIM), LRU_BLOCK_DIM ** -0.5),
        'even_b_a': nrm((N_EVEN, B_WIDTH), 0.01),
        'even_w_x': nrm((N_EVEN, LRU_BLOCKS, LRU_BLOCK_DIM, LRU_BLOCK_DIM), LRU_BLOCK_DIM ** -0.5),
        'even_b_x': nrm((N_EVEN, B_WIDTH), 0.01),
        'even_lru_lambda': lru_lambda,
        'even_w_out': nrm((N_EVEN, A_WIDTH + B_WIDTH, D_MODEL), DN_BETA * (A_WIDTH + B_WIDTH) ** -0.5),
        'odd_w_qkv': nrm((N_ODD, D_MODEL, 2 * QK_WIDTH + V_WIDTH), D_MODEL ** -0.5),
        'odd_lambda_q1': nrm((N_ODD, DIFF_HEAD_DIM), 0.1),
        'odd_lambda_k1': nrm((N_ODD, DIFF_HEAD_DIM), 0.1),
        'odd_lambda_q2': nrm((N_ODD, DIFF_HEAD_DIM), 0.1),
        'odd_lambda_k2': nrm((N_ODD, DIFF_HEAD_DIM), 0.1),
        'odd_subln_g': gain((N_ODD, DIFF_V_DIM)),
        'odd_w_out': nrm((N_ODD, V_WIDTH, D_MODEL), DN_BETA * V_WIDTH ** -0.5),
        'mix_ln_g': gain((DEPTH, D_MODEL)),
        'mix_ln_b': nrm((DEPTH, D_MODEL), 0.01),
        'ffn_w_gate': nrm((DEPTH, D_MODEL, D_FF), D_MODEL ** -0.5),
        'ffn_w_up': nrm((DEPTH, D_MODEL, D_FF), D_MODEL ** -0.5),
        'ffn_w_down': nrm((DEPTH, D_FF, D_MODEL), DN_BETA * D_FF ** -0.5),
        'ffn_ln_g': gain((DEPTH, D_MODEL)),
        'ffn_ln_b': nrm((DEPTH, D_MODEL), 0.01),
    }

def first_block(x, even_w_in, even_b_in, even_conv_w, even_conv_b, even_cnorm_g, even_cnorm_b,
              even_lru_conv_w, even_lru_conv_b, even_w_a, even_b_a, even_w_x, even_b_x,
              even_lru_lambda, even_w_out, odd_w_qkv, odd_lambda_q1, odd_lambda_k1,
              odd_lambda_q2, odd_lambda_k2, odd_subln_g, odd_w_out, mix_ln_g, mix_ln_b,
              ffn_w_gate, ffn_w_up, ffn_w_down, ffn_ln_g, ffn_ln_b):
    for layer in range(DEPTH):
        if layer % 2 == 0:
            e = layer // 2
            y = conv_lru_mixer(x, even_w_in[e], even_b_in[e], even_conv_w[e], even_conv_b[e],
                               even_cnorm_g[e], even_cnorm_b[e], even_lru_conv_w[e], even_lru_conv_b[e],
                               even_w_a[e], even_b_a[e], even_w_x[e], even_b_x[e],
                               even_lru_lambda[e], even_w_out[e])
        else:
            o = layer // 2
            lambda_init = 0.8 - 0.6 * math.exp(-0.3 * layer)
            y = diff_attention_mixer(x, odd_w_qkv[o], odd_lambda_q1[o], odd_lambda_k1[o],
                                     odd_lambda_q2[o], odd_lambda_k2[o], odd_subln_g[o],
                                     odd_w_out[o], lambda_init)
        x = layer_norm(DN_ALPHA * x + y, mix_ln_g[layer], mix_ln_b[layer])
        x = layer_norm(DN_ALPHA * x + swiglu(x, ffn_w_gate[layer], ffn_w_up[layer], ffn_w_down[layer]),
                       ffn_ln_g[layer], ffn_ln_b[layer])
    return x


DEPTH_2 = 1

N_MLSTM_HEADS = 4
MLSTM_WIDTH = D_MODEL // 2
V_HEAD_DIM = MLSTM_WIDTH // N_MLSTM_HEADS
QK_HEAD_DIM = V_HEAD_DIM // 2
QK_WIDTH_2 = N_MLSTM_HEADS * QK_HEAD_DIM
N_GATES = 4 * N_MLSTM_HEADS
CHUNK_2 = 128
N_FOURIER_GROUPS = 4
FOURIER_WIDTH = D_MODEL - MLSTM_WIDTH
FOURIER_GROUP_DIM = FOURIER_WIDTH // N_FOURIER_GROUPS
MIX_WIDTH = MLSTM_WIDTH + FOURIER_WIDTH
IN_SPLITS = [QK_WIDTH_2, QK_WIDTH_2, MLSTM_WIDTH, MLSTM_WIDTH, FOURIER_WIDTH, N_GATES]
IN_COLS = sum(IN_SPLITS)
D_FF_2 = 4 * D_MODEL
N_MOD = 6
ALPHA = (2 * DEPTH_2) ** 0.25
BETA = (8 * DEPTH_2) ** -0.25


def _ln_plain(x):
    xf = x.astype(jnp.float32)
    mu = xf.mean(-1, keepdims=True)
    var = jnp.square(xf - mu).mean(-1, keepdims=True)
    return ((xf - mu) * lax.rsqrt(var + LN_EPS)).astype(x.dtype)

def _ln_affine(x, g, b):
    xf = x.astype(jnp.float32)
    mu = xf.mean(-1, keepdims=True)
    var = jnp.square(xf - mu).mean(-1, keepdims=True)
    y = (xf - mu) * lax.rsqrt(var + LN_EPS) * g.astype(jnp.float32) + b.astype(jnp.float32)
    return y.astype(x.dtype)

def _mlstm_chunkwise(q, k, v, log_i, log_f):
    B, H, S, dk = q.shape
    dv = v.shape[-1]
    nc = S // CHUNK_2

    def to_chunks(a):
        return jnp.moveaxis(a.reshape((B, H, nc, CHUNK_2) + a.shape[3:]), 2, 0)

    xs = tuple(to_chunks(a) for a in (q, k, v, log_i, log_f))
    lower = jnp.tril(jnp.ones((CHUNK_2, CHUNK_2), dtype=bool))

    def step(carry, blk):
        C, n, m = carry
        qb, kb, vb, ib, fb = blk
        b = jnp.cumsum(fb, axis=-1)
        D = jnp.where(lower, b[..., :, None] - b[..., None, :] + ib[..., None, :], -jnp.inf)
        inter = b + m[..., None]
        m_t = jnp.maximum(inter, D.max(-1))
        w_intra = jnp.exp(D - m_t[..., None])
        w_inter = jnp.exp(inter - m_t)
        s = jnp.einsum('bhtd,bhsd->bhts', qb, kb) * w_intra
        num = jnp.einsum('bhts,bhsv->bhtv', s, vb) + w_inter[..., None] * jnp.einsum('bhtd,bhdv->bhtv', qb, C)
        den = s.sum(-1) + w_inter * jnp.einsum('bhtd,bhd->bht', qb, n)
        h = num / jnp.maximum(jnp.abs(den), jnp.exp(-m_t))[..., None]
        bL = b[..., -1]
        g = bL[..., None] - b + ib
        m_new = jnp.maximum(bL + m, g.max(-1))
        wk = jnp.exp(g - m_new[..., None])
        decay = jnp.exp(bL + m - m_new)
        C_new = decay[..., None, None] * C + jnp.einsum('bhs,bhsd,bhsv->bhdv', wk, kb, vb)
        n_new = decay[..., None] * n + jnp.einsum('bhs,bhsd->bhd', wk, kb)
        return (C_new, n_new, m_new), h

    init = (jnp.zeros((B, H, dk, dv), jnp.float32), jnp.zeros((B, H, dk), jnp.float32),
            jnp.zeros((B, H), jnp.float32))
    _, hs = lax.scan(step, init, xs)
    return jnp.moveaxis(hs, 0, 2).reshape(B, H, S, dv)

def _mlstm_group(q, k, v, o, gates, b_gate, norm_w):
    B, S, _ = q.shape
    H = N_MLSTM_HEADS
    f32 = jnp.float32
    qh = q.astype(f32).reshape(B, S, H, QK_HEAD_DIM).transpose(0, 2, 1, 3) * (QK_HEAD_DIM ** -0.5)
    kh = k.astype(f32).reshape(B, S, H, QK_HEAD_DIM).transpose(0, 2, 1, 3)
    vh = v.astype(f32).reshape(B, S, H, V_HEAD_DIM).transpose(0, 2, 1, 3)
    gt = (gates.astype(f32) + b_gate.astype(f32)).reshape(B, S, 4, H).transpose(2, 0, 3, 1)
    log_i_f, log_f_f = gt[0], jax.nn.log_sigmoid(gt[1])
    log_i_b, log_f_b = gt[2], jax.nn.log_sigmoid(gt[3])
    h_fwd = _mlstm_chunkwise(qh, kh, vh, log_i_f, log_f_f)
    rev = lambda a: jnp.flip(a, axis=2)
    h_bwd = rev(_mlstm_chunkwise(rev(qh), rev(kh), rev(vh), rev(log_i_b), rev(log_f_b)))
    h = h_fwd + h_bwd
    mu = h.mean(-1, keepdims=True)
    var = jnp.square(h - mu).mean(-1, keepdims=True)
    h = (h - mu) * lax.rsqrt(var + LN_EPS) * norm_w.astype(f32).reshape(H, 1, V_HEAD_DIM)
    h = h.transpose(0, 2, 1, 3).reshape(B, S, MLSTM_WIDTH)
    return (h * jax.nn.sigmoid(o.astype(f32))).astype(q.dtype)

def _fourier_group(z):
    B, S, _ = z.shape
    zg = z.astype(jnp.float32).reshape(B, S, N_FOURIER_GROUPS, FOURIER_GROUP_DIM)
    y = jnp.fft.fft2(zg, axes=(1, 3), norm='ortho').real
    return y.reshape(B, S, FOURIER_WIDTH).astype(z.dtype)

def _layer(x, c_act, w_ada, b_ada, w_in, b_gate, mlstm_norm_w, w_out, ln1_g, ln1_b,
           w_ff1, b_ff1, w_ff2, b_ff2, ln2_g, ln2_b):
    mod = (c_act @ w_ada + b_ada)[:, None, :]
    sh1, sc1, g1, sh2, sc2, g2 = jnp.split(mod, N_MOD, axis=-1)
    h = _ln_plain(x) * (1 + sc1) + sh1
    proj = h @ w_in
    q, k, v, o, fz, gates = jnp.split(proj, np.cumsum(IN_SPLITS)[:-1].tolist(), axis=-1)
    y_mlstm = _mlstm_group(q, k, v, o, gates, b_gate, mlstm_norm_w)
    y_fourier = _fourier_group(fz)
    mix = jnp.concatenate([y_mlstm, y_fourier], axis=-1) @ w_out
    x = _ln_affine(ALPHA * x + (1 + g1) * mix, ln1_g, ln1_b)
    h2 = _ln_plain(x) * (1 + sc2) + sh2
    ff = jnp.square(jax.nn.relu(h2 @ w_ff1 + b_ff1)) @ w_ff2 + b_ff2
    return _ln_affine(ALPHA * x + (1 + g2) * ff, ln2_g, ln2_b)

def second_inputs(seed: int = 0) -> dict:
    key = jax.random.key(seed)
    ks = jax.random.split(key, 20)
    f32 = jnp.float32
    nrm = lambda k, shape, s: jax.random.normal(k, shape, f32) * s
    f_bias = jnp.linspace(3.0, 6.0, N_MLSTM_HEADS, dtype=f32)
    gate_base = jnp.concatenate([jnp.zeros((N_MLSTM_HEADS,), f32), f_bias,
                                 jnp.zeros((N_MLSTM_HEADS,), f32), f_bias])
    return {
        "x": nrm(ks[0], (BATCH, SEQ, D_MODEL), 1.0),
        "c": nrm(ks[1], (BATCH, D_MODEL), 1.0),
        "w_ada": nrm(ks[2], (DEPTH_2, D_MODEL, N_MOD * D_MODEL), 0.1 * D_MODEL ** -0.5),
        "b_ada": nrm(ks[3], (DEPTH_2, N_MOD * D_MODEL), 0.01),
        "w_in": nrm(ks[4], (DEPTH_2, D_MODEL, IN_COLS), D_MODEL ** -0.5),
        "b_gate": gate_base[None, :] + nrm(ks[5], (DEPTH_2, N_GATES), 0.1),
        "mlstm_norm_w": 1.0 + nrm(ks[6], (DEPTH_2, MLSTM_WIDTH), 0.02),
        "w_out": nrm(ks[7], (DEPTH_2, MIX_WIDTH, D_MODEL), BETA * MIX_WIDTH ** -0.5),
        "ln1_g": 1.0 + nrm(ks[8], (DEPTH_2, D_MODEL), 0.02),
        "ln1_b": nrm(ks[9], (DEPTH_2, D_MODEL), 0.02),
        "w_ff1": nrm(ks[10], (DEPTH_2, D_MODEL, D_FF_2), D_MODEL ** -0.5),
        "b_ff1": nrm(ks[11], (DEPTH_2, D_FF_2), 0.02),
        "w_ff2": nrm(ks[12], (DEPTH_2, D_FF_2, D_MODEL), BETA * D_FF_2 ** -0.5),
        "b_ff2": nrm(ks[13], (DEPTH_2, D_MODEL), 0.02),
        "ln2_g": 1.0 + nrm(ks[14], (DEPTH_2, D_MODEL), 0.02),
        "ln2_b": nrm(ks[15], (DEPTH_2, D_MODEL), 0.02),
    }

def second_block(x, c, w_ada, b_ada, w_in, b_gate, mlstm_norm_w, w_out, ln1_g, ln1_b,
              w_ff1, b_ff1, w_ff2, b_ff2, ln2_g, ln2_b):
    c_act = jax.nn.silu(c)
    for l in range(DEPTH_2):
        x = _layer(x, c_act, w_ada[l], b_ada[l], w_in[l], b_gate[l], mlstm_norm_w[l], w_out[l],
                   ln1_g[l], ln1_b[l], w_ff1[l], b_ff1[l], w_ff2[l], b_ff2[l], ln2_g[l], ln2_b[l])
    return x


_first_inputs = second_inputs


def second_inputs(seed=0):
    import zlib

    import numpy as np

    out = dict(_first_inputs(seed))
    spreads = {}
    factors = {'b_ada': 2.841,
     'mlstm_norm_w': 8.0,
     'ln1_g': 2.877,
     'ln1_b': 2.737,
     'b_ff1': 4.781,
     'b_ff2': 3.833,
     'ln2_g': 2.884,
     'ln2_b': 2.865}
    for name, (base, spread) in spreads.items():
        noise = np.random.default_rng([zlib.crc32(name.encode()), seed]).standard_normal(out[name].shape)
        drawn = base * np.exp(spread * noise) if base else spread * noise
        out[name] = __import__('jax').numpy.asarray(drawn.astype(out[name].dtype))
    for name, factor in factors.items():
        out[name] = (out[name] * factor).astype(out[name].dtype)
    return out


_narrow_inputs = second_inputs


def second_inputs(seed=0):

    out = dict(_narrow_inputs(seed))
    wider = {'mlstm_norm_w': 3.72, 'ln1_g': 3.35, 'ln1_b': 3.35, 'ln2_g': 3.24, 'ln2_b': 3.24}
    for name, times in wider.items():
        mean = out[name].mean()
        out[name] = (mean + times * (out[name] - mean)).astype(out[name].dtype)
    return out


def setup_inputs(seed=0):
    out = dict(first_inputs(seed))
    for name, value in second_inputs(seed + 1).items():
        if name != "x":
            out[name + "_2"] = value
    return out


def reference(
    x, even_w_in, even_b_in, even_conv_w, even_conv_b, even_cnorm_g, even_cnorm_b,
    even_lru_conv_w, even_lru_conv_b, even_w_a, even_b_a, even_w_x, even_b_x, even_lru_lambda,
    even_w_out, odd_w_qkv, odd_lambda_q1, odd_lambda_k1, odd_lambda_q2, odd_lambda_k2,
    odd_subln_g, odd_w_out, mix_ln_g, mix_ln_b, ffn_w_gate, ffn_w_up, ffn_w_down, ffn_ln_g,
    ffn_ln_b, c_2, w_ada_2, b_ada_2, w_in_2, b_gate_2, mlstm_norm_w_2, w_out_2, ln1_g_2,
    ln1_b_2, w_ff1_2, b_ff1_2, w_ff2_2, b_ff2_2, ln2_g_2, ln2_b_2,
):
    x = first_block(
        x, even_w_in, even_b_in, even_conv_w, even_conv_b, even_cnorm_g, even_cnorm_b,
        even_lru_conv_w, even_lru_conv_b, even_w_a, even_b_a, even_w_x, even_b_x,
        even_lru_lambda, even_w_out, odd_w_qkv, odd_lambda_q1, odd_lambda_k1, odd_lambda_q2,
        odd_lambda_k2, odd_subln_g, odd_w_out, mix_ln_g, mix_ln_b, ffn_w_gate, ffn_w_up,
        ffn_w_down, ffn_ln_g, ffn_ln_b,
    )
    return second_block(
        x, c_2, w_ada_2, b_ada_2, w_in_2, b_gate_2, mlstm_norm_w_2, w_out_2, ln1_g_2, ln1_b_2,
        w_ff1_2, b_ff1_2, w_ff2_2, b_ff2_2, ln2_g_2, ln2_b_2,
    )


_drawn_inputs = setup_inputs


def setup_inputs(seed=0):
    import zlib

    import numpy as np

    out = dict(_drawn_inputs(seed))
    spreads = {}
    factors = {'even_cnorm_b': 3.012, 'even_b_a': 33.071, 'even_b_x': 8.0, 'odd_subln_g': 3.354}
    for name, (base, spread) in spreads.items():
        noise = np.random.default_rng([zlib.crc32(name.encode()), seed]).standard_normal(out[name].shape)
        drawn = base * np.exp(spread * noise) if base else spread * noise
        out[name] = __import__('jax').numpy.asarray(drawn.astype(out[name].dtype))
    for name, factor in factors.items():
        out[name] = (out[name] * factor).astype(out[name].dtype)
    return out
```

```python
import math
from contextlib import ExitStack

import numpy as np

import concourse.bass as bass
from concourse import mybir

F32 = mybir.dt.float32
F32R = mybir.dt.float32r
ACT = mybir.ActivationFunctionType
ALU = mybir.AluOpType
AX = mybir.AxisListType.X

P = 128
D = 1024
S = 1024
DB = D // P
HALF = 512
NT = S // P
FF = 2816
FFB = FF // P
FF2 = 4096
FF2B = FF2 // P
CONV_TAPS = 31
LRU_TAPS = 4
AB = 4
LN_EPS = 1e-5
ALPHA = 4.0 ** 0.25
ALPHA_2 = 2.0 ** 0.25
LRU_C = 8.0
HEADS = 8
HEAD_DIM = 64
LAMBDA_INIT = 0.8 - 0.6 * math.exp(-0.3)
ROPE_THETA = 10000.0
CHUNK_MASK = 64
NEG = -1e30
MH = 4
MDK = 64
MDV = 128
NMOD = 6

COLS = {}


def _columns():
    at = 0
    for name, n in [("b_in", 16), ("conv_w", AB * CONV_TAPS), ("conv_b", AB), ("cnorm_g", AB), ("cnorm_b", AB),
                    ("lru_w", AB * LRU_TAPS), ("lru_b", AB), ("b_a", AB), ("b_x", AB), ("lam", AB),
                    ("mix_g", 2 * DB), ("mix_b", 2 * DB), ("ffn_g", 2 * DB), ("ffn_b", 2 * DB),
                    ("subln_g", 1), ("lq1", 1), ("lk1", 1), ("lq2", 1), ("lk2", 1),
                    ("c", DB), ("b_ada", NMOD * DB), ("b_gate", 1), ("mnorm", MH),
                    ("ln1_g", DB), ("ln1_b", DB), ("b_ff1", FF2B), ("b_ff2", DB), ("ln2_g", DB), ("ln2_b", DB)]:
        COLS[name] = (at, n)
        at += n
    return at


NCOLS = _columns()

GROUPS_FF = [(0, 8), (8, 15), (15, 22)]
GROUPS_FF2 = [(0, 8), (8, 16), (16, 24), (24, 32)]


def program(nc, io, out):
    ctx = ExitStack()

    def sb(name, shape, dtype=F32, at=ctx):
        return at.enter_context(nc.sbuf_tensor(name, shape, dtype))

    def sem(name):
        return ctx.enter_context(nc.semaphore(name))

    x = sb("x", [P, DB, S])
    xh = sb("xh", [P, DB, S], F32R)
    xl = sb("xl", [P, DB, S], F32R)
    stage = [sb(f"stage{k}", [P, D]) for k in range(2)]
    whi = [sb(f"whi{k}", [P, D], F32R) for k in range(2)]
    wlo = [sb(f"wlo{k}", [P, D], F32R) for k in range(2)]
    cols = sb("cols", [P, NCOLS])
    ident = sb("ident", [P, P])
    mv = sb("mv", [P, 2, 2])
    stats = sb("stats", [P, 2, 2, 6])
    sd = sb("sd", [P, 2, 1])
    rstd = sb("rstd", [P, 2, 1])
    eps = sb("eps", [P, 1])
    credit = sb("credit", [P, 7])
    ps = [ctx.enter_context(nc.psum_tensor(f"ps{k}", [P, S], F32)) for k in range(4)]
    mod = sb("mod", [P, NMOD, DB])

    def col(name, k=0):
        at, n = COLS[name]
        return cols[:, at + k:at + k + 1] if isinstance(k, int) else cols[:, bass.ds(k + at, 1)]

    w_landed = [sem("w_landed0"), sem("w_landed1")]
    w_hi = sem("w_hi")
    w_split = sem("w_split")
    mm_done = sem("mm_done")
    acc_free = sem("acc_free")
    ln_tok, ln_stats, ln_aggr, ln_sd, ln_rstd, ln_norm, ln_feat, ln_x, ln_hi, ln_lo = [
        sem("ln_" + n) for n in ("tok", "stats", "aggr", "sd", "rstd", "norm", "feat", "x", "hi", "lo")]
    g_ready, hh_ready, h_split = sem("g_ready"), sem("hh_ready"), sem("h_split")
    params, consts = sem("params"), sem("consts")

    class Product:
        count = 0

        def __init__(self, n, src):
            self.base, self.n, self.src = Product.count, n, src
            Product.count += n

    def load(sp, g, i, k):
        slot, src = (g.base + k) % 2, g.src(i, k)
        sp.wait_ge(w_split, g.base + 2 * i + k + 1)
        sp.dma_start(stage[slot][:, 0:src.shape[-1]], src).then_inc(w_landed[slot], 16)

    def load_all(sp, g, following):
        if g.n >= 4:
            with sp.Fori(1, g.n // 2) as i:
                for k in range(2):
                    load(sp, g, i, k)
        if g.n % 2:
            load(sp, g, g.n // 2, 0)
        if following:
            for k in range(2):
                load(sp, following, 0, k)

    def split_hi(act, g, i, k):
        slot = (g.base + k) % 2
        act.wait_ge(w_landed[slot], 16 * ((g.base + k) // 2 + 1) + 16 * i)
        act.wait_ge(mm_done, g.base + 2 * i + k + 1)
        act.activation(whi[slot][:], stage[slot][:], ACT.Copy).then_inc(w_hi, 1)

    def split_lo(dve, g, i, k):
        slot = (g.base + k) % 2
        dve.wait_ge(w_hi, g.base + 2 * i + k + 1)
        dve.tensor_tensor(wlo[slot][:], stage[slot][:], whi[slot][:].bitcast(F32), ALU.subtract).then_inc(w_split, 1)

    def mm_unit(pe, g, i, k, kb, hi, lo, first=True, last=True, acc=None):
        slot, u = (g.base + k) % 2, g.base + 2 * i + k
        acc = ps[slot] if acc is None else acc
        pe.wait_ge(w_split, u + 3)
        pe.wait_ge(acc_free, u + 1)
        for b in range(kb):
            w = slice(b * P, (b + 1) * P)
            for wt, xt in ((whi, hi), (whi, lo), (wlo, hi)):
                for h in range(2):
                    done = pe.matmul(acc[:, h * HALF:(h + 1) * HALF], wt[slot][:, w],
                                     xt[:, b, h * HALF:(h + 1) * HALF],
                                     start=b == 0 and wt is whi and xt is hi,
                                     stop=b == kb - 1 and wt is wlo)
        done.then_inc(mm_done, 1)

    def pairs(eng, g, body):
        with eng.Fori(0, g.n // 2) as i:
            body(i)

    def blocks(w):
        return lambda i, k: w[bass.ds(2 * i + k, 1)].rearrange("a p n -> p (a n)")

    def pair_of(w0, w1, at):
        return lambda i, k: (w0, w1)[k][bass.ds(i + at, 1)].rearrange("a p n -> p (a n)")

    def groups(w, lo, hi):
        return lambda i, k: w[bass.ds(2 * i + k, 1), :, lo * P:hi * P].rearrange("a p n -> p (a n)")

    plan = {}

    def ffn_plan(layer):
        for n, (lo, hi) in enumerate(GROUPS_FF):
            plan[f"up{layer}_{n}"] = Product(2 * (hi - lo), pair_of(io[f"w_gate{layer}"], io[f"w_up{layer}"], lo))
            plan[f"down{layer}_{n}"] = Product(DB, groups(io[f"w_down{layer}"], lo, hi))

    plan["in0"] = Product(16, lambda i, k: io["w_in0"][bass.ds(2 * i + k, 1)].rearrange("a p n -> p (a n)"))
    plan["out0"] = Product(DB, blocks(io["w_out0"]))
    ffn_plan(0)
    plan["qkv"] = Product(3 * HEADS, blocks(io["w_qkv"]))
    plan["out1"] = Product(DB, blocks(io["w_qkv"][3 * HEADS:4 * HEADS]))
    ffn_plan(1)
    plan["in2"] = Product(17, blocks(io["w_in2"]))
    plan["dft"] = Product(2 * NT, blocks(io["dft"]))
    plan["out2"] = Product(DB, blocks(io["w_out2"]))
    for n, (lo, hi) in enumerate(GROUPS_FF2):
        plan[f"ff1_{n}"] = Product(hi - lo, lambda i, k, lo=lo: io["w_ff1"][bass.ds(2 * i + k + lo, 1)].rearrange("a p n -> p (a n)"))
        plan[f"ff2_{n}"] = Product(DB, groups(io["w_ff2"], lo, hi))
    order = list(plan.values())

    def after(g):
        n = order.index(g)
        return order[n + 1] if n + 1 < len(order) else None

    first = plan["in0"]
    with nc.Block(no_gpsimd_drain=True) as block:
        @block.sync
        def _(sp):
            sp.dma_start(cols[:], io["cols"]).then_inc(params, 16)
            sp.dma_start(ident[:], io["ident"]).then_inc(params, 16)
            sp.dma_start(x[:], io["x"]).then_inc(params, 16)
            for k in range(2):
                load(sp, first, 0, k)

        @block.vector
        def _(dve):
            dve.memset(eps[:], LN_EPS).then_inc(w_split, 1)
            for n, s in enumerate((w_split, mm_done, mm_done, acc_free, acc_free)):
                dve.memset(credit[:, n:n + 1], 0.0).then_inc(s, 1)
            dve.wait_ge(consts, 1)
            dve.tensor_tensor(xl[:], x[:], xh[:].bitcast(F32), ALU.subtract).then_inc(consts, 1)
            split_lo(dve, first, 0, 0)

        @block.scalar
        def _(act):
            act.wait_ge(params, 48)
            act.activation(xh[:], x[:], ACT.Copy).then_inc(consts, 1)
            split_hi(act, first, 0, 0)

    lns, ln_splits = [0], [0]

    def layer_norm(name, src, nblk, gain, bias, dst, func=None, split_at=0, split=True):
        base, sbase = lns[0], ln_splits[0]
        lns[0] += NT
        ln_splits[0] += NT if split else 0
        scope = ExitStack()
        xn = sb(name + "_xn", [P, 2, nblk * P], at=scope)
        xt = sb(name + "_xt", [P, 2, nblk, P], at=scope) if dst is None else None
        nsub = nblk * P // HALF

        def target(t, par):
            return xt[:, par] if dst is None else dst[:, :, bass.ts(t, P)]

        with nc.Block(no_gpsimd_drain=True) as block:
            @block.tensor
            def _(pe):
                def to_tokens(t):
                    if t >= 2:
                        pe.wait_ge(ln_norm, base + t - 1)
                    for b in range(nblk):
                        done = pe.transpose(ps[t % 2][:, b * P:(b + 1) * P], src[:, b, t * P:(t + 1) * P], ident[:])
                    done.then_inc(ln_tok, 1)

                def to_features(t):
                    pe.wait_ge(ln_norm, base + t + 1)
                    if t >= 2:
                        pe.wait_ge(ln_x, base + t - 1)
                    for b in range(nblk):
                        done = pe.transpose(ps[2 + t % 2][:, b * P:(b + 1) * P], xn[:, t % 2, b * P:(b + 1) * P], ident[:])
                    done.then_inc(ln_feat, 1)

                to_tokens(0)
                to_tokens(1)
                for t in range(NT):
                    to_features(t)
                    if t + 2 < NT:
                        to_tokens(t + 2)

            @block.vector
            def _(dve):
                def statistics(t, par):
                    dve.wait_ge(ln_tok, base + t + 1)
                    for k in range(nsub):
                        done = dve.bn_stats(stats[:, par, k, :], ps[par][:, k * HALF:(k + 1) * HALF])
                    done.then_inc(ln_stats, 1)
                    dve.wait_ge(ln_stats, base + t + 1)
                    dve.bn_aggr(mv[:, par, :], stats[:, par, 0:nsub, :]).then_inc(ln_aggr, 1)

                def normalise(t, par):
                    dve.wait_ge(ln_sd, base + t + 1)
                    dve.reciprocal(rstd[:, par, :], sd[:, par, :]).then_inc(ln_rstd, 1)
                    dve.wait_ge(ln_rstd, base + t + 1)
                    dve.tensor_scalar(xn[:, par, :], ps[par][:, 0:nblk * P], mv[:, par, 0:1], rstd[:, par, :],
                                      ALU.subtract, ALU.mult).then_inc(ln_norm, 1)

                def low(t, par):
                    if split:
                        dve.wait_ge(ln_hi, sbase + t + 1)
                        dve.tensor_tensor(xl[:, split_at:split_at + nblk, bass.ts(t, P)], target(t, par),
                                          xh[:, split_at:split_at + nblk, bass.ts(t, P)].bitcast(F32),
                                          ALU.subtract).then_inc(ln_lo, 1)

                statistics(0, 0)
                statistics(1, 1)
                normalise(0, 0)
                for t in range(1, NT - 1):
                    statistics(t + 1, (t + 1) % 2)
                    normalise(t, t % 2)
                    low(t - 1, (t - 1) % 2)
                normalise(NT - 1, 1)
                low(NT - 2, 0)
                low(NT - 1, 1)

            @block.scalar
            def _(act):
                def deviation(t, par):
                    act.wait_ge(ln_aggr, base + t + 1)
                    act.activation(sd[:, par, :], mv[:, par, 1:2], ACT.Sqrt, bias=eps[:]).then_inc(ln_sd, 1)

                def affine(t, par, reused):
                    act.wait_ge(ln_feat, base + t + 1)
                    if dst is None and reused:
                        act.wait_ge(ln_lo, sbase + t - 1)
                    for b in range(nblk):
                        done = act.activation(target(t, par)[:, b, :], ps[2 + par][:, b * P:(b + 1) * P], ACT.Identity,
                                              bias=bias(b), scale=gain(b))
                    done.then_inc(ln_x, 1)
                    if split:
                        act.wait_ge(ln_x, base + t + 1)
                        act.activation(xh[:, split_at:split_at + nblk, bass.ts(t, P)], target(t, par),
                                       ACT.Copy).then_inc(ln_hi, 1)

                deviation(0, 0)
                deviation(1, 1)
                affine(0, 0, False)
                deviation(2, 0)
                affine(1, 1, False)
                with act.Fori(1, (NT - 2) // 2) as i:
                    for k in range(2):
                        deviation(2 * i + k + 1, 1 - k)
                        affine(2 * i + k, k, True)
                deviation(NT - 1, 1)
                affine(NT - 2, 0, True)
                affine(NT - 1, 1, True)
        scope.close()

    def residual_product(g, kb, hi, lo, scale, gate=None):
        following = after(g)
        with nc.Block(no_gpsimd_drain=True) as block:
            @block.sync
            def _(sp):
                load_all(sp, g, following)

            @block.scalar
            def _(act):
                def body(i, last=False):
                    for k in range(2):
                        if following or not (last and k):
                            split_hi(act, g, i, k + 1)
                if following:
                    pairs(act, g, body)
                else:
                    with act.Fori(0, g.n // 2 - 1) as i:
                        body(i)
                    body(g.n // 2 - 1, True)

            @block.vector
            def _(dve):
                def body(i, last=False):
                    for k in range(2):
                        if following or not (last and k):
                            split_lo(dve, g, i, k + 1)
                        blk = x[:, bass.ds(2 * i + k, 1), :].rearrange("p a n -> p (a n)")
                        dve.wait_ge(mm_done, g.base + 2 * i + k + 3)
                        dve.scalar_tensor_tensor(blk, blk, scale, ps[(g.base + k) % 2][:], ALU.mult, ALU.add).then_inc(acc_free, 1)
                if following:
                    pairs(dve, g, body)
                else:
                    with dve.Fori(0, g.n // 2 - 1) as i:
                        body(i)
                    body(g.n // 2 - 1, True)

            @block.tensor
            def _(pe):
                def body(i):
                    for k in range(2):
                        mm_unit(pe, g, i, k, kb, hi, lo)
                pairs(pe, g, body)

    ffn_pairs = [0]

    def swiglu(layer):
        scope = ExitStack()
        hh = sb(f"hh{layer}", [P, DB, S], F32R, at=scope)
        hl = sb(f"hl{layer}", [P, DB, S], F32R, at=scope)
        g_t = sb(f"g_t{layer}", [P, S], at=scope)
        h_t = sb(f"h_t{layer}", [P, S], at=scope)
        for n, (lo, hi) in enumerate(GROUPS_FF):
            g = plan[f"up{layer}_{n}"]
            following = after(g)
            base = ffn_pairs[0]
            ffn_pairs[0] += hi - lo
            with nc.Block(no_gpsimd_drain=True) as block:
                @block.sync
                def _(sp):
                    load_all(sp, g, following)

                @block.scalar
                def _(act):
                    def body(i):
                        split_hi(act, g, i, 1)
                        act.wait_ge(mm_done, g.base + 2 * i + 3)
                        act.wait_ge(acc_free, g.base + 2 * i + 2)
                        act.activation(g_t[:], ps[g.base % 2][:], ACT.Silu).then_inc(acc_free, 1)
                        split_hi(act, g, i, 2)
                        act.wait_ge(acc_free, g.base + 2 * i + 4)
                        act.activation(hh[:, bass.ds(i, 1), :].rearrange("p a n -> p (a n)"), h_t[:], ACT.Copy).then_inc(hh_ready, 1)
                    pairs(act, g, body)

                @block.vector
                def _(dve):
                    def body(i):
                        split_lo(dve, g, i, 1)
                        split_lo(dve, g, i, 2)
                        dve.wait_ge(mm_done, g.base + 2 * i + 4)
                        dve.wait_ge(acc_free, g.base + 2 * i + 3)
                        dve.tensor_tensor(h_t[:], g_t[:], ps[(g.base + 1) % 2][:], ALU.mult).then_inc(acc_free, 1)
                        dve.wait_ge(hh_ready, base + i + 1)
                        j = bass.ds(i, 1)
                        dve.tensor_tensor(hl[:, j, :].rearrange("p a n -> p (a n)"), h_t[:],
                                          hh[:, j, :].bitcast(F32).rearrange("p a n -> p (a n)"), ALU.subtract).then_inc(h_split, 1)
                    pairs(dve, g, body)

                @block.tensor
                def _(pe):
                    def body(i):
                        for k in range(2):
                            mm_unit(pe, g, i, k, DB, xh, xl)
                    pairs(pe, g, body)
            residual_product(plan[f"down{layer}_{n}"], hi - lo, hh, hl, ALPHA if n == 0 else 1.0)
        scope.close()

    conv_scope = ExitStack()
    conv = sb("conv", [P, AB, S], at=conv_scope)
    rec = sb("rec", [P, AB, S], at=conv_scope)
    gel = sb("gel", [P, AB, S], at=conv_scope)
    pad_scope = ExitStack()
    PAD_A, PAD_R = CONV_TAPS - 1, LRU_TAPS - 1
    a_pad = sb("a_pad", [P, PAD_A + S], at=pad_scope)
    r_pad = sb("r_pad", [P, PAD_R + S], at=pad_scope)
    sig = sb("sig", [P, S], at=pad_scope)
    padded, a_ready, taps, r_ready, lru_taps = [sem(n) for n in ("padded", "a_ready", "taps", "r_ready", "lru_taps")]
    gin0 = plan["in0"]
    UPB = 4
    FIRST_TAPS = 20

    def split_hi4(act, i, k):
        slot = (gin0.base + k) % 2
        act.wait_ge(w_landed[slot], 16 * ((gin0.base + k) // 2 + 1) + 32 * i)
        act.wait_ge(mm_done, gin0.base + UPB * i + k + 1)
        act.activation(whi[slot][:], stage[slot][:], ACT.Copy).then_inc(w_hi, 1)

    def split_lo4(dve, i, k):
        slot = (gin0.base + k) % 2
        dve.wait_ge(w_hi, gin0.base + UPB * i + k + 1)
        dve.tensor_tensor(wlo[slot][:], stage[slot][:], whi[slot][:].bitcast(F32), ALU.subtract).then_inc(w_split, 1)

    with nc.Block(no_gpsimd_drain=True) as block:
        @block.sync
        def _(sp):
            load_all(sp, gin0, after(gin0))

        @block.tensor
        def _(pe):
            def body(i):
                for k in range(2):
                    mm_unit(pe, gin0, i, k, DB, xh, xl)
            pairs(pe, gin0, body)

        @block.scalar
        def _(act):
            with act.Fori(0, AB) as i:
                u = gin0.base + UPB * i
                split_hi4(act, i, 1)
                act.wait_ge(mm_done, u + 3)
                act.wait_ge(acc_free, u + 2)
                act.activation(sig[:], ps[0][:], ACT.Sigmoid, bias=col("b_in", UPB * i)).then_inc(acc_free, 1)
                split_hi4(act, i, 2)
                split_hi4(act, i, 3)
                split_hi4(act, i, 4)
                act.wait_ge(mm_done, u + 6)
                act.wait_ge(acc_free, u + 5)
                act.activation(gel[:, bass.ds(i, 1), :].rearrange("p a n -> p (a n)"), ps[1][:], ACT.Gelu_apprx_tanh,
                               bias=col("b_in", UPB * i + 3)).then_inc(acc_free, 1)

        @block.vector
        def _(dve):
            dve.memset(a_pad[:, 0:PAD_A], 0.0).then_inc(padded, 1)
            dve.memset(r_pad[:, 0:PAD_R], 0.0).then_inc(padded, 1)
            dve.wait_ge(padded, 2)
            with dve.Fori(0, AB) as i:
                u = gin0.base + UPB * i

                def tap(t, h, taps_n, pad, out, w, b, done):
                    dst = out[:, bass.ds(i, 1), h * HALF:(h + 1) * HALF].rearrange("p a n -> p (a n)")
                    src = pad[:, h * HALF + t:h * HALF + t + HALF]
                    if t == 0:
                        dve.tensor_scalar(dst, src, col(w, taps_n * i), col(b, i), ALU.mult, ALU.add).then_inc(done, 1)
                    else:
                        dve.wait_ge(done, 2 * taps_n * i + 2 * (t - 1) + h + 1)
                        dve.scalar_tensor_tensor(dst, src, col(w, taps_n * i + t), dst, ALU.mult, ALU.add).then_inc(done, 1)

                split_lo4(dve, i, 1)
                split_lo4(dve, i, 2)
                dve.wait_ge(mm_done, u + 4)
                dve.wait_ge(acc_free, u + 3)
                dve.scalar_tensor_tensor(a_pad[:, PAD_A:], ps[1][:], col("b_in", UPB * i + 1), sig[:],
                                         ALU.add, ALU.mult).then_inc(acc_free, 1)
                split_lo4(dve, i, 3)
                dve.wait_ge(acc_free, u + 4)
                for t in range(FIRST_TAPS):
                    for h in range(2):
                        tap(t, h, CONV_TAPS, a_pad, conv, "conv_w", "conv_b", taps)
                dve.wait_ge(mm_done, u + 5)
                dve.tensor_scalar(r_pad[:, PAD_R:], ps[0][:], col("b_in", UPB * i + 2), None, ALU.add).then_inc(acc_free, 1)
                split_lo4(dve, i, 4)
                dve.wait_ge(acc_free, u + 5)
                for t in range(FIRST_TAPS, CONV_TAPS):
                    for h in range(2):
                        tap(t, h, CONV_TAPS, a_pad, conv, "conv_w", "conv_b", taps)
                for t in range(LRU_TAPS):
                    for h in range(2):
                        tap(t, h, LRU_TAPS, r_pad, rec, "lru_w", "lru_b", lru_taps)
    pad_scope.close()

    lru_scope = ExitStack()
    w_gates = sb("w_gates", [P, 2, AB, P], at=lru_scope)
    sp_l = sb("sp_l", [P, 4, AB], at=lru_scope)
    g_r = sb("g_r", [P, S], at=lru_scope)
    g_i = sb("g_i", [P, S], at=lru_scope)
    a_t = sb("a_t", [P, S], at=lru_scope)
    v_t = sb("v_t", [P, S], at=lru_scope)
    wg_in, wg_zero, sp_step, gate_mm, gates, decays, root, lru_v, lru_m, lru_u, yb_hi, yb_lo, ya, ya_hi, ya_lo = [
        sem(n) for n in ("wg_in", "wg_zero", "sp_step", "gate_mm", "gates", "decays", "root", "lru_v", "lru_m", "lru_u",
                         "yb_hi", "yb_lo", "ya", "ya_hi", "ya_lo")]
    with nc.Block(no_gpsimd_drain=True) as block:
        @block.gpsimd
        def _(pool):
            pool.memset(w_gates[:], 0.0).then_inc(wg_zero, 1)

        @block.sync
        def _(sp):
            sp.wait_ge(wg_zero, 1)
            for k, w in enumerate(("w_a", "w_x")):
                for half in range(2):
                    q = slice(half * 64, half * 64 + 64)
                    sp.dma_start(w_gates[q, k, :, q], io[w][half]).then_inc(wg_in, 16)

        @block.tensor
        def _(pe):
            pe.wait_ge(wg_in, 64)
            for j in range(AB):
                if j:
                    pe.wait_ge(gates, 2 * j)
                for k in range(2):
                    for h in range(2):
                        done = pe.matmul(ps[k][:, h * HALF:(h + 1) * HALF], w_gates[:, k, j, :],
                                         rec[:, j, h * HALF:(h + 1) * HALF], start=True, stop=True)
                done.then_inc(gate_mm, 1)

        @block.scalar
        def _(act):
            at, n = COLS["lam"]
            lam = cols[:, at:at + n]
            act.activation(sp_l[:, 0, :], lam, ACT.Abs).then_inc(sp_step, 1)
            act.wait_ge(sp_step, 1)
            act.activation(sp_l[:, 1, :], sp_l[:, 0, :], ACT.Exp, scale=-1.0).then_inc(sp_step, 1)
            act.wait_ge(sp_step, 2)
            act.activation(sp_l[:, 2, :], sp_l[:, 1, :], ACT.Ln, bias=1.0).then_inc(sp_step, 1)
            with act.Fori(0, AB) as j:
                act.wait_ge(gate_mm, j + 1)
                act.wait_ge(lru_u, j + 6)
                act.activation(g_r[:], ps[0][:], ACT.Sigmoid, bias=col("b_a", j)).then_inc(gates, 1)
                act.activation(g_i[:], ps[1][:], ACT.Sigmoid, bias=col("b_x", j)).then_inc(gates, 1)
                act.wait_ge(gates, 2 * j + 1)
                act.activation(v_t[:], g_r[:], ACT.Tanh, scale=sp_l[:, 0, :][:, bass.ds(j, 1)]).then_inc(decays, 1)
                act.activation(a_t[:], g_r[:], ACT.Exp, scale=sp_l[:, 1, :][:, bass.ds(j, 1)]).then_inc(decays, 1)
                act.wait_ge(lru_v, 3 * j + 3)
                act.activation(v_t[:], v_t[:], ACT.Sqrt).then_inc(root, 1)
                act.wait_ge(lru_u, j + 7)
                act.activation(xh[:, bass.ds(j + AB, 1), :].rearrange("p a n -> p (a n)"),
                               rec[:, bass.ds(j, 1), :].rearrange("p a n -> p (a n)"), ACT.Copy).then_inc(yb_hi, 1)

        @block.vector
        def _(dve):
            at, n = COLS["lam"]
            dve.tensor_scalar(sp_l[:, 3, :], cols[:, at:at + n], -1.0, 0.0, ALU.mult, ALU.max).then_inc(lru_u, 1)
            dve.wait_ge(lru_u, 1)
            dve.wait_ge(sp_step, 3)
            dve.tensor_tensor(sp_l[:, 3, :], sp_l[:, 3, :], sp_l[:, 2, :], ALU.add).then_inc(lru_u, 1)
            dve.wait_ge(lru_u, 2)
            dve.tensor_scalar(sp_l[:, 0, :], sp_l[:, 3, :], LRU_C / 2, None, ALU.mult).then_inc(lru_u, 1)
            dve.tensor_scalar(sp_l[:, 1, :], sp_l[:, 3, :], -LRU_C, None, ALU.mult).then_inc(lru_u, 1)
            dve.wait_ge(lru_u, 4)
            for n in range(2):
                dve.memset(credit[:, 5 + n:6 + n], 0.0).then_inc(lru_u, 1)
            with dve.Fori(0, AB) as j:
                r = rec[:, bass.ds(j, 1), :].rearrange("p a n -> p (a n)")
                dve.wait_ge(decays, 2 * j + 2)
                dve.scalar_tensor_tensor(a_t[:], a_t[:], 1.0, v_t[:], ALU.add, ALU.mult).then_inc(lru_v, 1)
                dve.wait_ge(lru_v, 3 * j + 1)
                dve.tensor_scalar(a_t[:], a_t[:], -1.0, 1.0, ALU.mult, ALU.add).then_inc(lru_v, 1)
                dve.tensor_scalar(v_t[:], v_t[:], 2.0 ** -100, None, ALU.max).then_inc(lru_v, 1)
                dve.tensor_tensor(r, r, g_i[:], ALU.mult).then_inc(lru_m, 1)
                dve.wait_ge(root, j + 1)
                dve.wait_ge(lru_v, 3 * j + 3)
                dve.scalar_tensor_tensor(v_t[:], a_t[:], 1.0, v_t[:], ALU.add, ALU.mult).then_inc(lru_m, 1)
                dve.wait_ge(lru_m, 4 * j + 2)
                dve.tensor_tensor(r, r, v_t[:], ALU.mult).then_inc(lru_m, 1)
                dve.wait_ge(lru_m, 4 * j + 3)
                dve.tensor_tensor_scan(v_t[:], a_t[:], r, 0.0, ALU.mult, ALU.add).then_inc(lru_m, 1)
                dve.wait_ge(lru_m, 4 * j + 4)
                dve.tensor_tensor(r, v_t[:], gel[:, bass.ds(j, 1), :].rearrange("p a n -> p (a n)"), ALU.mult).then_inc(lru_u, 1)
                dve.wait_ge(yb_hi, j + 1)
                dve.tensor_tensor(xl[:, bass.ds(j + AB, 1), :].rearrange("p a n -> p (a n)"), r,
                                  xh[:, bass.ds(j + AB, 1), :].bitcast(F32).rearrange("p a n -> p (a n)"),
                                  ALU.subtract).then_inc(yb_lo, 1)
    lru_scope.close()
    layer_norm("cnorm", conv, AB, lambda b: col("cnorm_g", b), lambda b: col("cnorm_b", b), conv, split=False)
    with nc.Block(no_gpsimd_drain=True) as block:
        @block.scalar
        def _(act):
            for j in range(AB):
                act.activation(conv[:, j, :], conv[:, j, :], ACT.Silu).then_inc(ya, 1)
                act.wait_ge(ya, j + 1)
                act.activation(xh[:, j, :], conv[:, j, :], ACT.Copy).then_inc(ya_hi, 1)

        @block.vector
        def _(dve):
            for j in range(AB):
                dve.wait_ge(ya_hi, j + 1)
                dve.tensor_tensor(xl[:, j, :], conv[:, j, :], xh[:, j, :].bitcast(F32), ALU.subtract).then_inc(ya_lo, 1)
    conv_scope.close()
    residual_product(plan["out0"], DB, xh, xl, ALPHA)

    def mixed_norm(layer):
        layer_norm(f"mix{layer}", x, DB, lambda b: col("mix_g", layer * DB + b), lambda b: col("mix_b", layer * DB + b), x)

    mixed_norm(0)
    swiglu(0)
    layer_norm("ffn0", x, DB, lambda b: col("ffn_g", b), lambda b: col("ffn_b", b), x)

    attn_scope = ExitStack()
    o_t = sb("o_t", [P, HEADS, S], at=attn_scope)
    ones = sb("ones", [P, P], at=attn_scope)
    lam_t = sb("lam_t", [P, 8], at=attn_scope)
    head_scope = ExitStack()
    cos = sb("cos", [P, S], at=head_scope)
    sin = sb("sin", [P, S], at=head_scope)
    q_rot = [sb(f"q_rot{k}", [P, S], at=head_scope) for k in range(2)]
    k_rot = [sb(f"k_rot{k}", [P, S], at=head_scope) for k in range(2)]
    v_tok = sb("v_tok", [P, NT, P], at=head_scope)
    raw = sb("raw", [P, S], at=head_scope)
    swp = sb("swp", [P, S], at=head_scope)
    e0 = [sb(f"e0_{k}", [P, S - P + P * k], at=head_scope) for k in range(2)]
    e1 = sb("e1", [P, S], at=head_scope)
    a_t2 = [sb(f"a_t2_{k}", [P, HALF], at=head_scope) for k in range(2)]
    mx = sb("mx", [P, 2, 2], at=head_scope)
    nb = sb("nb", [P, 2, 2], at=head_scope)
    den = sb("den", [P, 2, 2], at=head_scope)
    rden = sb("rden", [P, 2, 2], at=head_scope)
    (rope_in, lam_s, lam_mm, lam_e, raw_ready, swapped, rope_a, rope_b, rope_done, sc_done, masked, mxs, nbs, exp0, exp1,
     recs, e1_scaled, attn, tr_done, tr_out, pv_done, o_out) = [sem(n) for n in (
         "rope_in", "lam_s", "lam_mm", "lam_e", "raw_ready", "swapped", "rope_a", "rope_b", "rope_done", "sc_done",
         "masked", "mxs", "nbs", "exp0", "exp1", "recs", "e1_scaled", "attn", "tr_done", "tr_out", "pv_done", "o_out")]
    gq = plan["qkv"]
    SCALE = HEAD_DIM ** -0.5
    acc, pT, pO, pS = ps[0], ps[1][:, 0:HALF], ps[1][:, HALF:S], (ps[2], ps[3])
    QUADS = [(0, 32), (32, 0), (64, 96), (96, 64)]
    UPH = 3
    BATCH = 4
    TPH = 14

    class Head:
        def __init__(self, const, i=0):
            self.const, self.i = const, i
            self.h = const + 2 * i
            self.par = const % 2

        def next(self):
            return Head(self.const + 1, self.i)

        def unit(self, k):
            u = gq.base + UPH * self.const + k
            return u + 2 * UPH * self.i, u % 2, 16 * (u // 2 + 1) + 16 * UPH * self.i

        def n(self, per, k=0):
            return per * self.h + k

    def batch(head, qt, b):
        return head.n(TPH, 2 + qt if qt < 4 else 6 + 2 * (qt - 4) + b)

    def head_hi(act, head, k):
        u, slot, landed = head.unit(k)
        act.wait_ge(w_landed[slot], landed)
        act.wait_ge(mm_done, u + 1)
        act.activation(whi[slot][:], stage[slot][:], ACT.Copy).then_inc(w_hi, 1)

    def head_lo(dve, head, k):
        u, slot, _ = head.unit(k)
        dve.wait_ge(w_hi, u + 1)
        dve.tensor_tensor(wlo[slot][:], stage[slot][:], whi[slot][:].bitcast(F32), ALU.subtract).then_inc(w_split, 1)

    def head_mm(pe, head, n):
        k, b = divmod(n, DB)
        u, slot, _ = head.unit(k)
        if b == 0:
            pe.wait_ge(w_split, u + 3)
            pe.wait_ge(acc_free, u + 2)
        for wt, xt in ((whi, xh), (whi, xl), (wlo, xh)):
            for h in range(2):
                done = pe.matmul(acc[:, h * HALF:(h + 1) * HALF], wt[slot][:, b * P:(b + 1) * P],
                                 xt[:, b, h * HALF:(h + 1) * HALF], start=b == 0 and wt is whi and xt is xh,
                                 stop=b == DB - 1 and wt is wlo)
        if b == DB - 1:
            done.then_inc(mm_done, 1)

    def head_raw(act, head, k):
        u, _, _ = head.unit(k)
        act.wait_ge(mm_done, u + 3)
        if k:
            act.wait_ge(rope_done, head.n(2, k))
        elif not (isinstance(head.h, int) and head.h == 0):
            act.wait_ge(tr_done, head.n(TPH, 2 - TPH))
        act.activation(raw[:], acc[:], ACT.Copy).then_inc(acc_free, 1)

    def head_swap(sp, head, k):
        u, _, _ = head.unit(k)
        sp.wait_ge(acc_free, u + 3)
        for to, of in QUADS:
            sp.dma_start(swp[to:to + 32, :], raw[of:of + 32, :]).then_inc(swapped, 16)

    def head_rope(dve, head, k):
        u, _, _ = head.unit(k)
        dst = (q_rot, k_rot)[k][head.par]
        dve.wait_ge(acc_free, u + 3)
        if not (isinstance(head.h, int) and head.h < 2):
            dve.wait_ge(sc_done, head.n(NT, -NT))
        dve.tensor_tensor(dst[:], raw[:], cos[:], ALU.mult).then_inc(rope_a, 1)
        dve.wait_ge(swapped, 64 * head.n(2, k + 1))
        dve.tensor_tensor(swp[:], swp[:], sin[:], ALU.mult).then_inc(rope_b, 1)
        dve.wait_ge(rope_a, head.n(2, k + 1))
        dve.wait_ge(rope_b, head.n(2, k + 1))
        dve.tensor_tensor(dst[:], dst[:], swp[:], ALU.add).then_inc(rope_done, 1)

    def head_load(sp, head, k):
        u, slot, _ = head.unit(k + 2)
        n = u - gq.base
        sp.wait_ge(w_split, u + 1)
        src = io["w_qkv"][n:n + 1] if isinstance(n, int) else io["w_qkv"][bass.ds(n, 1)]
        sp.dma_start(stage[slot][:], src.rearrange("a p n -> p (a n)")).then_inc(w_landed[slot], 16)

    def scores(pe, head, qt):
        w = (qt + 1) * P
        if qt == 0:
            pe.wait_ge(rope_done, head.n(2, 2))
        if qt or not (isinstance(head.h, int) and head.h == 0):
            pe.wait_ge(exp1, head.n(NT, qt))
        for at in range(0, w, HALF):
            n = min(HALF, w - at)
            for m in range(2):
                f = slice(m * HEAD_DIM, (m + 1) * HEAD_DIM)
                done = pe.matmul(pS[m][:, at:at + n], q_rot[head.par][f, qt * P:(qt + 1) * P],
                                 k_rot[head.par][f, at:at + n], start=True, stop=True)
        done.then_inc(sc_done, 1)

    def weights_t(pe, head, qt, b):
        idx = batch(head, qt, b)
        if b == 0:
            pe.wait_ge(attn, head.n(NT, qt + 1))
        pe.wait_ge(tr_out, idx)
        for j in range(BATCH * b, min(BATCH * (b + 1), qt + 1)):
            done = pe.transpose(pT[:, (j - BATCH * b) * P:(j - BATCH * b + 1) * P], e0[qt % 2][:, j * P:(j + 1) * P], ident[:])
        done.then_inc(tr_done, 1)

    def values_t(pe, head, b):
        u, _, _ = head.unit(2)
        idx = head.n(TPH, b)
        pe.wait_ge(acc_free, u + 3)
        if b or not (isinstance(head.h, int) and head.h == 0):
            pe.wait_ge(tr_out, idx)
        for j in range(BATCH):
            done = pe.transpose(pT[:, j * P:(j + 1) * P], raw[:, (BATCH * b + j) * P:(BATCH * b + j + 1) * P], ident[:])
        done.then_inc(tr_done, 1)

    def weighted(pe, head, qt, b):
        idx = batch(head, qt, b)
        pe.wait_ge(tr_out, idx + 1)
        if b == 0 and (qt >= 4 or not (isinstance(head.h, int) and head.h == 0)):
            pe.wait_ge(o_out, head.n(NT, qt - 3))
        at = (qt % 4) * P
        for j in range(BATCH * b, min(BATCH * (b + 1), qt + 1)):
            done = pe.matmul(pO[:, at:at + P], v_tok[:, j, :], a_t2[b][:, (j - BATCH * b) * P:(j - BATCH * b + 1) * P],
                             start=j == 0, stop=j == qt)
        if BATCH * (b + 1) > qt:
            done.then_inc(pv_done, 1)

    def pe_head(pe, head, before, project):
        nxt = head.next()
        for qt in range(NT):
            scores(pe, head, qt)
            if qt == 1:
                values_t(pe, head, 1)
            if project:
                head_mm(pe, nxt, 3 * qt)
            who, tile = (before, NT - 1) if qt == 0 else (head, qt - 1)
            if who:
                weights_t(pe, who, tile, 0)
            if project:
                head_mm(pe, nxt, 3 * qt + 1)
            if who:
                weighted(pe, who, tile, 0)
                if tile >= BATCH:
                    weights_t(pe, who, tile, 1)
            if project:
                head_mm(pe, nxt, 3 * qt + 2)
            if who and tile >= BATCH:
                weighted(pe, who, tile, 1)
            if qt == 0:
                values_t(pe, head, 0)

    def act_weights(act, head, qt, b):
        idx = batch(head, qt, b)
        n = (min(BATCH * (b + 1), qt + 1) - BATCH * b) * P
        act.wait_ge(tr_done, idx + 1)
        tiles = qt - 1 if b == 0 else (qt - 1 if qt > BATCH else (-1))
        if b == 0:
            if qt or not (isinstance(head.h, int) and head.h == 0):
                act.wait_ge(pv_done, head.n(NT, qt))
        elif qt > BATCH or not (isinstance(head.h, int) and head.h == 0):
            act.wait_ge(pv_done, head.n(NT, qt))
        act.activation(a_t2[b][:, 0:n], pT[:, 0:n], ACT.Copy).then_inc(tr_out, 1)

    def act_values(act, head, b):
        act.wait_ge(tr_done, head.n(TPH, b + 1))
        if not (isinstance(head.h, int) and head.h == 0):
            act.wait_ge(pv_done, head.n(NT))
        act.activation(v_tok[:, BATCH * b:BATCH * (b + 1), :].rearrange("p a n -> p (a n)"), pT[:], ACT.Copy).then_inc(tr_out, 1)

    def act_out(act, head, qt):
        act.wait_ge(pv_done, head.n(NT, qt + 1))
        at = (qt % 4) * P
        h = slice(head.h, head.h + 1) if isinstance(head.h, int) else bass.ds(head.h, 1)
        act.activation(o_t[:, h, qt * P:(qt + 1) * P].rearrange("p a n -> p (a n)"), pO[:, at:at + P], ACT.Copy).then_inc(o_out, 1)

    def act_head(act, head, before, project):
        nxt = head.next()
        for qt in range(NT):
            w, par = (qt + 1) * P, qt % 2
            who, tile = (before, NT - 1) if qt == 0 else (head, qt - 1)
            act.wait_ge(nbs, head.n(NT, qt + 1))
            act.activation(e0[par][:, 0:w], pS[0][:, 0:w], ACT.Exp, bias=nb[:, par, 0:1], scale=SCALE,
                           accum_out=den[:, par, 0:1]).then_inc(exp0, 1)
            if qt == 1:
                act_values(act, head, 1)
            if who:
                act_weights(act, who, tile, 0)
            if qt or who:
                act.wait_ge(attn, head.n(NT, qt))
            act.activation(e1[:, 0:w], pS[1][:, 0:w], ACT.Exp, bias=nb[:, par, 1:2], scale=SCALE,
                           accum_out=den[:, par, 1:2]).then_inc(exp1, 1)
            if project and qt == 0:
                head_hi(act, nxt, 1)
            if project and qt == 2:
                head_raw(act, nxt, 0)
                head_hi(act, nxt, 2)
            if project and qt == 5:
                head_raw(act, nxt, 1)
                head_hi(act, nxt, 3)
            if who and tile >= BATCH:
                act_weights(act, who, tile, 1)
            if who:
                act_out(act, who, tile)
            if qt == 0:
                act_values(act, head, 0)
            if project and qt == 7:
                head_raw(act, nxt, 2)

    def dve_head(dve, head, before, project):
        nxt = head.next()
        for qt in range(NT):
            w, par = (qt + 1) * P, qt % 2
            at = qt * P
            dve.wait_ge(sc_done, head.n(NT, qt + 1))
            for m in range(2):
                dve.memset(pS[m][0:CHUNK_MASK, at + CHUNK_MASK:at + P], NEG).then_inc(masked, 1)
            dve.wait_ge(masked, head.n(2 * NT, 2 * qt + 2))
            for m in range(2):
                dve.reduce_max(mx[:, par, m:m + 1], pS[m][:, 0:w], AX).then_inc(mxs, 1)
            dve.wait_ge(mxs, head.n(2 * NT, 2 * qt + 2))
            dve.tensor_scalar(nb[:, par, :], mx[:, par, :], -SCALE, None, ALU.mult).then_inc(nbs, 1)
            if project and qt == 0:
                head_lo(dve, nxt, 1)
            if project and qt == 3:
                head_lo(dve, nxt, 2)
                head_rope(dve, nxt, 0)
            if project and qt == 6:
                head_lo(dve, nxt, 3)
                head_rope(dve, nxt, 1)
            dve.wait_ge(exp1, head.n(NT, qt + 1))
            dve.reciprocal(rden[:, par, :], den[:, par, :]).then_inc(recs, 1)
            dve.wait_ge(recs, head.n(NT, qt + 1))
            dve.tensor_scalar(e1[:, 0:w], e1[:, 0:w], rden[:, par, 1:2], lam_t[:, 4:5], ALU.mult, ALU.mult).then_inc(e1_scaled, 1)
            dve.wait_ge(e1_scaled, head.n(NT, qt + 1))
            dve.scalar_tensor_tensor(e0[par][:, 0:w], e0[par][:, 0:w], rden[:, par, 0:1], e1[:, 0:w],
                                     ALU.mult, ALU.subtract).then_inc(attn, 1)

    def all_heads(eng, run):
        run(eng, Head(0), None, True)
        with eng.Fori(0, (HEADS - 2) // 2) as i:
            run(eng, Head(1, i), Head(0, i), True)
            run(eng, Head(2, i), Head(1, i), True)
        run(eng, Head(HEADS - 1), Head(HEADS - 2), False)

    with nc.Block(no_gpsimd_drain=True) as block:
        @block.sync
        def _(sp):
            sp.dma_start(cos[:], io["cos"]).then_inc(rope_in, 16)
            sp.dma_start(sin[:], io["sin"]).then_inc(rope_in, 16)

            def project(head):
                for k in range(UPH):
                    head_load(sp, head, k)
                    if k < 2:
                        head_swap(sp, head, k)
            project(Head(0))
            project(Head(1))
            with sp.Fori(0, (HEADS - 2) // 2) as i:
                project(Head(2, i))
                project(Head(3, i))

        @block.tensor
        def _(pe):
            pe.wait_ge(lam_s, 3)
            pe.matmul(ps[3][:, 0:2], ones[:], lam_t[:, 0:2], start=True, stop=True).then_inc(lam_mm, 1)
            for n in range(UPH * DB):
                head_mm(pe, Head(0), n)
            pe.wait_ge(lam_e, 1)
            all_heads(pe, pe_head)
            last = Head(HEADS - 1)
            for b in range(2):
                weights_t(pe, last, NT - 1, b)
                weighted(pe, last, NT - 1, b)

        @block.scalar
        def _(act):
            act.wait_ge(lam_mm, 1)
            act.activation(lam_t[:, 2:4], ps[3][:, 0:2], ACT.Exp).then_inc(lam_e, 1)
            for k in range(UPH):
                head_hi(act, Head(0), k + 1)
                head_raw(act, Head(0), k)
            all_heads(act, act_head)
            last = Head(HEADS - 1)
            for b in range(2):
                act_weights(act, last, NT - 1, b)
            act_out(act, last, NT - 1)

        @block.vector
        def _(dve):
            for n in range(2):
                dve.tensor_tensor(lam_t[:, n:n + 1], col(f"lq{n + 1}"), col(f"lk{n + 1}"), ALU.mult).then_inc(lam_s, 1)
            dve.memset(ones[:], 1.0).then_inc(lam_s, 1)
            dve.tensor_scalar(lam_t[:, 5:6], col("subln_g"), 1.0 - LAMBDA_INIT, None, ALU.mult).then_inc(lam_s, 1)
            dve.wait_ge(lam_e, 1)
            dve.tensor_tensor(lam_t[:, 6:7], lam_t[:, 2:3], lam_t[:, 3:4], ALU.subtract).then_inc(lam_s, 1)
            dve.wait_ge(lam_s, 5)
            dve.tensor_scalar(lam_t[:, 4:5], lam_t[:, 6:7], LAMBDA_INIT, None, ALU.add).then_inc(lam_s, 1)
            dve.wait_ge(lam_s, 6)
            dve.wait_ge(rope_in, 32)
            head_lo(dve, Head(0), 1)
            head_lo(dve, Head(0), 2)
            head_rope(dve, Head(0), 0)
            head_lo(dve, Head(0), 3)
            head_rope(dve, Head(0), 1)
            all_heads(dve, dve_head)
    head_scope.close()

    sub_scope = ExitStack()
    sq = sb("sq", [P, 2, S], at=sub_scope)
    ln_ms = sb("ln_ms", [P, S], at=sub_scope)
    rs = sb("rs", [P, 2, S], at=sub_scope)
    sub_sq, sub_mm, sub_ln, sub_rs, sub_o, sub_hi, sub_lo = [sem("sub_" + n) for n in ("sq", "mm", "ln", "rs", "o", "hi", "lo")]
    with nc.Block(no_gpsimd_drain=True) as block:
        @block.tensor
        def _(pe):
            for h in range(HEADS):
                pe.wait_ge(sub_sq, h + 1)
                if h >= 2:
                    pe.wait_ge(sub_ln, h - 1)
                for k in range(2):
                    done = pe.matmul(ps[h % 2][:, k * HALF:(k + 1) * HALF], ones[:], sq[:, h % 2, k * HALF:(k + 1) * HALF],
                                     start=True, stop=True)
                done.then_inc(sub_mm, 1)

        @block.scalar
        def _(act):
            def square(h):
                if h >= 2:
                    act.wait_ge(sub_mm, h - 1)
                act.activation(sq[:, h % 2, :], o_t[:, h, :], ACT.Square).then_inc(sub_sq, 1)

            def high(h):
                act.wait_ge(sub_o, h + 1)
                act.activation(xh[:, h, :], o_t[:, h, :], ACT.Copy).then_inc(sub_hi, 1)

            square(0)
            for h in range(HEADS):
                if h + 1 < HEADS:
                    square(h + 1)
                act.wait_ge(sub_mm, h + 1)
                if h:
                    act.wait_ge(sub_rs, h)
                act.activation(ln_ms[:], ps[h % 2][:], ACT.Ln, bias=eps[:], scale=1.0 / P).then_inc(sub_ln, 1)
                act.wait_ge(sub_ln, h + 1)
                if h >= 2:
                    act.wait_ge(sub_o, h - 1)
                act.activation(rs[:, h % 2, :], ln_ms[:], ACT.Exp, scale=-0.5).then_inc(sub_rs, 1)
                if h:
                    high(h - 1)
            high(HEADS - 1)

        @block.vector
        def _(dve):
            for h in range(HEADS):
                dve.wait_ge(sub_rs, h + 1)
                dve.scalar_tensor_tensor(o_t[:, h, :], o_t[:, h, :], lam_t[:, 5:6], rs[:, h % 2, :], ALU.mult, ALU.mult).then_inc(sub_o, 1)
                dve.wait_ge(sub_hi, h + 1)
                dve.tensor_tensor(xl[:, h, :], o_t[:, h, :], xh[:, h, :].bitcast(F32), ALU.subtract).then_inc(sub_lo, 1)
    sub_scope.close()
    attn_scope.close()
    residual_product(plan["out1"], DB, xh, xl, ALPHA)
    mixed_norm(1)
    swiglu(1)
    layer_norm("ffn1", x, DB, lambda b: col("ffn_g", DB + b), lambda b: col("ffn_b", DB + b), x, split=False)

    gb2 = sb("gb2", [P, DB])
    ada_scope = ExitStack()
    ADA_SLOTS = 6
    ada = [sb(f"ada{k}", [P, D], at=ada_scope) for k in range(ADA_SLOTS)]
    c_act = sb("c_act", [P, DB], at=ada_scope)
    ada_in = [sem(f"ada_in{k}") for k in range(ADA_SLOTS)]
    ada_c, ada_mm, mod_s = sem("ada_c"), sem("ada_mm"), sem("mod_s")
    UNITS = NMOD * DB
    with nc.Block(no_gpsimd_drain=True) as block:
        @block.sync
        def _(sp):
            for k in range(ADA_SLOTS):
                sp.dma_start(ada[k][:], io["w_ada"][k]).then_inc(ada_in[k], 16)
            with sp.Fori(1, UNITS // ADA_SLOTS) as i:
                for k in range(ADA_SLOTS):
                    sp.wait_ge(ada_mm, ADA_SLOTS * i + (k - ADA_SLOTS + 1))
                    sp.dma_start(ada[k][:], io["w_ada"][bass.ds(ADA_SLOTS * i + k, 1)].rearrange("a p n -> p (a n)")).then_inc(ada_in[k], 16)

        @block.scalar
        def _(act):
            at, n = COLS["c"]
            act.activation(c_act[:], cols[:, at:at + n], ACT.Silu).then_inc(ada_c, 1)

        @block.tensor
        def _(pe):
            pe.wait_ge(ada_c, 1)
            with pe.Fori(0, UNITS // ADA_SLOTS) as i:
                for k in range(ADA_SLOTS):
                    pe.wait_ge(ada_in[k], 16 * i + 16)
                    for b in range(DB):
                        done = pe.matmul(ps[0][:, bass.ds(ADA_SLOTS * i + k, 1)], ada[k][:, b * P:(b + 1) * P], c_act[:, b:b + 1],
                                         start=b == 0, stop=b == DB - 1)
                    done.then_inc(ada_mm, 1)

        @block.vector
        def _(dve):
            at, n = COLS["b_ada"]
            flat = mod[:].rearrange("p m b -> p (m b)")
            dve.wait_ge(ada_mm, UNITS)
            dve.tensor_tensor(flat, ps[0][:, 0:UNITS], cols[:, at:at + n], ALU.add).then_inc(mod_s, 1)
            dve.wait_ge(mod_s, 1)
            for first_mod in (1, 4):
                dve.tensor_scalar(mod[:, first_mod:first_mod + 2, :], mod[:, first_mod:first_mod + 2, :], 1.0, None, ALU.add).then_inc(mod_s, 1)
            dve.wait_ge(mod_s, 3)
            at, n = COLS["b_ff2"]
            dve.tensor_tensor(gb2[:], mod[:, 5, :], cols[:, at:at + n], ALU.mult).then_inc(mod_s, 1)
    ada_scope.close()

    layer_norm("mod1", x, DB, lambda b: mod[:, 1, b:b + 1], lambda b: mod[:, 0, b:b + 1], None)

    mix_scope = ExitStack()
    arena = sb("arena", [P, 17 * S + 8 * MH * (MDV + 1)], at=mix_scope)

    def tile(at, n, tokens=S):
        return arena[:, at * S:(at + n) * S].rearrange("p (a n) -> p a n", n=tokens)

    qt, kt, so, vt, zt, gt = tile(0, 2), tile(2, 2), tile(4, 4), tile(8, 4), tile(12, 4), tile(16, 1)[:, 0, :]
    v1 = arena[:, 17 * S:].rearrange("p (c h d) -> p c h d", c=NT, h=MH)
    yf = zt
    k_tok = tile(8, 2, MH * MDK)
    lf, bb, a_r, mt, wk, wint = [arena[0:64, n * S:(n + 1) * S] for n in (10, 11, 12, 13, 14, 15)]
    keep, lift = wk, wint
    gates_t = gt[0:64, :]
    w_dir = [tile(10, 1)[:, 0, :], tile(11, 1)[:, 0, :]]
    kw = arena[:, 12 * S:13 * S].rearrange("p (c e d) -> p c e d", c=NT, e=2)
    h_tok = arena[:, 12 * S:13 * S].rearrange("p (c d) -> p c d", c=NT)
    cst = arena[:, 14 * S:14 * S + 7 * (MDV + 1)].rearrange("p (c d) -> p c d", c=7)
    qs = gt
    gin2, gdft = plan["in2"], plan["dft"]

    in2_out = sem("in2_out")
    with nc.Block(no_gpsimd_drain=True) as block:
        @block.sync
        def _(sp):
            load_all(sp, gin2, gdft)

        @block.tensor
        def _(pe):
            def body(i):
                for k in range(2):
                    mm_unit(pe, gin2, i, k, DB, xh, xl)
            pairs(pe, gin2, body)
            mm_unit(pe, gin2, gin2.n // 2, 0, DB, xh, xl)

        @block.vector
        def _(dve):
            def body(i):
                for k in range(2):
                    split_lo(dve, gin2, i, k + 1)
            pairs(dve, gin2, body)
            split_lo(dve, gin2, gin2.n // 2, 1)

        @block.scalar
        def _(act):
            def out_of(i, k, dst, func=ACT.Copy, **more):
                act.wait_ge(mm_done, gin2.base + 2 * i + k + 3)
                act.activation(dst, ps[(gin2.base + k) % 2][:], func, **more).then_inc(acc_free, 1)
            places = ([(zt[:, b, :], ACT.Copy, {}) for b in range(4)]
                      + [(qt[:, b, :], ACT.Copy, dict(scale=MDK ** -0.5)) for b in range(2)]
                      + [(kt[:, b, :], ACT.Copy, {}) for b in range(2)]
                      + [(vt[:, b, :], ACT.Copy, {}) for b in range(4)]
                      + [(so[:, b, :], ACT.Sigmoid, {}) for b in range(4)]
                      + [(gt, ACT.Identity, dict(bias=col("b_gate")))])
            for n, (dst, func, more) in enumerate(places):
                split_hi(act, gin2, n // 2, n % 2 + 1)
                out_of(n // 2, n % 2, dst, func, **more)

    dft_scope = ExitStack()
    ones_col = sem("ones_col")
    cs_in, ch_mm, ch_hi, ch_lo, y_out, y_tr, yf_out = [sem(n) for n in ("cs_in", "ch_mm", "ch_hi", "ch_lo", "y_out", "y_tr", "yf_out")]
    cs = arena[:, 17 * S:17 * S + 2 * P]
    ytk = [arena[:, 17 * S + (1 + k) * HALF:17 * S + (2 + k) * HALF] for k in range(2)]
    xhv, xlv = [t[:].rearrange("p a (b n) -> p (a b) n", n=HALF) for t in (xh, xl)]
    with nc.Block(no_gpsimd_drain=True) as block:
        @block.sync
        def _(sp):
            sp.dma_start(cs, io["dft_channel"]).then_inc(cs_in, 16)

        @block.tensor
        def _(pe):
            pe.wait_ge(cs_in, 16)
            for n in range(NT):
                if n >= 2:
                    pe.wait_ge(ch_lo, 2 * n - 2)
                for g in range(4):
                    done = pe.matmul(ps[n % 2][:, g * 2 * P:(g + 1) * 2 * P], zt[:, g, n * P:(n + 1) * P], cs, start=True, stop=True)
                done.then_inc(ch_mm, 1)

        @block.scalar
        def _(act):
            for n in range(NT):
                act.wait_ge(ch_mm, n + 1)
                part = ps[n % 2][:].rearrange("p (g e c) -> p g e c", g=4, e=2)
                for e in range(2):
                    act.activation(xhv[:, NT * e + n, :].rearrange("p (g c) -> p g c", g=4), part[:, :, e, :], ACT.Copy).then_inc(ch_hi, 1)

        @block.vector
        def _(dve):
            for n in range(NT):
                part = ps[n % 2][:].rearrange("p (g e c) -> p g e c", g=4, e=2)
                dve.wait_ge(ch_hi, 2 * n + 2)
                for e in range(2):
                    dve.tensor_tensor(xlv[:, NT * e + n, :].rearrange("p (g c) -> p g c", g=4), part[:, :, e, :],
                                      xhv[:, NT * e + n, :].bitcast(F32).rearrange("p (g c) -> p g c", g=4), ALU.subtract).then_inc(ch_lo, 1)

    with nc.Block(no_gpsimd_drain=True) as block:
        @block.sync
        def _(sp):
            load_all(sp, gdft, after(gdft))

        @block.tensor
        def _(pe):
            def transposes(t):
                pe.wait_ge(acc_free, gdft.base + 2 * t + 4)
                if t >= 2:
                    pe.wait_ge(yf_out, t - 1)
                for g in range(4):
                    done = pe.transpose(ps[2 + t % 2][:, g * P:(g + 1) * P], ytk[t % 2][:, g * P:(g + 1) * P], ident[:])
                done.then_inc(y_tr, 1)

            for t in range(NT):
                for k in range(2):
                    u = gdft.base + 2 * t + k
                    slot = u % 2
                    pe.wait_ge(w_split, u + 3)
                    if k == 0:
                        pe.wait_ge(acc_free, u)
                    for b in range(DB):
                        for wt, xt in ((whi, xhv), (whi, xlv), (wlo, xhv)):
                            done = pe.matmul(ps[t % 2][:, 0:HALF], wt[slot][:, b * P:(b + 1) * P], xt[:, NT * k + b, :],
                                             start=k == 0 and b == 0 and wt is whi and xt is xhv,
                                             stop=k == 1 and b == DB - 1 and wt is wlo)
                    done.then_inc(mm_done, 1)
                if t:
                    transposes(t - 1)
            transposes(NT - 1)

        @block.scalar
        def _(act):
            def out_of(t):
                act.wait_ge(y_tr, t + 1)
                act.activation(yf[:, :, t * P:(t + 1) * P], ps[2 + t % 2][:, 0:HALF].rearrange("p (g c) -> p g c", g=4), ACT.Copy).then_inc(yf_out, 1)

            for t in range(NT):
                split_hi(act, gdft, t, 1)
                split_hi(act, gdft, t, 2)
                act.wait_ge(mm_done, gdft.base + 2 * t + 4)
                if t >= 2:
                    act.wait_ge(y_tr, t - 1)
                for h in range(2):
                    q = slice(h * 2 * P, (h + 1) * 2 * P)
                    act.activation(ytk[t % 2][:, q], ps[t % 2][:, q], ACT.Copy).then_inc(acc_free, 1)
                if t:
                    out_of(t - 1)
            out_of(NT - 1)

        @block.vector
        def _(dve):
            def body(i):
                for k in range(2):
                    split_lo(dve, gdft, i, k + 1)
            pairs(dve, gdft, body)
    dft_scope.close()

    kv_tr, kv_out, yf_hi, yf_lo = [sem(n) for n in ("kv_tr", "kv_out", "yf_hi", "yf_lo")]
    with nc.Block(no_gpsimd_drain=True) as block:
        @block.tensor
        def _(pe):
            for n in range(6):
                src = vt[:, n, :] if n < 4 else kt[:, n - 4, :]
                if n >= 2:
                    pe.wait_ge(kv_out, n - 1)
                for c in range(NT):
                    done = pe.transpose(ps[n % 2][:, c * P:(c + 1) * P], src[:, c * P:(c + 1) * P], ident[:])
                done.then_inc(kv_tr, 1)

        @block.scalar
        def _(act):
            for n in range(6):
                act.wait_ge(kv_tr, n + 1)
                if n == 4:
                    act.wait_ge(kv_tr, 4)
                dst = v1[:, :, n, 0:MDV] if n < 4 else k_tok[:, :, (n - 4) * P:(n - 3) * P]
                act.activation(dst, ps[n % 2][:].rearrange("p (c d) -> p c d", c=NT), ACT.Copy).then_inc(kv_out, 1)
            act.activation(xh[:, MH:2 * MH, :], yf, ACT.Copy).then_inc(yf_hi, 1)

        @block.vector
        def _(dve):
            dve.memset(v1[:, :, :, MDV:MDV + 1], 1.0).then_inc(ones_col, 1)
            dve.wait_ge(yf_hi, 1)
            dve.tensor_tensor(xl[:, MH:2 * MH, :], yf, xh[:, MH:2 * MH, :].bitcast(F32), ALU.subtract).then_inc(yf_lo, 1)

    rows_scope = ExitStack()
    small = sb("small", [P, 8, NT + 1], at=mix_scope)
    amx, bl, m_in, m_out, m_end, dec = [small[0:64, n, 0:NT] for n in range(6)]
    m_scan = small[0:64, 6, :]
    colt = sb("colt", [P, 3, NT, 2, MH], at=mix_scope)
    decay = sb("decay", [P, MH, NT], at=mix_scope)
    gs, ga, sl, row_tr, row_out, dec_mm = [sem(n) for n in ("gs", "ga", "sl", "row_tr", "row_out", "dec_mm")]
    DIRS = (slice(0, 32), slice(32, 64))

    def chunks(t):
        return t.rearrange("p (c n) -> p c n", c=NT)

    def over(t):
        return t.rearrange("p (c o) -> p c o", o=1).to_broadcast([64, NT, P])

    with nc.Block(no_gpsimd_drain=True) as block:
        @block.scalar
        def _(act):
            act.activation(lf, gt[64:128, :], ACT.Abs).then_inc(ga, 1)
            act.wait_ge(ga, 1)
            act.activation(lf, lf, ACT.Exp, scale=-1.0).then_inc(ga, 1)
            act.wait_ge(ga, 2)
            act.activation(lf, lf, ACT.Ln, bias=1.0).then_inc(ga, 1)
            act.wait_ge(gs, 17)
            act.activation(wk, wk, ACT.Exp).then_inc(ga, 1)
            act.activation(wint, wint, ACT.Exp).then_inc(ga, 1)
            act.activation(lf, lf, ACT.Exp, scale=-1.0).then_inc(ga, 1)
            act.activation(dec, dec, ACT.Exp).then_inc(ga, 1)
            for n in range(3):
                act.wait_ge(row_tr, n + 1)
                part = ps[n][:, 0:HALF].rearrange("p (c e r) -> p c e r", c=NT, e=2)[:, :, :, 0:MH]
                act.activation(colt[:, n], part, ACT.Copy).then_inc(row_out, 1)
            act.wait_ge(dec_mm, 1)
            for e in range(2):
                f = slice(e * 64, (e + 1) * 64)
                act.activation(decay[f].rearrange("p h c -> p (h c)"), ps[3][f, e * MH * NT:(e + 1) * MH * NT], ACT.Copy).then_inc(row_out, 1)

        @block.vector
        def _(dve):
            n = [0]

            def step(done, last=True):
                done.then_inc(gs, 1)
                n[0] += 1
                if last:
                    dve.wait_ge(gs, n[0])

            step(dve.memset(keep, 1.0), False)
            step(dve.memset(lift, 0.0))
            for e, t in ((0, 0), (1, P - 1)):
                step(dve.memset(chunks(keep)[DIRS[e], :, t:t + 1], 0.0), False)
                step(dve.memset(chunks(lift)[DIRS[e], :, t:t + 1], NEG), False)
            step(dve.tensor_scalar(bb, gt[64:128, :], 0.0, None, ALU.min))
            dve.wait_ge(ga, 3)
            step(dve.tensor_tensor(lf, bb, lf, ALU.subtract))
            step(dve.tensor_tensor_scan(bb[DIRS[0]], keep[DIRS[0]], lf[DIRS[0]], 0.0, ALU.mult, ALU.add), False)
            step(dve.tensor_tensor_scan(bb[DIRS[1], ::-1], keep[DIRS[1], ::-1], lf[DIRS[1], ::-1], 0.0, ALU.mult, ALU.add))
            step(dve.tensor_tensor(a_r, gates_t, bb, ALU.subtract))
            step(dve.tensor_tensor_scan(mt[DIRS[0]], lift[DIRS[0]], a_r[DIRS[0]], 0.0, ALU.add, ALU.max), False)
            step(dve.tensor_tensor_scan(mt[DIRS[1], ::-1], lift[DIRS[1], ::-1], a_r[DIRS[1], ::-1], 0.0, ALU.add, ALU.max))
            m = [0]

            def little(done, last=True):
                done.then_inc(sl, 1)
                m[0] += 1
                if last:
                    dve.wait_ge(sl, m[0])

            for e, t in ((0, P - 1), (1, 0)):
                little(dve.tensor_copy(amx[DIRS[e]].rearrange("p (c o) -> p c o", o=1), chunks(mt)[DIRS[e], :, t:t + 1]), False)
                little(dve.tensor_copy(bl[DIRS[e]].rearrange("p (c o) -> p c o", o=1), chunks(bb)[DIRS[e], :, t:t + 1]), False)
            little(dve.memset(m_scan, 0.0))
            little(dve.tensor_tensor_scan(m_scan[DIRS[0], 1:NT + 1], amx[DIRS[0]], bl[DIRS[0]], 0.0, ALU.max, ALU.add), False)
            back = slice(NT - 1, None, -1)
            little(dve.tensor_tensor_scan(m_scan[DIRS[1], back], amx[DIRS[1], ::-1], bl[DIRS[1], ::-1], 0.0, ALU.max, ALU.add))
            little(dve.tensor_copy(m_in[DIRS[0]], m_scan[DIRS[0], 0:NT]), False)
            little(dve.tensor_copy(m_in[DIRS[1]], m_scan[DIRS[1], 1:NT + 1]))
            little(dve.tensor_tensor(m_end, m_in, amx, ALU.max))
            little(dve.tensor_tensor(dec, m_in, m_end, ALU.subtract), False)
            step(dve.tensor_tensor(chunks(mt), chunks(mt), over(m_in), ALU.max))
            step(dve.tensor_tensor(chunks(wk), chunks(a_r), over(m_end), ALU.subtract), False)
            step(dve.tensor_tensor(chunks(wint), over(m_in), chunks(mt), ALU.subtract), False)
            step(dve.tensor_tensor(lf, bb, mt, ALU.add), False)
            assert n[0] == 17, n

        @block.tensor
        def _(pe):
            pe.wait_ge(ga, 7)
            for n, src in enumerate((a_r, wk, lf)):
                for c in range(NT):
                    done = pe.transpose(ps[n][:, c * 64:(c + 1) * 64], src[:, c * P:(c + 1) * P], ident[0:64, 0:64])
                done.then_inc(row_tr, 1)
            for e in range(2):
                for h in range(MH):
                    r = 32 * e + h
                    done = pe.matmul(ps[3][:, (e * MH + h) * NT:(e * MH + h + 1) * NT], ident[0:64, r:r + 1].to_broadcast([64, P]), dec,
                                     start=True, stop=True)
            done.then_inc(dec_mm, 1)
    rows_scope.close()

    spare = arena[:, 14 * S + 7 * (MDV + 1):15 * S]
    den_t = spare[:, 0:16].rearrange("p (e c) -> p e c", e=2)
    hst = spare[:, 16:64].rearrange("p (c k) -> p c k", c=NT)
    hmv = spare[:, 64:80].rearrange("p (c k) -> p c k", c=NT)
    hrs = spare[:, 80:88]
    (m_sc, m_bc, m_bcu, m_sel, m_w, m_kw, m_u, m_chain, m_pt, m_num, m_den, m_rden, m_hh, m_stat, m_mv, m_sd, m_rs, m_hn,
     m_tr, m_y, m_hi, m_lo) = [sem("m_" + n) for n in ("sc", "bc", "bcu", "sel", "w", "kw", "u", "chain", "pt", "num", "den",
                                                       "rden", "hh", "stat", "mv", "sd", "rs", "hn", "tr", "y", "hi", "lo")]
    W1 = MDV + 1
    PER_BANK = HALF // W1
    BANKS = [ps[2][:, 0:HALF], ps[2][:, HALF:S], ps[3][:, 0:HALF]]
    BANK_CHUNKS = [(b * PER_BANK, min((b + 1) * PER_BANK, NT)) for b in range(3)]
    CHAIN = NT - 1

    def place(c):
        return BANKS[c // PER_BANK][:, (c % PER_BANK) * W1:(c % PER_BANK + 1) * W1]

    def state(e, c):
        return cst[e * 64:(e + 1) * 64, c - 1 if e == 0 else c, :]

    with nc.Block(no_gpsimd_drain=True) as block:
        @block.tensor
        def _(pe):
            for h in range(MH):
                hb = slice((h % 2) * 64, (h % 2) * 64 + 64)
                if h:
                    pe.wait_ge(m_pt, 2 * h)
                for c in range(NT):
                    t = slice(c * P, (c + 1) * P)
                    done = pe.matmul(ps[0][:, t], kt[hb, h // 2, t], qt[hb, h // 2, t], start=True, stop=True)
                done.then_inc(m_sc, 1)
                for n, (src, e) in enumerate(((mt, 0), (mt, 1), (wint, 0), (wint, 1))):
                    if n:
                        pe.wait_ge(m_bcu, 4 * h + n)
                    elif h:
                        pe.wait_ge(m_y, h)
                    r = 32 * e + h
                    for k in range(2):
                        q = slice(k * HALF, (k + 1) * HALF)
                        done = pe.matmul(ps[1][:, q], ident[0:64, r:r + 1].to_broadcast([64, P]), src[:, q], start=True, stop=True)
                    done.then_inc(m_bc, 1)
                pe.wait_ge(m_kw, 2 * h + 2)
                if h:
                    pe.wait_ge(m_hh, 6 * h)
                for c in range(NT):
                    done = pe.matmul(place(c), kw[:, c, :, :].rearrange("p e d -> p (e d)"), v1[:, c, h, :], start=True, stop=True)
                done.then_inc(m_u, 1)
                for e in range(2):
                    pe.wait_ge(m_chain, 2 * CHAIN * (h + 1))
                    pe.wait_ge(m_pt, 2 * h + e + 1)
                    pe.wait_ge(m_bcu, 4 * h + 3 + e)
                    if e:
                        pe.wait_ge(m_hh, 6 * h + 3)
                    for c in range(NT):
                        t = slice(c * P, (c + 1) * P)
                        stateless = c == (0 if e == 0 else NT - 1)
                        done = pe.matmul(place(c), w_dir[e][:, t], v1[:, c, h, :], start=True, stop=stateless)
                        if not stateless:
                            done = pe.matmul(place(c), qs[e * 64:(e + 1) * 64, t], state(e, c), start=False, stop=True)
                    done.then_inc(m_num, 1)
                pe.wait_ge(m_hn, h + 1)
                pe.wait_ge(m_bcu, 4 * h + 4)
                for c in range(NT):
                    done = pe.transpose(ps[1][:, c * P:(c + 1) * P], h_tok[:, c, :], ident[:])
                done.then_inc(m_tr, 1)

        @block.gpsimd
        def _(pool):
            for h in range(MH):
                for e in range(2):
                    pool.wait_ge(m_bcu, 4 * h + e + 1)
                    pool.affine_select(out=chunks(w_dir[e]), in_=chunks(w_dir[e]), compare_op=ALU.is_ge, fill=-NEG, base=0,
                                       pattern=[[0, NT], [1 - 2 * e, P]], channel_multiplier=2 * e - 1).then_inc(m_sel, 1)

        @block.scalar
        def _(act):
            for h in range(MH):
                for e in range(2):
                    act.wait_ge(m_sel, 2 * h + e + 1)
                    act.activation(w_dir[e], w_dir[e], ACT.Exp, scale=-1.0).then_inc(m_w, 1)
                act.wait_ge(m_mv, h + 1)
                act.activation(hrs, hmv[:, :, 1], ACT.Sqrt, bias=eps[:]).then_inc(m_sd, 1)
                act.wait_ge(m_y, h + 1)
                act.activation(xh[:, h, :], so[:, h, :], ACT.Copy).then_inc(m_hi, 1)

        @block.vector
        def _(dve):
            for h in range(MH):
                hb = slice((h % 2) * 64, (h % 2) * 64 + 64)
                if h:
                    dve.wait_ge(m_num, 2 * h)
                    dve.wait_ge(m_tr, h)
                for e in range(2):
                    dve.wait_ge(m_bc, 4 * h + e + 1)
                    dve.tensor_tensor(chunks(w_dir[e]), chunks(ps[1][:]), colt[:, 0, :, e, h:h + 1].to_broadcast([P, NT, P]),
                                      ALU.subtract).then_inc(m_bcu, 1)
                    dve.tensor_tensor(kw[:, :, e, :], k_tok[:, :, h * MDK:(h + 1) * MDK],
                                      colt[:, 1, :, e, h:h + 1].to_broadcast([P, NT, MDK]), ALU.mult).then_inc(m_kw, 1)
                for e in range(2):
                    dve.wait_ge(m_bc, 4 * h + e + 3)
                    dve.tensor_tensor(qs[e * 64:(e + 1) * 64, :], qt[hb, h // 2, :], ps[1][hb, :], ALU.mult).then_inc(m_bcu, 1)
                dve.wait_ge(m_u, h + 1)
                done = 2 * CHAIN * h
                for n in range(CHAIN):
                    for e in range(2):
                        f = slice(e * 64, (e + 1) * 64)
                        c, to = (n, n + 1) if e == 0 else (NT - 1 - n, NT - 2 - n)
                        if n == 0:
                            dve.tensor_copy(state(e, to), place(c)[f]).then_inc(m_chain, 1)
                        else:
                            dve.wait_ge(m_chain, done - 1)
                            dve.scalar_tensor_tensor(state(e, to), state(e, c), decay[f, h, c:c + 1], place(c)[f],
                                                     ALU.mult, ALU.add).then_inc(m_chain, 1)
                        done += 1
                for e in range(2):
                    dve.wait_ge(m_w, 2 * h + e + 1)
                    if e == 0:
                        dve.wait_ge(m_sc, h + 1)
                    dve.tensor_tensor(w_dir[e], ps[0][:], w_dir[e], ALU.mult).then_inc(m_pt, 1)
                for e in range(2):
                    dve.wait_ge(m_num, 2 * h + e + 1)
                    for b, (c0, c1) in enumerate(BANK_CHUNKS):
                        part = BANKS[b][:, 0:(c1 - c0) * W1].rearrange("p (c d) -> p c d", d=W1)
                        dve.tensor_tensor(den_t[:, e, c0:c1].rearrange("p (c o) -> p c o", o=1), part[:, :, MDV:W1],
                                          colt[:, 2, c0:c1, e, h:h + 1], ALU.max).then_inc(m_den, 1)
                    for b, (c0, c1) in enumerate(BANK_CHUNKS):
                        part = BANKS[b][:, 0:(c1 - c0) * W1].rearrange("p (c d) -> p c d", d=W1)
                        d = den_t[:, e, c0:c1].rearrange("p (c o) -> p c o", o=1)
                        dve.wait_ge(m_den, 12 * h + 6 * e + b + 1)
                        dve.scalar_tensor_tensor(d, part[:, :, MDV:W1], -1.0, d, ALU.mult, ALU.max).then_inc(m_den, 1)
                    dve.wait_ge(m_den, 12 * h + 6 * e + 6)
                    dve.reciprocal(den_t[:, e, :], den_t[:, e, :]).then_inc(m_rden, 1)
                    dve.wait_ge(m_rden, 2 * h + e + 1)
                    for b, (c0, c1) in enumerate(BANK_CHUNKS):
                        part = BANKS[b][:, 0:(c1 - c0) * W1].rearrange("p (c d) -> p c d", d=W1)[:, :, 0:MDV]
                        r = den_t[:, e, c0:c1].rearrange("p (c o) -> p c o", o=1).to_broadcast([P, c1 - c0, MDV])
                        dst = h_tok if e == 0 else chunks(w_dir[0])
                        dve.tensor_tensor(dst[:, c0:c1, :], part, r, ALU.mult).then_inc(m_hh, 1)
                dve.wait_ge(m_hh, 6 * h + 6)
                dve.tensor_tensor(h_tok, h_tok, chunks(w_dir[0]), ALU.add).then_inc(m_stat, 1)
                dve.wait_ge(m_stat, 2 * h + 1)
                for c in range(NT):
                    done = dve.bn_stats(hst[:, c, :], h_tok[:, c, :])
                done.then_inc(m_stat, 1)
                dve.wait_ge(m_stat, 2 * h + 2)
                for c in range(NT):
                    done = dve.bn_aggr(hmv[:, c, :], hst[:, c, :])
                done.then_inc(m_mv, 1)
                dve.wait_ge(m_sd, h + 1)
                dve.reciprocal(hrs, hrs).then_inc(m_rs, 1)
                dve.wait_ge(m_rs, h + 1)
                for c in range(NT):
                    done = dve.tensor_scalar(h_tok[:, c, :], h_tok[:, c, :], hmv[:, c, 0:1], hrs[:, c:c + 1], ALU.subtract, ALU.mult)
                done.then_inc(m_hn, 1)
                dve.wait_ge(m_tr, h + 1)
                dve.scalar_tensor_tensor(so[:, h, :], ps[1][:], col("mnorm", h), so[:, h, :], ALU.mult, ALU.mult).then_inc(m_y, 1)
                dve.wait_ge(m_hi, h + 1)
                dve.tensor_tensor(xl[:, h, :], so[:, h, :], xh[:, h, :].bitcast(F32), ALU.subtract).then_inc(m_lo, 1)
    mix_scope.close()

    scaled = sem("scaled")
    scaled_n = [0]

    def gated_product(g, kb, hi, lo, gate, before=None):
        following = after(g)
        base = scaled_n[0]
        scaled_n[0] += g.n if before else 0
        with nc.Block(no_gpsimd_drain=True) as block:
            @block.sync
            def _(sp):
                load_all(sp, g, following)

            def ahead(eng, split, rest):
                def body(i, last=False):
                    for k in range(2):
                        if following or not (last and k):
                            split(eng, g, i, k + 1)
                        rest(i, k)
                if following:
                    pairs(eng, g, body)
                else:
                    with eng.Fori(0, g.n // 2 - 1) as i:
                        body(i)
                    body(g.n // 2 - 1, True)

            @block.scalar
            def _(act):
                ahead(act, split_hi, lambda i, k: None)

            @block.vector
            def _(dve):
                def rest(i, k):
                    j = 2 * i + k
                    blk = x[:, bass.ds(j, 1), :].rearrange("p a n -> p (a n)")
                    if before:
                        dve.tensor_scalar(blk, blk, ALPHA_2, before(j), ALU.mult, ALU.add).then_inc(scaled, 1)
                        dve.wait_ge(scaled, base + j + 1)
                    dve.wait_ge(mm_done, g.base + j + 3)
                    dve.scalar_tensor_tensor(blk, ps[(g.base + k) % 2][:], mod[:, gate, bass.ds(j, 1)], blk, ALU.mult, ALU.add).then_inc(acc_free, 1)
                ahead(dve, split_lo, rest)

            @block.tensor
            def _(pe):
                def body(i):
                    for k in range(2):
                        mm_unit(pe, g, i, k, kb, hi, lo)
                pairs(pe, g, body)

    gated_product(plan["out2"], DB, xh, xl, 2, lambda j: 0.0)
    layer_norm("ln1", x, DB, lambda b: col("ln1_g", b), lambda b: col("ln1_b", b), x, split=False)
    layer_norm("mod2", x, DB, lambda b: mod[:, 4, b:b + 1], lambda b: mod[:, 3, b:b + 1], None)
    ff_scope = ExitStack()
    hh2 = sb("hh2", [P, DB, S], F32R, at=ff_scope)
    hl2 = sb("hl2", [P, DB, S], F32R, at=ff_scope)
    r_t = sb("r_t", [P, S], at=ff_scope)
    s_t = sb("s_t", [P, 2, S], at=ff_scope)
    sq_ready, s_hi, s_lo = sem("sq_ready"), sem("s_hi"), sem("s_lo")
    for n, (lo_b, hi_b) in enumerate(GROUPS_FF2):
        g1 = plan[f"ff1_{n}"]

        def ff1(g, lo_b=lo_b):
            with nc.Block(no_gpsimd_drain=True) as block:
                @block.sync
                def _(sp):
                    load_all(sp, g, after(g))

                @block.tensor
                def _(pe):
                    def body(i):
                        for k in range(2):
                            mm_unit(pe, g, i, k, DB, xh, xl)
                    pairs(pe, g, body)

                @block.scalar
                def _(act):
                    def body(i):
                        for k in range(2):
                            j = 2 * i + k
                            split_hi(act, g, i, k + 1)
                            act.wait_ge(mm_done, g.base + j + 3)
                            act.activation(r_t[:], ps[(g.base + k) % 2][:], ACT.Relu, bias=col("b_ff1", lo_b + j)).then_inc(acc_free, 1)
                            act.wait_ge(sq_ready, lo_b + j + 1)
                            act.activation(hh2[:, bass.ds(j, 1), :].rearrange("p a n -> p (a n)"), s_t[:, k, :], ACT.Copy).then_inc(s_hi, 1)
                    pairs(act, g, body)

                @block.vector
                def _(dve):
                    def body(i):
                        for k in range(2):
                            j = 2 * i + k
                            split_lo(dve, g, i, k + 1)
                            dve.wait_ge(acc_free, g.base + j + 3)
                            dve.tensor_tensor(s_t[:, k, :], r_t[:], r_t[:], ALU.mult).then_inc(sq_ready, 1)
                            dve.wait_ge(s_hi, lo_b + j + 1)
                            dve.tensor_tensor(hl2[:, bass.ds(j, 1), :].rearrange("p a n -> p (a n)"), s_t[:, k, :],
                                              hh2[:, bass.ds(j, 1), :].bitcast(F32).rearrange("p a n -> p (a n)"), ALU.subtract).then_inc(s_lo, 1)
                    pairs(dve, g, body)
        ff1(g1)
        gated_product(plan[f"ff2_{n}"], hi_b - lo_b, hh2, hl2, 5,
                      (lambda j: gb2[:, bass.ds(j, 1)]) if n == 0 else None)
    ff_scope.close()
    layer_norm("ln2", x, DB, lambda b: col("ln2_g", b), lambda b: col("ln2_b", b), x, split=False)

    stored = sem("stored")
    with nc.Block(no_gpsimd_drain=True) as block:
        @block.sync
        def _(sp):
            for b in range(DB):
                sp.dma_start(out[:, b, :], x[:, b, :]).then_inc(stored, 16)
            sp.wait_ge(stored, 16 * DB)
    ctx.close()


def unit_layout(w):
    k, n = w.shape
    return np.ascontiguousarray(w.reshape(k // P, P, n // P, P).transpose(2, 1, 0, 3).reshape(n // P, P, k))


def feature_columns(v):
    return np.ascontiguousarray(np.reshape(v, (-1, P)).T)


def layouts(a):
    a = {k: np.asarray(v) for k, v in a.items()}
    io = {"x": np.ascontiguousarray(a["x"][0].T.reshape(DB, P, S).transpose(1, 0, 2))}
    table = {}

    def put(name, v):
        table[name] = feature_columns(v)

    def even(v):
        val, gate, bgate, rec = np.split(v, 4, axis=-1)
        parts = [np.split(t, AB, axis=-1) for t in (gate, val, rec, bgate)]
        return np.concatenate([parts[k][j] for j in range(AB) for k in range(4)], axis=-1)

    put("b_in", even(a["even_b_in"][0]))
    put("conv_w", a["even_conv_w"][0].T.reshape(AB, P, CONV_TAPS).transpose(0, 2, 1))
    put("conv_b", a["even_conv_b"])
    put("cnorm_g", a["even_cnorm_g"])
    put("cnorm_b", a["even_cnorm_b"])
    put("lru_w", a["even_lru_conv_w"][0].T.reshape(AB, P, LRU_TAPS).transpose(0, 2, 1))
    put("lru_b", a["even_lru_conv_b"])
    put("b_a", a["even_b_a"])
    put("b_x", a["even_b_x"])
    put("lam", a["even_lru_lambda"])
    for n in ("mix", "ffn"):
        put(n + "_g", a[n + "_ln_g"])
        put(n + "_b", a[n + "_ln_b"])
    put("subln_g", a["odd_subln_g"])
    for n in ("q1", "k1", "q2", "k2"):
        put("l" + n, np.pad(a["odd_lambda_" + n][0], (0, P - HEAD_DIM)))
    put("c", a["c_2"])
    put("b_ada", a["b_ada_2"])
    gate_rows = np.zeros((4, 32), np.float32)
    gate_rows[:, :MH] = a["b_gate_2"][0].reshape(4, MH)[[0, 2, 1, 3]]
    put("b_gate", gate_rows)
    put("mnorm", a["mlstm_norm_w_2"])
    for n in ("ln1_g", "ln1_b", "b_ff1", "b_ff2", "ln2_g", "ln2_b"):
        put(n, a[n + "_2"])
    assert all(table[n].shape[1] == c for n, (_, c) in COLS.items()), {n: table[n].shape for n in table}
    io["cols"] = np.ascontiguousarray(np.concatenate([table[n] for n in COLS], axis=1))
    io["ident"] = np.eye(P, dtype=np.float32)
    io["w_in0"] = unit_layout(even(a["even_w_in"][0]))
    io["w_out0"] = unit_layout(a["even_w_out"][0])
    for n, w in (("w_a", "even_w_a"), ("w_x", "even_w_x")):
        io[n] = np.ascontiguousarray(a[w][0].reshape(AB, 2, 64, 64).transpose(1, 2, 0, 3))
    for layer in range(2):
        io[f"w_gate{layer}"] = unit_layout(a["ffn_w_gate"][layer])
        io[f"w_up{layer}"] = unit_layout(a["ffn_w_up"][layer])
        io[f"w_down{layer}"] = unit_layout(a["ffn_w_down"][layer])
    more_layouts(a, io)
    return io


def more_layouts(a, io):
    qkv = a["odd_w_qkv"][0].reshape(D, 3, HEADS, P).transpose(0, 2, 1, 3).reshape(D, 3 * D)
    io["w_qkv"] = np.concatenate([unit_layout(np.ascontiguousarray(qkv)), unit_layout(a["odd_w_out"][0])])
    inv = np.float32(ROPE_THETA) ** (-np.arange(0, HEAD_DIM, 2, dtype=np.float32) / np.float32(HEAD_DIM))
    ang = np.tile(inv[:, None] * np.arange(S, dtype=np.float32)[None, :], (4, 1))
    sign = np.where(np.arange(P) % HEAD_DIM < HEAD_DIM // 2, -1.0, 1.0)[:, None]
    io["cos"] = np.cos(ang.astype(np.float64)).astype(np.float32)
    io["sin"] = (sign * np.sin(ang.astype(np.float64))).astype(np.float32)
    wq, wk, wv, wo, wf, wg = np.split(a["w_in_2"][0], np.cumsum([256, 256, 512, 512, 512]), axis=1)
    gate_cols = np.zeros((D, 4, 32), np.float32)
    gate_cols[:, :, :MH] = wg.reshape(D, 4, MH)[:, [0, 2, 1, 3]]
    io["w_in2"] = unit_layout(np.concatenate([wf, wq, wk, wv, wo, gate_cols.reshape(D, P)], axis=1))
    io["w_out2"] = unit_layout(a["w_out_2"][0])
    io["w_ff1"] = unit_layout(a["w_ff1_2"][0])
    io["w_ff2"] = unit_layout(a["w_ff2_2"][0])
    io["w_ada"] = unit_layout(a["w_ada_2"][0])
    turn = 2.0 * np.pi * (np.outer(np.arange(S), np.arange(S)) % S) / S
    token = np.stack([unit_layout(np.cos(turn) * S ** -0.5), unit_layout(-np.sin(turn) * S ** -0.5)], axis=1)
    io["dft"] = np.ascontiguousarray(token.reshape(2 * NT, P, S).astype(np.float32))
    turn = 2.0 * np.pi * (np.outer(np.arange(P), np.arange(P)) % P) / P
    io["dft_channel"] = np.concatenate([np.cos(turn), np.sin(turn)], axis=1).astype(np.float32) * np.float32(P ** -0.5)


def kernel(**inputs):
    import concourse.bacc as bacc
    from concourse.bass_utils import run_bass_kernel_spmd as run

    nc = bacc.Bacc("TRN2", target_bir_lowering=False, num_devices=1)
    arrays = layouts(inputs)
    io = {n: nc.dram_tensor(f"in_{n}", v.shape, mybir.dt.from_np(v.dtype), kind="ExternalInput").ap() for n, v in arrays.items()}
    out = nc.dram_tensor("out", (P, DB, S), F32, kind="ExternalOutput").ap()
    program(nc, io, out)
    got = run(nc, [{f"in_{n}": v for n, v in arrays.items()}], core_ids=[0]).results[0]["out"]
    return np.ascontiguousarray(got.transpose(1, 0, 2).reshape(D, S).T)[None]
```

```python
import math
from contextlib import ExitStack

import numpy as np

import concourse.bass as bass
from concourse import mybir

F32 = mybir.dt.float32
F32R = mybir.dt.float32r
ACT = mybir.ActivationFunctionType
ALU = mybir.AluOpType
AX = mybir.AxisListType.X

P = 128
D = 1024
S = 1024
DB = D // P
HALF = 512
NT = S // P
FF = 2816
FFB = FF // P
FF2 = 4096
FF2B = FF2 // P
CONV_TAPS = 31
LRU_TAPS = 4
AB = 4
LN_EPS = 1e-5
ALPHA = 4.0 ** 0.25
ALPHA_2 = 2.0 ** 0.25
LRU_C = 8.0
HEADS = 8
HEAD_DIM = 64
LAMBDA_INIT = 0.8 - 0.6 * math.exp(-0.3)
ROPE_THETA = 10000.0
CHUNK_MASK = 64
NEG = -1e30
MH = 4
MDK = 64
MDV = 128
NMOD = 6

COLS = {}


def _columns():
    at = 0
    for name, n in [("b_in", 16), ("conv_w", AB * CONV_TAPS), ("conv_b", AB), ("cnorm_g", AB), ("cnorm_b", AB),
                    ("lru_w", AB * LRU_TAPS), ("lru_b", AB), ("b_a", AB), ("b_x", AB), ("lam", AB),
                    ("mix_g", 2 * DB), ("mix_b", 2 * DB), ("ffn_g", 2 * DB), ("ffn_b", 2 * DB),
                    ("subln_g", 1), ("lq1", 1), ("lk1", 1), ("lq2", 1), ("lk2", 1),
                    ("b_ada", NMOD * DB), ("b_gate", 1), ("mnorm", MH),
                    ("ln1_g", DB), ("ln1_b", DB), ("b_ff1", FF2B), ("b_ff2", DB), ("ln2_g", DB), ("ln2_b", DB)]:
        COLS[name] = (at, n)
        at += n
    return at


NCOLS = _columns()

GROUPS_FF = [(0, 8), (8, 15), (15, 22)]
GROUPS_FF2 = [(0, 8), (8, 16), (16, 24), (24, 32)]


def program(nc, io, out):
    ctx = ExitStack()

    def sb(name, shape, dtype=F32, at=ctx):
        return at.enter_context(nc.sbuf_tensor(name, shape, dtype))

    def sem(name):
        return ctx.enter_context(nc.semaphore(name))

    x = sb("x", [P, DB, S])
    xh = sb("xh", [P, DB, S], F32R)
    xl = sb("xl", [P, DB, S], F32R)
    stage = [sb(f"stage{k}", [P, D]) for k in range(2)]
    whi = [sb(f"whi{k}", [P, D], F32R) for k in range(2)]
    wlo = [sb(f"wlo{k}", [P, D], F32R) for k in range(2)]
    cols = sb("cols", [P, NCOLS])
    ident = sb("ident", [P, P])
    mv = sb("mv", [P, 2, 2])
    stats = sb("stats", [P, 2, 2, 6])
    sd = sb("sd", [P, 2, 1])
    rstd = sb("rstd", [P, 2, 1])
    eps = sb("eps", [P, 1])
    credit = sb("credit", [P, 9])
    ps = [ctx.enter_context(nc.psum_tensor(f"ps{k}", [P, S], F32)) for k in range(4)]
    mod = sb("mod", [P, NMOD, DB])
    ada_sum = sb("ada_sum", [P, 2])

    def col(name, k=0):
        at, n = COLS[name]
        return cols[:, at + k:at + k + 1] if isinstance(k, int) else cols[:, bass.ds(k + at, 1)]

    w_landed = [sem("w_landed0"), sem("w_landed1")]
    w_hi = sem("w_hi")
    w_split = sem("w_split")
    mm_done = sem("mm_done")
    acc_free = sem("acc_free")
    ln_tok, ln_stats, ln_aggr, ln_sd, ln_rstd, ln_norm, ln_feat, ln_x, ln_hi, ln_lo = [
        sem("ln_" + n) for n in ("tok", "stats", "aggr", "sd", "rstd", "norm", "feat", "x", "hi", "lo")]
    g_ready, hh_ready, h_split = sem("g_ready"), sem("hh_ready"), sem("h_split")
    c_in, c_act, ada_done, mod_s = [sem(n) for n in ("c_in", "c_act", "ada_done", "mod_s")]
    ada_in = [sem(f"ada_in{k}") for k in range(2)]
    params, xh_ready, xl_ready = sem("params"), sem("xh_ready"), sem("xl_ready")

    class Product:
        count = 0

        def __init__(self, n, src):
            self.base, self.n, self.src = Product.count, n, src
            Product.count += n

    def load(sp, g, i, k):
        slot, src = (g.base + k) % 2, g.src(i, k)
        sp.wait_ge(w_split, g.base + 2 * i + k + 1)
        sp.dma_start(stage[slot][:, 0:src.shape[-1]], src).then_inc(w_landed[slot], 16)

    def load_all(sp, g, following, beside=None):
        beside = beside or (lambda i, k: None)
        if g.n >= 4:
            with sp.Fori(1, g.n // 2) as i:
                for k in range(2):
                    load(sp, g, i, k)
                    beside(i - 1, k)
        if g.n % 2:
            load(sp, g, g.n // 2, 0)
        if following:
            for k in range(2):
                load(sp, following, 0, k)
                beside(g.n // 2 - 1, k)

    def split_hi(act, g, i, k):
        slot = (g.base + k) % 2
        act.wait_ge(w_landed[slot], 16 * ((g.base + k) // 2 + 1) + 16 * i)
        act.wait_ge(mm_done, g.base + 2 * i + k + 1)
        act.activation(whi[slot][:], stage[slot][:], ACT.Copy).then_inc(w_hi, 1)

    def split_lo(dve, g, i, k):
        slot = (g.base + k) % 2
        dve.wait_ge(w_hi, g.base + 2 * i + k + 1)
        dve.tensor_tensor(wlo[slot][:], stage[slot][:], whi[slot][:].bitcast(F32), ALU.subtract).then_inc(w_split, 1)

    def mm_unit(pe, g, i, k, kb, hi, lo, ready=None):
        slot, u = (g.base + k) % 2, g.base + 2 * i + k
        acc = ps[slot]
        pe.wait_ge(w_split, u + 3)
        pe.wait_ge(acc_free, u + 1)
        for b in range(kb):
            if ready and k == 0:
                ready(b)
            w = slice(b * P, (b + 1) * P)
            for wt, xt in ((whi, hi), (whi, lo), (wlo, hi)):
                for h in range(2):
                    done = pe.matmul(acc[:, h * HALF:(h + 1) * HALF], wt[slot][:, w],
                                     xt[:, b, h * HALF:(h + 1) * HALF],
                                     start=b == 0 and wt is whi and xt is hi,
                                     stop=b == kb - 1 and wt is wlo)
        done.then_inc(mm_done, 1)

    def pairs(eng, g, body):
        with eng.Fori(0, g.n // 2) as i:
            body(i)

    def blocks(w):
        return lambda i, k: w[bass.ds(2 * i + k, 1)].rearrange("a p n -> p (a n)")

    def pair_of(w0, w1, at):
        return lambda i, k: (w0, w1)[k][bass.ds(i + at, 1)].rearrange("a p n -> p (a n)")

    def groups(w, lo, hi):
        return lambda i, k: w[bass.ds(2 * i + k, 1), :, lo * P:hi * P].rearrange("a p n -> p (a n)")

    plan = {}

    def ffn_plan(layer):
        for n, (lo, hi) in enumerate(GROUPS_FF):
            plan[f"up{layer}_{n}"] = Product(2 * (hi - lo), pair_of(io[f"w_gate{layer}"], io[f"w_up{layer}"], lo))
            plan[f"down{layer}_{n}"] = Product(DB, groups(io[f"w_down{layer}"], lo, hi))

    plan["in0"] = Product(16, lambda i, k: io["w_in0"][bass.ds(2 * i + k, 1)].rearrange("a p n -> p (a n)"))
    plan["out0"] = Product(DB, blocks(io["w_out0"]))
    ffn_plan(0)
    plan["qkv"] = Product(3 * HEADS, blocks(io["w_qkv"]))
    plan["out1"] = Product(DB, blocks(io["w_qkv"][3 * HEADS:4 * HEADS]))
    ffn_plan(1)
    plan["in2"] = Product(17, blocks(io["w_in2"]))
    plan["dft"] = Product(NT, blocks(io["dft"]))
    plan["out2"] = Product(DB, blocks(io["w_out2"]))
    for n, (lo, hi) in enumerate(GROUPS_FF2):
        plan[f"ff1_{n}"] = Product(hi - lo, lambda i, k, lo=lo: io["w_ff1"][bass.ds(2 * i + k + lo, 1)].rearrange("a p n -> p (a n)"))
        plan[f"ff2_{n}"] = Product(DB, groups(io["w_ff2"], lo, hi))
    order = list(plan.values())

    def after(g):
        n = order.index(g)
        return order[n + 1] if n + 1 < len(order) else None

    first = plan["in0"]
    x_in = [sem(f"x_in{b}") for b in range(DB)]

    def start_sync(sp):
        load(sp, first, 0, 0)
        for b in range(DB):
            sp.dma_start(x[:, b, :], io["x"][:, b, :]).then_inc(x_in[b], 16)
            if b == 0:
                sp.dma_start(cols[:], io["cols"]).then_inc(params, 16)
        load(sp, first, 0, 1)
        sp.dma_start(ident[:], io["ident"]).then_inc(params, 16)

    def start_act(act):
        for b in range(DB):
            act.wait_ge(x_in[b], 16)
            act.activation(xh[:, b, :], x[:, b, :], ACT.Copy).then_inc(xh_ready, 1)
            if b == 0:
                split_hi(act, first, 0, 0)

    def start_dve(dve):
        dve.memset(eps[:], LN_EPS).then_inc(w_split, 1)
        for n, s in enumerate((w_split, mm_done, mm_done, acc_free, acc_free, ada_done, ada_done)):
            dve.memset(credit[:, n:n + 1], 0.0).then_inc(s, 1)
        for b in range(DB):
            dve.wait_ge(xh_ready, b + 1)
            dve.tensor_tensor(xl[:, b, :], x[:, b, :], xh[:, b, :].bitcast(F32), ALU.subtract).then_inc(xl_ready, 1)
            if b == 0:
                split_lo(dve, first, 0, 0)
        dve.wait_ge(params, 32)

    lns, ln_splits = [0], [0]

    def layer_norm(name, src, nblk, gain, bias, dst, split=True):
        base, sbase = lns[0], ln_splits[0]
        lns[0] += NT
        ln_splits[0] += NT if split else 0
        scope = ExitStack()
        xn = sb(name + "_xn", [P, 2, nblk * P], at=scope)
        xt = sb(name + "_xt", [P, 2, nblk, P], at=scope) if dst is None else None
        nsub = nblk * P // HALF

        def target(t, par):
            return xt[:, par] if dst is None else (dst[:, :, t * P:(t + 1) * P] if isinstance(t, int) else dst[:, :, bass.ts(t, P)])

        with nc.Block(no_gpsimd_drain=True) as block:
            @block.tensor
            def _(pe):
                def to_tokens(t):
                    if t >= 2:
                        pe.wait_ge(ln_norm, base + t - 1)
                    for b in range(nblk):
                        done = pe.transpose(ps[t % 2][:, b * P:(b + 1) * P], src[:, b, t * P:(t + 1) * P], ident[:])
                    done.then_inc(ln_tok, 1)

                def to_features(t):
                    pe.wait_ge(ln_norm, base + t + 1)
                    if t >= 2:
                        pe.wait_ge(ln_x, base + t - 1)
                    for b in range(nblk):
                        done = pe.transpose(ps[2 + t % 2][:, b * P:(b + 1) * P], xn[:, t % 2, b * P:(b + 1) * P], ident[:])
                    done.then_inc(ln_feat, 1)

                to_tokens(0)
                to_tokens(1)
                for t in range(NT):
                    to_features(t)
                    if t + 2 < NT:
                        to_tokens(t + 2)

            @block.vector
            def _(dve):
                def statistics(t, par):
                    dve.wait_ge(ln_tok, base + t + 1)
                    for k in range(nsub):
                        done = dve.bn_stats(stats[:, par, k, :], ps[par][:, k * HALF:(k + 1) * HALF])
                    done.then_inc(ln_stats, 1)
                    dve.wait_ge(ln_stats, base + t + 1)
                    dve.bn_aggr(mv[:, par, :], stats[:, par, 0:nsub, :]).then_inc(ln_aggr, 1)

                def normalise(t, par):
                    dve.wait_ge(ln_sd, base + t + 1)
                    dve.reciprocal(rstd[:, par, :], sd[:, par, :]).then_inc(ln_rstd, 1)
                    dve.wait_ge(ln_rstd, base + t + 1)
                    dve.tensor_scalar(xn[:, par, :], ps[par][:, 0:nblk * P], mv[:, par, 0:1], rstd[:, par, :],
                                      ALU.subtract, ALU.mult).then_inc(ln_norm, 1)

                statistics(0, 0)
                statistics(1, 1)
                for t in range(NT):
                    if t >= 2:
                        statistics(t, t % 2)
                    normalise(t, t % 2)
                if split:
                    dve.wait_ge(ln_lo, sbase + NT)

            if split:
                @block.gpsimd
                def _(pool):
                    for t in range(NT):
                        pool.wait_ge(ln_hi, sbase + t + 1)
                        pool.tensor_tensor(xl[:, 0:nblk, t * P:(t + 1) * P], target(t, t % 2),
                                           xh[:, 0:nblk, t * P:(t + 1) * P].bitcast(F32),
                                           ALU.subtract).then_inc(ln_lo, 1)

            @block.scalar
            def _(act):
                def deviation(t, par):
                    act.wait_ge(ln_aggr, base + t + 1)
                    act.activation(sd[:, par, :], mv[:, par, 1:2], ACT.Sqrt, bias=eps[:]).then_inc(ln_sd, 1)

                def affine(t, par, reused):
                    act.wait_ge(ln_feat, base + t + 1)
                    if dst is None and reused:
                        act.wait_ge(ln_lo, sbase + t - 1)
                    for b in range(nblk):
                        done = act.activation(target(t, par)[:, b, :], ps[2 + par][:, b * P:(b + 1) * P], ACT.Identity,
                                              bias=bias(b), scale=gain(b))
                    done.then_inc(ln_x, 1)
                    if split:
                        act.wait_ge(ln_x, base + t + 1)
                        act.activation(xh[:, 0:nblk, bass.ts(t, P)], target(t, par),
                                       ACT.Copy).then_inc(ln_hi, 1)

                deviation(0, 0)
                deviation(1, 1)
                affine(0, 0, False)
                deviation(2, 0)
                affine(1, 1, False)
                with act.Fori(1, (NT - 2) // 2) as i:
                    for k in range(2):
                        deviation(2 * i + k + 1, 1 - k)
                        affine(2 * i + k, k, True)
                deviation(NT - 1, 1)
                affine(NT - 2, 0, True)
                affine(NT - 1, 1, True)
        scope.close()

    def ahead(eng, g, split, rest, split_second=True):
        def body(i, skip=None):
            for k in range(2):
                if k != skip:
                    split(eng, g, i, k + 1)
                rest(i, k)
        if not split_second:
            body(0, 0)
        with eng.Fori(0 if split_second else 1, g.n // 2 - (0 if after(g) else 1)) as i:
            body(i)
        if not after(g):
            body(g.n // 2 - 1, 1)

    def product_pe(pe, g, kb, hi, lo, ready=None):
        def body(i):
            for k in range(2):
                mm_unit(pe, g, i, k, kb, hi, lo, ready)
        pairs(pe, g, body)

    def split_act(act, g, split_second=True):
        ahead(act, g, split_hi, lambda i, k: None, split_second)

    def residual_dve(dve, g, scale, beside=None, split_second=True):
        def rest(i, k):
            blk = x[:, bass.ds(2 * i + k, 1), :].rearrange("p a n -> p (a n)")
            dve.wait_ge(mm_done, g.base + 2 * i + k + 3)
            dve.scalar_tensor_tensor(blk, blk, scale, ps[(g.base + k) % 2][:], ALU.mult, ALU.add).then_inc(acc_free, 1)
            if beside:
                beside(i, k)
        ahead(dve, g, split_lo, rest, split_second)

    def residual_product(g, kb, hi, lo, scale):
        with nc.Block(no_gpsimd_drain=True) as block:
            @block.sync
            def _(sp):
                load_all(sp, g, after(g))

            @block.scalar
            def _(act):
                split_act(act, g)

            @block.vector
            def _(dve):
                residual_dve(dve, g, scale)

            @block.tensor
            def _(pe):
                product_pe(pe, g, kb, hi, lo)

    ffn_pairs = [0]

    def swiglu(layer):
        scope = ExitStack()
        hh = sb(f"hh{layer}", [P, DB, S], F32R, at=scope)
        hl = sb(f"hl{layer}", [P, DB, S], F32R, at=scope)
        g_t = sb(f"g_t{layer}", [P, S], at=scope)
        h_t = sb(f"h_t{layer}", [P, S], at=scope)
        c_row = sb(f"c_row{layer}", [P, D], at=scope)
        ada = [sb(f"ada{layer}_{k}", [P, D], at=scope) for k in range(2)]
        runs = []
        for n, (lo, hi) in enumerate(GROUPS_FF):
            runs.append((plan[f"up{layer}_{n}"], plan[f"down{layer}_{n}"], hi - lo, ffn_pairs[0], (layer * len(GROUPS_FF) + n) * DB))
            ffn_pairs[0] += hi - lo

        with nc.Block(no_gpsimd_drain=True) as block:
            @block.sync
            def _(sp):
                sp.dma_start(c_row[:], io["c_rows"]).then_inc(c_in, 16)
                for up, down, kb, base, ada_at in runs:
                    def ada_load(i, k):
                        u = 2 * i + (k + ada_at)
                        sp.wait_ge(ada_done, u + 1)
                        sp.dma_start(ada[k][:], io["w_ada"][bass.ds(u, 1)].rearrange("a p n -> p (a n)")
                                     if not isinstance(u, int) else io["w_ada"][u]).then_inc(ada_in[k], 16)
                    load_all(sp, up, down)
                    load_all(sp, down, after(down), ada_load)

            @block.scalar
            def _(act):
                for n, (up, down, kb, base, ada_at) in enumerate(runs):
                    def body(i):
                        split_hi(act, up, i, 1)
                        act.wait_ge(mm_done, up.base + 2 * i + 3)
                        act.wait_ge(acc_free, up.base + 2 * i + 2)
                        act.activation(g_t[:], ps[up.base % 2][:], ACT.Silu).then_inc(acc_free, 1)
                        split_hi(act, up, i, 2)
                        act.wait_ge(acc_free, up.base + 2 * i + 4)
                        act.activation(hh[:, bass.ds(i, 1), :].rearrange("p a n -> p (a n)"), h_t[:], ACT.Copy).then_inc(hh_ready, 1)
                    pairs(act, up, body)
                    if n == 0:
                        act.wait_ge(c_in, 16 * (layer + 1))
                        act.activation(c_row[:], c_row[:], ACT.Silu).then_inc(c_act, 1)
                    split_act(act, down)

            @block.vector
            def _(dve):
                for n, (up, down, kb, base, ada_at) in enumerate(runs):
                    def body(i):
                        split_lo(dve, up, i, 1)
                        split_lo(dve, up, i, 2)
                        dve.wait_ge(mm_done, up.base + 2 * i + 4)
                        dve.wait_ge(acc_free, up.base + 2 * i + 3)
                        dve.tensor_tensor(h_t[:], g_t[:], ps[(up.base + 1) % 2][:], ALU.mult).then_inc(acc_free, 1)
                        dve.wait_ge(hh_ready, base + i + 1)
                        j = bass.ds(i, 1)
                        dve.tensor_tensor(hl[:, j, :].rearrange("p a n -> p (a n)"), h_t[:],
                                          hh[:, j, :].bitcast(F32).rearrange("p a n -> p (a n)"), ALU.subtract).then_inc(h_split, 1)

                    def modulation(i, k):
                        u = 2 * i + (k + ada_at)
                        dve.wait_ge(ada_in[k], 16 * (ada_at // 2 + 1) + 16 * i)
                        dve.tensor_tensor_reduce(h_t[:], ada[k][:], c_row[:], 1.0, 0.0, ALU.mult, ALU.add,
                                                 ada_sum[:, k:k + 1]).then_inc(ada_done, 1)
                        dve.wait_ge(ada_done, u + 3)
                        dve.tensor_tensor(mod[:].rearrange("p m b -> p (m b)")[:, bass.ds(u, 1)], ada_sum[:, k:k + 1],
                                          col("b_ada", u), ALU.add).then_inc(mod_s, 1)

                    pairs(dve, up, body)
                    if n == 0:
                        dve.wait_ge(c_act, layer + 1)
                    residual_dve(dve, down, ALPHA if n == 0 else 1.0, modulation)

            @block.tensor
            def _(pe):
                for up, down, kb, base, ada_at in runs:
                    def ready(b):
                        if b == 0:
                            pe.wait_ge(h_split, base + kb - 1)
                        if b == kb - 1:
                            pe.wait_ge(h_split, base + kb)
                    product_pe(pe, up, DB, xh, xl)
                    product_pe(pe, down, kb, hh, hl, ready)
        scope.close()

    conv_scope = ExitStack()
    conv = sb("conv", [P, AB, S], at=conv_scope)
    yb = sb("yb", [P, AB, S], at=conv_scope)
    lru_scope = ExitStack()
    PAD_A, PAD_R = CONV_TAPS - 1, LRU_TAPS - 1
    a_pad = sb("a_pad", [P, PAD_A + S], at=lru_scope)
    r_pad = sb("r_pad", [P, PAD_R + S], at=lru_scope)
    sig = sb("sig", [P, S], at=lru_scope)
    rec = sb("rec", [P, S], at=lru_scope)
    gel = sb("gel", [P, S], at=lru_scope)
    w_gates = sb("w_gates", [P, AB + 1, 2, P], at=lru_scope)
    w_now = sb("w_now", [P, 2, P], at=lru_scope)
    sp_l = sb("sp_l", [P, 4, AB], at=lru_scope)
    g_r = sb("g_r", [P, S], at=lru_scope)
    g_i = sb("g_i", [P, S], at=lru_scope)
    a_t = sb("a_t", [P, S], at=lru_scope)
    v_t = sb("v_t", [P, S], at=lru_scope)
    padded, taps, lru_taps = [sem(n) for n in ("padded", "taps", "lru_taps")]
    (wg_in, wg_zero, gate_w, sp_step, gate_mm, gates, decays, root, lru_v, lru_m, lru_u, ya, y_hi, y_lo) = [
        sem(n) for n in ("wg_in", "wg_zero", "gate_w", "sp_step", "gate_mm", "gates", "decays", "root", "lru_v", "lru_m", "lru_u",
                         "ya", "y_hi", "y_lo")]
    gin0 = plan["in0"]
    UPB = 4
    TAPS_BEFORE_REC, TAPS_BEFORE_LRU, TAPS_BEFORE_SCAN = 7, 20, 24

    def split_hi4(act, i, k):
        slot = (gin0.base + k) % 2
        act.wait_ge(w_landed[slot], 16 * ((gin0.base + k) // 2 + 1) + 32 * i)
        act.wait_ge(mm_done, gin0.base + UPB * i + k + 1)
        act.activation(whi[slot][:], stage[slot][:], ACT.Copy).then_inc(w_hi, 1)

    def split_lo4(dve, i, k):
        slot = (gin0.base + k) % 2
        dve.wait_ge(w_hi, gin0.base + UPB * i + k + 1)
        dve.tensor_tensor(wlo[slot][:], stage[slot][:], whi[slot][:].bitcast(F32), ALU.subtract).then_inc(w_split, 1)

    with nc.Block(no_gpsimd_drain=True) as block:
        @block.gpsimd
        def _(pool):
            pool.memset(w_gates[:], 0.0).then_inc(wg_zero, 1)

        @block.sync
        def _(sp):
            start_sync(sp)
            sp.wait_ge(wg_zero, 1)
            for k, w in enumerate(("w_a", "w_x")):
                for half in range(2):
                    q = slice(half * 64, half * 64 + 64)
                    sp.dma_start(w_gates[q, 0:AB, k, q], io[w][half]).then_inc(wg_in, 16)
            load_all(sp, gin0, after(gin0))

        @block.tensor
        def _(pe):
            def ready(b):
                pe.wait_ge(xl_ready, b + 1)

            with pe.Fori(0, AB) as i:
                for q in range(2):
                    for k in range(2):
                        mm_unit(pe, gin0, 2 * i + q, k, DB, xh, xl, ready)
                pe.wait_ge(gate_w, i + 1)
                pe.wait_ge(lru_taps, 2 * LRU_TAPS * i + 2 * LRU_TAPS)
                for k in range(2):
                    for h in range(2):
                        done = pe.matmul(ps[2 + k][:, h * HALF:(h + 1) * HALF], w_now[:, k, :],
                                         rec[:, h * HALF:(h + 1) * HALF], start=True, stop=True)
                done.then_inc(gate_mm, 1)

        @block.scalar
        def _(act):
            start_act(act)
            act.wait_ge(params, 32)
            at, n = COLS["lam"]
            lam = cols[:, at:at + n]
            act.activation(sp_l[:, 0, :], lam, ACT.Abs).then_inc(sp_step, 1)
            act.wait_ge(sp_step, 1)
            act.activation(sp_l[:, 1, :], sp_l[:, 0, :], ACT.Exp, scale=-1.0).then_inc(sp_step, 1)
            act.wait_ge(sp_step, 2)
            act.activation(sp_l[:, 2, :], sp_l[:, 1, :], ACT.Ln, bias=1.0).then_inc(sp_step, 1)
            act.wait_ge(wg_in, 64)
            act.activation(w_now[:], w_gates[:, 0], ACT.Copy).then_inc(gate_w, 1)
            split_hi(act, gin0, 0, 1)
            with act.Fori(0, AB) as i:
                u = gin0.base + UPB * i
                act.wait_ge(mm_done, u + 3)
                act.wait_ge(acc_free, u + 2)
                act.activation(sig[:], ps[0][:], ACT.Sigmoid, bias=col("b_in", UPB * i)).then_inc(acc_free, 1)
                split_hi4(act, i, 2)
                split_hi4(act, i, 3)
                split_hi4(act, i, 4)
                act.wait_ge(mm_done, u + 6)
                act.wait_ge(acc_free, u + 5)
                act.wait_ge(lru_u, i + 6)
                act.activation(gel[:], ps[1][:], ACT.Gelu_apprx_tanh, bias=col("b_in", UPB * i + 3)).then_inc(acc_free, 1)
                split_hi4(act, i, 5)
                act.wait_ge(gate_mm, i + 1)
                act.activation(g_r[:], ps[2][:], ACT.Sigmoid, bias=col("b_a", i)).then_inc(gates, 1)
                act.activation(g_i[:], ps[3][:], ACT.Sigmoid, bias=col("b_x", i)).then_inc(gates, 1)
                act.wait_ge(gates, 2 * i + 1)
                act.activation(v_t[:], g_r[:], ACT.Tanh, scale=sp_l[:, 0, :][:, bass.ds(i, 1)]).then_inc(decays, 1)
                act.activation(a_t[:], g_r[:], ACT.Exp, scale=sp_l[:, 1, :][:, bass.ds(i, 1)]).then_inc(decays, 1)
                act.activation(w_now[:], w_gates[:, bass.ds(i + 1, 1)].rearrange("p a k n -> p (a k) n"), ACT.Copy).then_inc(gate_w, 1)
                act.wait_ge(lru_v, 3 * i + 3)
                act.activation(v_t[:], v_t[:], ACT.Sqrt).then_inc(root, 1)

        @block.vector
        def _(dve):
            start_dve(dve)
            dve.memset(a_pad[:, 0:PAD_A], 0.0).then_inc(padded, 1)
            dve.memset(r_pad[:, 0:PAD_R], 0.0).then_inc(padded, 1)
            dve.wait_ge(padded, 2)
            at, n = COLS["lam"]
            dve.tensor_scalar(sp_l[:, 3, :], cols[:, at:at + n], -1.0, 0.0, ALU.mult, ALU.max).then_inc(lru_u, 1)
            dve.wait_ge(lru_u, 1)
            dve.wait_ge(sp_step, 3)
            dve.tensor_tensor(sp_l[:, 3, :], sp_l[:, 3, :], sp_l[:, 2, :], ALU.add).then_inc(lru_u, 1)
            dve.wait_ge(lru_u, 2)
            dve.tensor_scalar(sp_l[:, 0, :], sp_l[:, 3, :], LRU_C / 2, None, ALU.mult).then_inc(lru_u, 1)
            dve.tensor_scalar(sp_l[:, 1, :], sp_l[:, 3, :], -LRU_C, None, ALU.mult).then_inc(lru_u, 1)
            dve.wait_ge(lru_u, 4)
            for n in range(2):
                dve.memset(credit[:, 7 + n:8 + n], 0.0).then_inc(lru_u, 1)
            split_lo(dve, gin0, 0, 1)
            with dve.Fori(0, AB) as i:
                u = gin0.base + UPB * i

                def tap(t, h, taps_n, pad, dst, w, b, done):
                    src = pad[:, h * HALF + t:h * HALF + t + HALF]
                    if t == 0:
                        dve.tensor_scalar(dst, src, col(w, taps_n * i), col(b, i), ALU.mult, ALU.add).then_inc(done, 1)
                    else:
                        dve.wait_ge(done, 2 * taps_n * i + 2 * (t - 1) + h + 1)
                        dve.scalar_tensor_tensor(dst, src, col(w, taps_n * i + t), dst, ALU.mult, ALU.add).then_inc(done, 1)

                def conv_taps(lo, hi):
                    for t in range(lo, hi):
                        for h in range(2):
                            dst = conv[:, bass.ds(i, 1), h * HALF:(h + 1) * HALF].rearrange("p a n -> p (a n)")
                            tap(t, h, CONV_TAPS, a_pad, dst, "conv_w", "conv_b", taps)

                split_lo4(dve, i, 2)
                dve.wait_ge(mm_done, u + 4)
                dve.wait_ge(acc_free, u + 3)
                dve.scalar_tensor_tensor(a_pad[:, PAD_A:], ps[1][:], col("b_in", UPB * i + 1), sig[:],
                                         ALU.add, ALU.mult).then_inc(acc_free, 1)
                split_lo4(dve, i, 3)
                dve.wait_ge(acc_free, u + 4)
                conv_taps(0, TAPS_BEFORE_REC)
                dve.wait_ge(mm_done, u + 5)
                dve.tensor_scalar(r_pad[:, PAD_R:], ps[0][:], col("b_in", UPB * i + 2), None, ALU.add).then_inc(acc_free, 1)
                split_lo4(dve, i, 4)
                dve.wait_ge(acc_free, u + 5)
                for t in range(LRU_TAPS):
                    for h in range(2):
                        tap(t, h, LRU_TAPS, r_pad, rec[:, h * HALF:(h + 1) * HALF], "lru_w", "lru_b", lru_taps)
                conv_taps(TAPS_BEFORE_REC, TAPS_BEFORE_LRU)
                split_lo4(dve, i, 5)
                dve.wait_ge(decays, 2 * i + 2)
                dve.scalar_tensor_tensor(a_t[:], a_t[:], 1.0, v_t[:], ALU.add, ALU.mult).then_inc(lru_v, 1)
                dve.wait_ge(lru_v, 3 * i + 1)
                dve.tensor_scalar(v_t[:], v_t[:], 2.0 ** -100, None, ALU.max).then_inc(lru_v, 1)
                dve.tensor_scalar(a_t[:], a_t[:], -1.0, 1.0, ALU.mult, ALU.add).then_inc(lru_v, 1)
                dve.tensor_tensor(rec[:], rec[:], g_i[:], ALU.mult).then_inc(lru_m, 1)
                conv_taps(TAPS_BEFORE_LRU, TAPS_BEFORE_SCAN)
                dve.wait_ge(root, i + 1)
                dve.wait_ge(lru_v, 3 * i + 3)
                dve.scalar_tensor_tensor(v_t[:], a_t[:], 1.0, v_t[:], ALU.add, ALU.mult).then_inc(lru_m, 1)
                dve.wait_ge(lru_m, 4 * i + 2)
                dve.tensor_tensor(rec[:], rec[:], v_t[:], ALU.mult).then_inc(lru_m, 1)
                dve.wait_ge(lru_m, 4 * i + 3)
                dve.tensor_tensor_scan(v_t[:], a_t[:], rec[:], 0.0, ALU.mult, ALU.add).then_inc(lru_m, 1)
                dve.wait_ge(lru_m, 4 * i + 4)
                dve.wait_ge(acc_free, u + 6)
                dve.tensor_tensor(yb[:, bass.ds(i, 1), :].rearrange("p a n -> p (a n)"), v_t[:], gel[:], ALU.mult).then_inc(lru_u, 1)
                conv_taps(TAPS_BEFORE_SCAN, CONV_TAPS)
                dve.wait_ge(taps, 2 * CONV_TAPS * i + 2 * CONV_TAPS)
    lru_scope.close()
    layer_norm("cnorm", conv, AB, lambda b: col("cnorm_g", b), lambda b: col("cnorm_b", b), conv, split=False)
    gout0 = plan["out0"]
    with nc.Block(no_gpsimd_drain=True) as block:
        @block.sync
        def _(sp):
            load_all(sp, gout0, after(gout0))

        @block.tensor
        def _(pe):
            def ready(b):
                pe.wait_ge(y_lo, b + 1)
            product_pe(pe, gout0, DB, xh, xl, ready)

        @block.scalar
        def _(act):
            for j in range(2 * AB):
                src = yb[:, j, :] if j < AB else conv[:, j - AB, :]
                if j >= AB:
                    act.wait_ge(ya, j - AB + 1)
                act.activation(xh[:, j, :], src, ACT.Copy).then_inc(y_hi, 1)
                if AB - 1 <= j < 2 * AB - 1:
                    n = j - AB + 1
                    act.activation(conv[:, n, :], conv[:, n, :], ACT.Silu).then_inc(ya, 1)
            split_act(act, gout0, False)

        @block.vector
        def _(dve):
            for j in range(2 * AB):
                dve.wait_ge(y_hi, j + 1)
                dve.tensor_tensor(xl[:, j, :], yb[:, j, :] if j < AB else conv[:, j - AB, :], xh[:, j, :].bitcast(F32),
                                  ALU.subtract).then_inc(y_lo, 1)
            residual_dve(dve, gout0, ALPHA, split_second=False)
    conv_scope.close()

    def mixed_norm(layer):
        layer_norm(f"mix{layer}", x, DB, lambda b: col("mix_g", layer * DB + b), lambda b: col("mix_b", layer * DB + b), x)

    mixed_norm(0)
    swiglu(0)
    layer_norm("ffn0", x, DB, lambda b: col("ffn_g", b), lambda b: col("ffn_b", b), x)

    attn_scope = ExitStack()
    o_t = sb("o_t", [P, HEADS, S], at=attn_scope)
    ones = sb("ones", [P, P], at=attn_scope)
    lam_t = sb("lam_t", [P, 8], at=attn_scope)
    head_scope = ExitStack()
    cos = sb("cos", [P, S], at=head_scope)
    sin = sb("sin", [P, S], at=head_scope)
    q_rot = [sb(f"q_rot{k}", [P, S], at=head_scope) for k in range(2)]
    k_rot = [sb(f"k_rot{k}", [P, S], at=head_scope) for k in range(2)]
    v_tok = sb("v_tok", [P, NT, P], at=head_scope)
    raw = sb("raw", [P, S], at=head_scope)
    swp = sb("swp", [P, S], at=head_scope)
    e0 = [sb(f"e0_{k}", [P, S - P + P * k], at=head_scope) for k in range(2)]
    e1 = sb("e1", [P, S], at=head_scope)
    a_t2 = [sb(f"a_t2_{k}", [P, HALF], at=head_scope) for k in range(2)]
    mx = sb("mx", [P, 2, 2], at=head_scope)
    nb = sb("nb", [P, 2, 2], at=head_scope)
    den = sb("den", [P, 2, 2], at=head_scope)
    rden = sb("rden", [P, 2, 2], at=head_scope)
    (rope_in, lam_s, lam_mm, lam_e, raw_ready, swapped, rope_a, rope_b, rope_done, sc_done, masked, mxs, nbs, exp0, exp1,
     recs, e1_scaled, attn, tr_done, tr_out, pv_done, o_out) = [sem(n) for n in (
         "rope_in", "lam_s", "lam_mm", "lam_e", "raw_ready", "swapped", "rope_a", "rope_b", "rope_done", "sc_done",
         "masked", "mxs", "nbs", "exp0", "exp1", "recs", "e1_scaled", "attn", "tr_done", "tr_out", "pv_done", "o_out")]
    gq = plan["qkv"]
    SCALE = HEAD_DIM ** -0.5
    acc, pT, pO, pS = ps[0], ps[1][:, 0:HALF], ps[1][:, HALF:S], (ps[2], ps[3])
    QUADS = [(0, 32), (32, 0), (64, 96), (96, 64)]
    UPH = 3
    BATCH = 4
    TPH = 14

    class Head:
        def __init__(self, const, i=0):
            self.const, self.i = const, i
            self.h = const + 2 * i
            self.par = const % 2

        def next(self):
            return Head(self.const + 1, self.i)

        def unit(self, k):
            u = gq.base + UPH * self.const + k
            return u + 2 * UPH * self.i, u % 2, 16 * (u // 2 + 1) + 16 * UPH * self.i

        def n(self, per, k=0):
            return per * self.h + k

    def batch(head, qt, b):
        return head.n(TPH, 2 + qt if qt < 4 else 6 + 2 * (qt - 4) + b)

    def head_hi(act, head, k):
        u, slot, landed = head.unit(k)
        act.wait_ge(w_landed[slot], landed)
        act.wait_ge(mm_done, u + 1)
        act.activation(whi[slot][:], stage[slot][:], ACT.Copy).then_inc(w_hi, 1)

    def head_lo(dve, head, k):
        u, slot, _ = head.unit(k)
        dve.wait_ge(w_hi, u + 1)
        dve.tensor_tensor(wlo[slot][:], stage[slot][:], whi[slot][:].bitcast(F32), ALU.subtract).then_inc(w_split, 1)

    def head_mm(pe, head, n):
        k, b = divmod(n, DB)
        u, slot, _ = head.unit(k)
        if b == 0:
            pe.wait_ge(w_split, u + 3)
            pe.wait_ge(acc_free, u + 2)
        for wt, xt in ((whi, xh), (whi, xl), (wlo, xh)):
            for h in range(2):
                done = pe.matmul(acc[:, h * HALF:(h + 1) * HALF], wt[slot][:, b * P:(b + 1) * P],
                                 xt[:, b, h * HALF:(h + 1) * HALF], start=b == 0 and wt is whi and xt is xh,
                                 stop=b == DB - 1 and wt is wlo)
        if b == DB - 1:
            done.then_inc(mm_done, 1)

    def head_raw(act, head, k):
        u, _, _ = head.unit(k)
        act.wait_ge(mm_done, u + 3)
        if k:
            act.wait_ge(rope_done, head.n(2, k))
        elif not (isinstance(head.h, int) and head.h == 0):
            act.wait_ge(tr_done, head.n(TPH, 2 - TPH))
        act.activation(raw[:], acc[:], ACT.Copy).then_inc(acc_free, 1)

    def head_swap(sp, head, k):
        u, _, _ = head.unit(k)
        sp.wait_ge(acc_free, u + 3)
        for to, of in QUADS:
            sp.dma_start(swp[to:to + 32, :], raw[of:of + 32, :]).then_inc(swapped, 16)

    def head_rope(dve, head, k):
        u, _, _ = head.unit(k)
        dst = (q_rot, k_rot)[k][head.par]
        dve.wait_ge(acc_free, u + 3)
        if not (isinstance(head.h, int) and head.h < 2):
            dve.wait_ge(sc_done, head.n(NT, -NT))
        dve.tensor_tensor(dst[:], raw[:], cos[:], ALU.mult).then_inc(rope_a, 1)
        dve.wait_ge(swapped, 64 * head.n(2, k + 1))
        dve.tensor_tensor(swp[:], swp[:], sin[:], ALU.mult).then_inc(rope_b, 1)
        dve.wait_ge(rope_a, head.n(2, k + 1))
        dve.wait_ge(rope_b, head.n(2, k + 1))
        dve.tensor_tensor(dst[:], dst[:], swp[:], ALU.add).then_inc(rope_done, 1)

    def head_load(sp, head, k):
        u, slot, _ = head.unit(k + 2)
        n = u - gq.base
        sp.wait_ge(w_split, u + 1)
        src = io["w_qkv"][n:n + 1] if isinstance(n, int) else io["w_qkv"][bass.ds(n, 1)]
        sp.dma_start(stage[slot][:], src.rearrange("a p n -> p (a n)")).then_inc(w_landed[slot], 16)

    def scores(pe, head, qt):
        w = (qt + 1) * P
        if qt == 0:
            pe.wait_ge(rope_done, head.n(2, 2))
        if qt or not (isinstance(head.h, int) and head.h == 0):
            pe.wait_ge(exp1, head.n(NT, qt))
        for at in range(0, w, HALF):
            n = min(HALF, w - at)
            for m in range(2):
                f = slice(m * HEAD_DIM, (m + 1) * HEAD_DIM)
                done = pe.matmul(pS[m][:, at:at + n], q_rot[head.par][f, qt * P:(qt + 1) * P],
                                 k_rot[head.par][f, at:at + n], start=True, stop=True)
        done.then_inc(sc_done, 1)

    def weights_t(pe, head, qt, b):
        idx = batch(head, qt, b)
        if b == 0:
            pe.wait_ge(attn, head.n(NT, qt + 1))
        pe.wait_ge(tr_out, idx)
        for j in range(BATCH * b, min(BATCH * (b + 1), qt + 1)):
            done = pe.transpose(pT[:, (j - BATCH * b) * P:(j - BATCH * b + 1) * P], e0[qt % 2][:, j * P:(j + 1) * P], ident[:])
        done.then_inc(tr_done, 1)

    def values_t(pe, head, b):
        u, _, _ = head.unit(2)
        idx = head.n(TPH, b)
        pe.wait_ge(acc_free, u + 3)
        if b or not (isinstance(head.h, int) and head.h == 0):
            pe.wait_ge(tr_out, idx)
        for j in range(BATCH):
            done = pe.transpose(pT[:, j * P:(j + 1) * P], raw[:, (BATCH * b + j) * P:(BATCH * b + j + 1) * P], ident[:])
        done.then_inc(tr_done, 1)

    def weighted(pe, head, qt, b):
        idx = batch(head, qt, b)
        pe.wait_ge(tr_out, idx + 1)
        if b == 0 and (qt >= 4 or not (isinstance(head.h, int) and head.h == 0)):
            pe.wait_ge(o_out, head.n(NT, qt - 3))
        at = (qt % 4) * P
        for j in range(BATCH * b, min(BATCH * (b + 1), qt + 1)):
            done = pe.matmul(pO[:, at:at + P], v_tok[:, j, :], a_t2[b][:, (j - BATCH * b) * P:(j - BATCH * b + 1) * P],
                             start=j == 0, stop=j == qt)
        if BATCH * (b + 1) > qt:
            done.then_inc(pv_done, 1)

    def pe_head(pe, head, before, project):
        nxt = head.next()
        for qt in range(NT):
            scores(pe, head, qt)
            if qt == 1:
                values_t(pe, head, 1)
            if project:
                head_mm(pe, nxt, 3 * qt)
            who, tile = (before, NT - 1) if qt == 0 else (head, qt - 1)
            if who:
                weights_t(pe, who, tile, 0)
            if project:
                head_mm(pe, nxt, 3 * qt + 1)
            if who:
                weighted(pe, who, tile, 0)
                if tile >= BATCH:
                    weights_t(pe, who, tile, 1)
            if project:
                head_mm(pe, nxt, 3 * qt + 2)
            if who and tile >= BATCH:
                weighted(pe, who, tile, 1)
            if qt == 0:
                values_t(pe, head, 0)

    def act_weights(act, head, qt, b):
        idx = batch(head, qt, b)
        n = (min(BATCH * (b + 1), qt + 1) - BATCH * b) * P
        act.wait_ge(tr_done, idx + 1)
        tiles = qt - 1 if b == 0 else (qt - 1 if qt > BATCH else (-1))
        if b == 0:
            if qt or not (isinstance(head.h, int) and head.h == 0):
                act.wait_ge(pv_done, head.n(NT, qt))
        elif qt > BATCH or not (isinstance(head.h, int) and head.h == 0):
            act.wait_ge(pv_done, head.n(NT, qt))
        act.activation(a_t2[b][:, 0:n], pT[:, 0:n], ACT.Copy).then_inc(tr_out, 1)

    def act_values(act, head, b):
        act.wait_ge(tr_done, head.n(TPH, b + 1))
        if not (isinstance(head.h, int) and head.h == 0):
            act.wait_ge(pv_done, head.n(NT))
        act.activation(v_tok[:, BATCH * b:BATCH * (b + 1), :].rearrange("p a n -> p (a n)"), pT[:], ACT.Copy).then_inc(tr_out, 1)

    def act_out(act, head, qt):
        act.wait_ge(pv_done, head.n(NT, qt + 1))
        at = (qt % 4) * P
        h = slice(head.h, head.h + 1) if isinstance(head.h, int) else bass.ds(head.h, 1)
        act.activation(o_t[:, h, qt * P:(qt + 1) * P].rearrange("p a n -> p (a n)"), pO[:, at:at + P], ACT.Copy).then_inc(o_out, 1)

    def act_head(act, head, before, project):
        nxt = head.next()
        for qt in range(NT):
            w, par = (qt + 1) * P, qt % 2
            who, tile = (before, NT - 1) if qt == 0 else (head, qt - 1)
            if qt == 1:
                act_values(act, head, 1)
            if who:
                act_weights(act, who, tile, 0)
            act.wait_ge(nbs, head.n(NT, qt + 1))
            act.activation(e0[par][:, 0:w], pS[0][:, 0:w], ACT.Exp, bias=nb[:, par, 0:1], scale=SCALE,
                           accum_out=den[:, par, 0:1]).then_inc(exp0, 1)
            if qt or who:
                act.wait_ge(attn, head.n(NT, qt))
            act.activation(e1[:, 0:w], pS[1][:, 0:w], ACT.Exp, bias=nb[:, par, 1:2], scale=SCALE,
                           accum_out=den[:, par, 1:2]).then_inc(exp1, 1)
            if project and qt == 0:
                head_hi(act, nxt, 1)
            if project and qt == 2:
                head_raw(act, nxt, 0)
                head_hi(act, nxt, 2)
            if project and qt == 5:
                head_raw(act, nxt, 1)
                head_hi(act, nxt, 3)
            if who and tile >= BATCH:
                act_weights(act, who, tile, 1)
            if who:
                act_out(act, who, tile)
            if qt == 0:
                act_values(act, head, 0)
            if project and qt == 7:
                head_raw(act, nxt, 2)

    def dve_head(dve, head, before, project):
        nxt = head.next()
        for qt in range(NT):
            w, par = (qt + 1) * P, qt % 2
            at = qt * P
            dve.wait_ge(sc_done, head.n(NT, qt + 1))
            for m in range(2):
                dve.memset(pS[m][0:CHUNK_MASK, at + CHUNK_MASK:at + P], NEG).then_inc(masked, 1)
            dve.wait_ge(masked, head.n(2 * NT, 2 * qt + 2))
            for m in range(2):
                dve.reduce_max(mx[:, par, m:m + 1], pS[m][:, 0:w], AX).then_inc(mxs, 1)
            dve.wait_ge(mxs, head.n(2 * NT, 2 * qt + 2))
            dve.tensor_scalar(nb[:, par, :], mx[:, par, :], -SCALE, None, ALU.mult).then_inc(nbs, 1)
            if project and qt == 0:
                head_lo(dve, nxt, 1)
            if project and qt == 3:
                head_lo(dve, nxt, 2)
                head_rope(dve, nxt, 0)
            if project and qt == 6:
                head_lo(dve, nxt, 3)
                head_rope(dve, nxt, 1)
            dve.wait_ge(exp1, head.n(NT, qt + 1))
            dve.reciprocal(rden[:, par, :], den[:, par, :]).then_inc(recs, 1)
            dve.wait_ge(recs, head.n(NT, qt + 1))
            dve.tensor_scalar(e1[:, 0:w], e1[:, 0:w], rden[:, par, 1:2], lam_t[:, 4:5], ALU.mult, ALU.mult).then_inc(e1_scaled, 1)
            dve.wait_ge(e1_scaled, head.n(NT, qt + 1))
            dve.scalar_tensor_tensor(e0[par][:, 0:w], e0[par][:, 0:w], rden[:, par, 0:1], e1[:, 0:w],
                                     ALU.mult, ALU.subtract).then_inc(attn, 1)

    def all_heads(eng, run):
        run(eng, Head(0), None, True)
        with eng.Fori(0, (HEADS - 2) // 2) as i:
            run(eng, Head(1, i), Head(0, i), True)
            run(eng, Head(2, i), Head(1, i), True)
        run(eng, Head(HEADS - 1), Head(HEADS - 2), False)

    with nc.Block(no_gpsimd_drain=True) as block:
        @block.sync
        def _(sp):
            sp.dma_start(cos[:], io["cos"]).then_inc(rope_in, 16)
            sp.dma_start(sin[:], io["sin"]).then_inc(rope_in, 16)

            def project(head):
                for k in range(UPH):
                    head_load(sp, head, k)
                    if k < 2:
                        head_swap(sp, head, k)
            project(Head(0))
            project(Head(1))
            with sp.Fori(0, (HEADS - 2) // 2) as i:
                project(Head(2, i))
                project(Head(3, i))

        @block.tensor
        def _(pe):
            pe.wait_ge(lam_s, 3)
            pe.matmul(ps[3][:, 0:2], ones[:], lam_t[:, 0:2], start=True, stop=True).then_inc(lam_mm, 1)
            for n in range(UPH * DB):
                head_mm(pe, Head(0), n)
            pe.wait_ge(lam_e, 1)
            all_heads(pe, pe_head)
            last = Head(HEADS - 1)
            for b in range(2):
                weights_t(pe, last, NT - 1, b)
                weighted(pe, last, NT - 1, b)

        @block.scalar
        def _(act):
            act.wait_ge(lam_mm, 1)
            act.activation(lam_t[:, 2:4], ps[3][:, 0:2], ACT.Exp).then_inc(lam_e, 1)
            for k in range(UPH):
                head_hi(act, Head(0), k + 1)
                head_raw(act, Head(0), k)
            all_heads(act, act_head)
            last = Head(HEADS - 1)
            for b in range(2):
                act_weights(act, last, NT - 1, b)
            act_out(act, last, NT - 1)

        @block.vector
        def _(dve):
            for n in range(2):
                dve.tensor_tensor(lam_t[:, n:n + 1], col(f"lq{n + 1}"), col(f"lk{n + 1}"), ALU.mult).then_inc(lam_s, 1)
            dve.memset(ones[:], 1.0).then_inc(lam_s, 1)
            dve.tensor_scalar(lam_t[:, 5:6], col("subln_g"), 1.0 - LAMBDA_INIT, None, ALU.mult).then_inc(lam_s, 1)
            dve.wait_ge(lam_e, 1)
            dve.tensor_tensor(lam_t[:, 6:7], lam_t[:, 2:3], lam_t[:, 3:4], ALU.subtract).then_inc(lam_s, 1)
            dve.wait_ge(lam_s, 5)
            dve.tensor_scalar(lam_t[:, 4:5], lam_t[:, 6:7], LAMBDA_INIT, None, ALU.add).then_inc(lam_s, 1)
            dve.wait_ge(lam_s, 6)
            dve.wait_ge(rope_in, 32)
            head_lo(dve, Head(0), 1)
            head_lo(dve, Head(0), 2)
            head_rope(dve, Head(0), 0)
            head_lo(dve, Head(0), 3)
            head_rope(dve, Head(0), 1)
            all_heads(dve, dve_head)
    head_scope.close()

    sub_scope = ExitStack()
    sq = sb("sq", [P, 2, S], at=sub_scope)
    rs = sb("rs", [P, HEADS, S], at=sub_scope)
    sub_sq, sub_mm, sub_ln, sub_rs, sub_o, sub_hi, sub_lo = [sem("sub_" + n) for n in ("sq", "mm", "ln", "rs", "o", "hi", "lo")]
    gout1 = plan["out1"]
    with nc.Block(no_gpsimd_drain=True) as block:
        @block.sync
        def _(sp):
            load_all(sp, gout1, after(gout1))

        @block.tensor
        def _(pe):
            for h in range(HEADS):
                pe.wait_ge(sub_sq, h + 1)
                if h >= 2:
                    pe.wait_ge(sub_ln, h - 1)
                for k in range(2):
                    done = pe.matmul(ps[2 + h % 2][:, k * HALF:(k + 1) * HALF], ones[:], sq[:, h % 2, k * HALF:(k + 1) * HALF],
                                     start=True, stop=True)
                done.then_inc(sub_mm, 1)

            def ready(b):
                pe.wait_ge(sub_lo, b + 1)
            product_pe(pe, gout1, DB, xh, xl, ready)

        @block.scalar
        def _(act):
            for h in range(HEADS):
                act.wait_ge(sub_mm, h + 1)
                act.activation(rs[:, h, :], ps[2 + h % 2][:], ACT.Ln, bias=eps[:], scale=1.0 / P).then_inc(sub_ln, 1)

            def high(h):
                act.wait_ge(sub_o, h + 1)
                act.activation(xh[:, h, :], o_t[:, h, :], ACT.Copy).then_inc(sub_hi, 1)

            for h in range(HEADS):
                act.wait_ge(sub_ln, h + 1)
                act.activation(rs[:, h, :], rs[:, h, :], ACT.Exp, scale=-0.5).then_inc(sub_rs, 1)
                if h:
                    high(h - 1)
            high(HEADS - 1)
            split_act(act, gout1)

        @block.vector
        def _(dve):
            for h in range(HEADS):
                if h >= 2:
                    dve.wait_ge(sub_mm, h - 1)
                dve.tensor_tensor(sq[:, h % 2, :], o_t[:, h, :], o_t[:, h, :], ALU.mult).then_inc(sub_sq, 1)
            for h in range(HEADS):
                dve.wait_ge(sub_rs, h + 1)
                dve.scalar_tensor_tensor(o_t[:, h, :], o_t[:, h, :], lam_t[:, 5:6], rs[:, h, :], ALU.mult, ALU.mult).then_inc(sub_o, 1)
                dve.wait_ge(sub_hi, h + 1)
                dve.tensor_tensor(xl[:, h, :], o_t[:, h, :], xh[:, h, :].bitcast(F32), ALU.subtract).then_inc(sub_lo, 1)
            residual_dve(dve, gout1, ALPHA)
    sub_scope.close()
    attn_scope.close()
    mixed_norm(1)
    swiglu(1)
    layer_norm("ffn1", x, DB, lambda b: col("ffn_g", DB + b), lambda b: col("ffn_b", DB + b), x, split=False)

    gb2 = sb("gb2", [P, DB])
    with nc.Block(no_gpsimd_drain=True) as block:
        @block.vector
        def _(dve):
            for first_mod in (1, 4):
                dve.tensor_scalar(mod[:, first_mod:first_mod + 2, :], mod[:, first_mod:first_mod + 2, :], 1.0, None, ALU.add).then_inc(mod_s, 1)
            dve.wait_ge(mod_s, NMOD * DB + 2)
            at, n = COLS["b_ff2"]
            dve.tensor_tensor(gb2[:], mod[:, 5, :], cols[:, at:at + n], ALU.mult).then_inc(mod_s, 1)

    layer_norm("mod1", x, DB, lambda b: mod[:, 1, b:b + 1], lambda b: mod[:, 0, b:b + 1], None)

    mix_scope = ExitStack()
    arena = sb("arena", [P, 17 * S + 8 * MH * (MDV + 1)], at=mix_scope)

    def tile(at, n, tokens=S):
        return arena[:, at * S:(at + n) * S].rearrange("p (a n) -> p a n", n=tokens)

    qt, kt, so, vt, zt, gt = tile(0, 2), tile(2, 2), tile(4, 4), tile(8, 4), tile(12, 4), tile(16, 1)[:, 0, :]
    v1 = arena[:, 17 * S:].rearrange("p (c h d) -> p c h d", c=NT, h=MH)
    yf = zt
    k_tok = tile(8, 2, MH * MDK)
    lf, bb, a_r, mt, wk, wint = [arena[0:64, n * S:(n + 1) * S] for n in (10, 11, 12, 13, 14, 15)]
    keep, lift = wk, wint
    gates_t = gt[0:64, :]
    kw = arena[:, 12 * S:13 * S].rearrange("p (c e d) -> p c e d", c=NT, e=2)
    h_tok = arena[:, 12 * S:13 * S].rearrange("p (c d) -> p c d", c=NT)

    def w_dirs(h):
        return (tile(10, 1)[:, 0, :], tile(11, 1)[:, 0, :]) if h % 2 else (stage[0][:], stage[1][:])
    cst = arena[:, 14 * S:14 * S + 7 * (MDV + 1)].rearrange("p (c d) -> p c d", c=7)
    qs = gt
    gin2, gdft = plan["in2"], plan["dft"]

    in2_out = sem("in2_out")
    with nc.Block(no_gpsimd_drain=True) as block:
        @block.sync
        def _(sp):
            load_all(sp, gin2, gdft)

        @block.tensor
        def _(pe):
            def body(i):
                for k in range(2):
                    mm_unit(pe, gin2, i, k, DB, xh, xl)
            pairs(pe, gin2, body)
            mm_unit(pe, gin2, gin2.n // 2, 0, DB, xh, xl)

        @block.vector
        def _(dve):
            def body(i):
                for k in range(2):
                    split_lo(dve, gin2, i, k + 1)
            pairs(dve, gin2, body)
            split_lo(dve, gin2, gin2.n // 2, 1)

        @block.scalar
        def _(act):
            def out_of(i, k, dst, func=ACT.Copy, **more):
                act.wait_ge(mm_done, gin2.base + 2 * i + k + 3)
                act.activation(dst, ps[(gin2.base + k) % 2][:], func, **more).then_inc(acc_free, 1)
            places = ([(zt[:, b, :], ACT.Copy, {}) for b in range(4)]
                      + [(qt[:, b, :], ACT.Copy, dict(scale=MDK ** -0.5)) for b in range(2)]
                      + [(kt[:, b, :], ACT.Copy, {}) for b in range(2)]
                      + [(vt[:, b, :], ACT.Copy, {}) for b in range(4)]
                      + [(so[:, b, :], ACT.Sigmoid, {}) for b in range(4)]
                      + [(gt, ACT.Identity, dict(bias=col("b_gate")))])
            for n, (dst, func, more) in enumerate(places):
                split_hi(act, gin2, n // 2, n % 2 + 1)
                out_of(n // 2, n % 2, dst, func, **more)

    ones_col = sem("ones_col")
    cs_in, ch_mm, ch_hi, ch_lo, q_out, y_out, y_tr, yf_out = [sem(n) for n in (
        "cs_in", "ch_mm", "ch_hi", "ch_lo", "q_out", "y_out", "y_tr", "yf_out")]
    ch_alt = sem("ch_alt")
    cs = arena[:, 17 * S:17 * S + 2 * P]
    alt = [arena[:, 17 * S + 2 * P + 4 * n:17 * S + 2 * P + 4 * n + 4] for n in range(3)]

    def half_tile(n):
        at = 17 * S + HALF + n * HALF
        return arena[:, at:at + HALF]

    y_sin = [half_tile(k) for k in range(2)]
    y_sum, y_dif = [half_tile(2 + k) for k in range(2)], [half_tile(4 + k) for k in range(2)]
    xhv, xlv = [t[:].rearrange("p a (b n) -> p (a b) n", n=HALF) for t in (xh, xl)]
    with nc.Block(no_gpsimd_drain=True) as block:
        @block.sync
        def _(sp):
            sp.dma_start(cs, io["dft_channel"]).then_inc(cs_in, 16)

        @block.tensor
        def _(pe):
            pe.wait_ge(cs_in, 16)
            for n in range(NT):
                if n >= 2:
                    pe.wait_ge(ch_lo, 2 * n - 2)
                for g in range(4):
                    done = pe.matmul(ps[n % 2][:, g * 2 * P:(g + 1) * 2 * P], zt[:, g, n * P:(n + 1) * P], cs, start=True, stop=True)
                done.then_inc(ch_mm, 1)
            pe.wait_ge(ch_alt, 3)
            pe.matmul(ps[2][:, 0:4], cs[:, 0:P], alt[2], start=True, stop=True)

        @block.scalar
        def _(act):
            for n in range(NT):
                act.wait_ge(ch_mm, n + 1)
                part = ps[n % 2][:].rearrange("p (g e c) -> p g e c", g=4, e=2)
                for e in range(2):
                    act.activation(xhv[:, NT * e + n, :].rearrange("p (g c) -> p g c", g=4), part[:, :, e, :], ACT.Copy).then_inc(ch_hi, 1)

        @block.vector
        def _(dve):
            for n in range(2):
                dve.reduce_sum(alt[n], zt.rearrange("p g (t e) -> p g t e", e=2)[:, :, :, n], AX).then_inc(ch_alt, 1)
            dve.wait_ge(ch_alt, 2)
            dve.tensor_tensor(alt[2], alt[0], alt[1], ALU.subtract).then_inc(ch_alt, 1)
            for n in range(NT):
                part = ps[n % 2][:].rearrange("p (g e c) -> p g e c", g=4, e=2)
                dve.wait_ge(ch_hi, 2 * n + 2)
                for e in range(2):
                    dve.tensor_tensor(xlv[:, NT * e + n, :].rearrange("p (g c) -> p g c", g=4), part[:, :, e, :],
                                      xhv[:, NT * e + n, :].bitcast(F32).rearrange("p (g c) -> p g c", g=4), ALU.subtract).then_inc(ch_lo, 1)

    with nc.Block(no_gpsimd_drain=True) as block:
        @block.sync
        def _(sp):
            load_all(sp, gdft, None)

        @block.tensor
        def _(pe):
            def transposes(t):
                pe.wait_ge(y_out, 2 * t + 2)
                pe.wait_ge(yf_out, max(2 * t - 1, 1))
                for n, part in enumerate((y_sum, y_dif)):
                    for g in range(4):
                        done = pe.transpose(ps[2 + t % 2][:, n * HALF + g * P:n * HALF + (g + 1) * P], part[t % 2][:, g * P:(g + 1) * P], ident[:])
                done.then_inc(y_tr, 1)

            for t in range(NT // 2):
                pe.wait_ge(acc_free, gdft.base + 2 * t)
                for k in range(2):
                    slot = (gdft.base + k) % 2
                    pe.wait_ge(w_split, gdft.base + 2 * t + k + 3)
                    for b in range(DB):
                        for wt, xt in ((whi, xhv), (whi, xlv), (wlo, xhv)):
                            done = pe.matmul(ps[t % 2][:, k * HALF:(k + 1) * HALF], wt[slot][:, b * P:(b + 1) * P], xt[:, NT * k + b, :],
                                             start=b == 0 and wt is whi and xt is xhv, stop=b == DB - 1 and wt is wlo)
                    done.then_inc(mm_done, 1)
                if t:
                    transposes(t - 1)
            transposes(NT // 2 - 1)

        @block.scalar
        def _(act):
            def out_of(t):
                act.wait_ge(y_tr, t + 1)
                act.activation(yf[:, :, t * P:(t + 1) * P], ps[2 + t % 2][:, 0:HALF].rearrange("p (g c) -> p g c", g=4), ACT.Copy).then_inc(yf_out, 1)
                skip = 1 if t == 0 else 0
                act.activation(yf[:, :, S - t * P - skip:S - (t + 1) * P:-1],
                               ps[2 + t % 2][:, HALF:S].rearrange("p (g c) -> p g c", g=4)[:, :, skip:P], ACT.Copy).then_inc(yf_out, 1)

            act.activation(yf[:, :, HALF:HALF + 1], ps[2][:, 0:4].rearrange("p (g c) -> p g c", g=4), ACT.Copy, scale=S ** -0.5).then_inc(yf_out, 1)
            for t in range(NT // 2):
                split_hi(act, gdft, t, 1)
                if t + 1 < NT // 2:
                    split_hi(act, gdft, t, 2)
                act.wait_ge(mm_done, gdft.base + 2 * t + 4)
                act.wait_ge(acc_free, gdft.base + 2 * t)
                act.activation(y_sin[t % 2], ps[t % 2][:, HALF:S], ACT.Copy).then_inc(q_out, 1)
                if t:
                    out_of(t - 1)
            out_of(NT // 2 - 1)

        @block.vector
        def _(dve):
            for t in range(NT // 2):
                split_lo(dve, gdft, t, 1)
                if t + 1 < NT // 2:
                    split_lo(dve, gdft, t, 2)
                dve.wait_ge(q_out, t + 1)
                if t >= 2:
                    dve.wait_ge(y_tr, t - 1)
                dve.tensor_tensor(y_sum[t % 2], ps[t % 2][:, 0:HALF], y_sin[t % 2], ALU.add).then_inc(y_out, 1)
                dve.tensor_tensor(y_dif[t % 2], ps[t % 2][:, 0:HALF], y_sin[t % 2], ALU.subtract).then_inc(y_out, 1)
                dve.wait_ge(y_out, 2 * t + 2)
                dve.memset(credit[:, 0:1], 0.0).then_inc(acc_free, 2)

    kv_tr, kv_out, yf_hi, yf_lo = [sem(n) for n in ("kv_tr", "kv_out", "yf_hi", "yf_lo")]
    with nc.Block(no_gpsimd_drain=True) as block:
        @block.tensor
        def _(pe):
            for n in range(6):
                src = vt[:, n, :] if n < 4 else kt[:, n - 4, :]
                if n >= 2:
                    pe.wait_ge(kv_out, n - 1)
                for c in range(NT):
                    done = pe.transpose(ps[n % 2][:, c * P:(c + 1) * P], src[:, c * P:(c + 1) * P], ident[:])
                done.then_inc(kv_tr, 1)

        @block.scalar
        def _(act):
            for n in range(6):
                act.wait_ge(kv_tr, n + 1)
                if n == 4:
                    act.wait_ge(kv_tr, 4)
                dst = v1[:, :, n, 0:MDV] if n < 4 else k_tok[:, :, (n - 4) * P:(n - 3) * P]
                act.activation(dst, ps[n % 2][:].rearrange("p (c d) -> p c d", c=NT), ACT.Copy).then_inc(kv_out, 1)
            act.activation(xh[:, MH:2 * MH, :], yf, ACT.Copy).then_inc(yf_hi, 1)

        @block.vector
        def _(dve):
            dve.memset(v1[:, :, :, MDV:MDV + 1], 1.0).then_inc(ones_col, 1)
            dve.wait_ge(yf_hi, 1)
            dve.tensor_tensor(xl[:, MH:2 * MH, :], yf, xh[:, MH:2 * MH, :].bitcast(F32), ALU.subtract).then_inc(yf_lo, 1)

    small = sb("small", [P, 8, NT + 1], at=mix_scope)
    amx, bl, m_in, m_out, m_end, dec = [small[0:64, n, 0:NT] for n in range(6)]
    m_scan = small[0:64, 6, :]
    colt = sb("colt", [P, 3, NT, 2, MH], at=mix_scope)
    decay = sb("decay", [P, MH, NT], at=mix_scope)
    gs, ga, sl, row_tr, row_out, dec_mm = [sem(n) for n in ("gs", "ga", "sl", "row_tr", "row_out", "dec_mm")]
    DIRS = (slice(0, 32), slice(32, 64))

    def chunks(t):
        return t.rearrange("p (c n) -> p c n", c=NT)

    def over(t):
        return t.rearrange("p (c o) -> p c o", o=1).to_broadcast([64, NT, P])

    with nc.Block(no_gpsimd_drain=True) as block:
        @block.scalar
        def _(act):
            act.activation(lf, gt[64:128, :], ACT.Abs).then_inc(ga, 1)
            act.wait_ge(ga, 1)
            act.activation(lf, lf, ACT.Exp, scale=-1.0).then_inc(ga, 1)
            act.wait_ge(ga, 2)
            act.activation(lf, lf, ACT.Ln, bias=1.0).then_inc(ga, 1)
            act.wait_ge(gs, 17)
            act.activation(wk, wk, ACT.Exp).then_inc(ga, 1)
            act.activation(wint, wint, ACT.Exp).then_inc(ga, 1)
            act.activation(lf, lf, ACT.Exp, scale=-1.0).then_inc(ga, 1)
            act.activation(dec, dec, ACT.Exp).then_inc(ga, 1)
            for n in range(3):
                act.wait_ge(row_tr, n + 1)
                part = ps[n][:, 0:HALF].rearrange("p (c e r) -> p c e r", c=NT, e=2)[:, :, :, 0:MH]
                act.activation(colt[:, n], part, ACT.Copy).then_inc(row_out, 1)
            act.wait_ge(dec_mm, 1)
            for e in range(2):
                f = slice(e * 64, (e + 1) * 64)
                act.activation(decay[f].rearrange("p h c -> p (h c)"), ps[3][f, e * MH * NT:(e + 1) * MH * NT], ACT.Copy).then_inc(row_out, 1)

        @block.vector
        def _(dve):
            n = [0]

            def step(done, last=True):
                done.then_inc(gs, 1)
                n[0] += 1
                if last:
                    dve.wait_ge(gs, n[0])

            step(dve.memset(keep, 1.0), False)
            step(dve.memset(lift, 0.0))
            for e, t in ((0, 0), (1, P - 1)):
                step(dve.memset(chunks(keep)[DIRS[e], :, t:t + 1], 0.0), False)
                step(dve.memset(chunks(lift)[DIRS[e], :, t:t + 1], NEG), False)
            step(dve.tensor_scalar(bb, gt[64:128, :], 0.0, None, ALU.min))
            dve.wait_ge(ga, 3)
            step(dve.tensor_tensor(lf, bb, lf, ALU.subtract))
            step(dve.tensor_tensor_scan(bb[DIRS[0]], keep[DIRS[0]], lf[DIRS[0]], 0.0, ALU.mult, ALU.add), False)
            step(dve.tensor_tensor_scan(bb[DIRS[1], ::-1], keep[DIRS[1], ::-1], lf[DIRS[1], ::-1], 0.0, ALU.mult, ALU.add))
            step(dve.tensor_tensor(a_r, gates_t, bb, ALU.subtract))
            step(dve.tensor_tensor_scan(mt[DIRS[0]], lift[DIRS[0]], a_r[DIRS[0]], 0.0, ALU.add, ALU.max), False)
            step(dve.tensor_tensor_scan(mt[DIRS[1], ::-1], lift[DIRS[1], ::-1], a_r[DIRS[1], ::-1], 0.0, ALU.add, ALU.max))
            m = [0]

            def little(done, last=True):
                done.then_inc(sl, 1)
                m[0] += 1
                if last:
                    dve.wait_ge(sl, m[0])

            for e, t in ((0, P - 1), (1, 0)):
                little(dve.tensor_copy(amx[DIRS[e]].rearrange("p (c o) -> p c o", o=1), chunks(mt)[DIRS[e], :, t:t + 1]), False)
                little(dve.tensor_copy(bl[DIRS[e]].rearrange("p (c o) -> p c o", o=1), chunks(bb)[DIRS[e], :, t:t + 1]), False)
            little(dve.memset(m_scan, 0.0))
            little(dve.tensor_tensor_scan(m_scan[DIRS[0], 1:NT + 1], amx[DIRS[0]], bl[DIRS[0]], 0.0, ALU.max, ALU.add), False)
            back = slice(NT - 1, None, -1)
            little(dve.tensor_tensor_scan(m_scan[DIRS[1], back], amx[DIRS[1], ::-1], bl[DIRS[1], ::-1], 0.0, ALU.max, ALU.add))
            little(dve.tensor_copy(m_in[DIRS[0]], m_scan[DIRS[0], 0:NT]), False)
            little(dve.tensor_copy(m_in[DIRS[1]], m_scan[DIRS[1], 1:NT + 1]))
            little(dve.tensor_tensor(m_end, m_in, amx, ALU.max))
            little(dve.tensor_tensor(dec, m_in, m_end, ALU.subtract), False)
            step(dve.tensor_tensor(chunks(mt), chunks(mt), over(m_in), ALU.max))
            step(dve.tensor_tensor(chunks(wk), chunks(a_r), over(m_end), ALU.subtract), False)
            step(dve.tensor_tensor(chunks(wint), over(m_in), chunks(mt), ALU.subtract), False)
            step(dve.tensor_tensor(lf, bb, mt, ALU.add), False)
            assert n[0] == 17, n

        @block.tensor
        def _(pe):
            pe.wait_ge(ga, 7)
            for n, src in enumerate((a_r, wk, lf)):
                for c in range(NT):
                    done = pe.transpose(ps[n][:, c * 64:(c + 1) * 64], src[:, c * P:(c + 1) * P], ident[0:64, 0:64])
                done.then_inc(row_tr, 1)
            for e in range(2):
                for h in range(MH):
                    r = 32 * e + h
                    done = pe.matmul(ps[3][:, (e * MH + h) * NT:(e * MH + h + 1) * NT], ident[0:64, r:r + 1].to_broadcast([64, P]), dec,
                                     start=True, stop=True)
            done.then_inc(dec_mm, 1)

    spare = arena[:, 14 * S + 7 * (MDV + 1):15 * S]
    den_t = spare[:, 0:16].rearrange("p (e c) -> p e c", e=2)
    hst = spare[:, 16:64].rearrange("p (c k) -> p c k", c=NT)
    hmv = spare[:, 64:80].rearrange("p (c k) -> p c k", c=NT)
    hrs = spare[:, 80:88]
    (m_sc, m_bc, m_bcu, m_sel, m_w, m_kw, m_u, m_chain, m_pt, m_num, m_den, m_rden, m_hh, m_stat, m_mv, m_sd, m_rs, m_hn,
     m_tr, m_y, m_hi, m_lo) = [sem("m_" + n) for n in ("sc", "bc", "bcu", "sel", "w", "kw", "u", "chain", "pt", "num", "den",
                                                       "rden", "hh", "stat", "mv", "sd", "rs", "hn", "tr", "y", "hi", "lo")]
    W1 = MDV + 1
    PER_BANK = HALF // W1
    BANKS = [ps[2][:, 0:HALF], ps[2][:, HALF:S], ps[3][:, 0:HALF]]
    BANK_CHUNKS = [(b * PER_BANK, min((b + 1) * PER_BANK, NT)) for b in range(3)]
    CHAIN = NT - 1

    def place(c):
        return BANKS[c // PER_BANK][:, (c % PER_BANK) * W1:(c % PER_BANK + 1) * W1]

    def state(e, c):
        return cst[e * 64:(e + 1) * 64, c - 1 if e == 0 else c, :]

    gout2 = plan["out2"]
    with nc.Block(no_gpsimd_drain=True) as block:
        @block.sync
        def _(sp):
            sp.wait_ge(m_stat, 2 * (MH - 2) + 1)
            for k in range(2):
                load(sp, gout2, 0, k)

        @block.tensor
        def _(pe):
            def spread(h, e, src):
                r = 32 * e + h
                for k in range(2):
                    q = slice(k * HALF, (k + 1) * HALF)
                    done = pe.matmul(ps[1][:, q], ident[0:64, r:r + 1].to_broadcast([64, P]), src[:, q], start=True, stop=True)
                done.then_inc(m_bc, 1)

            def stabilisers(h, e):
                if h or e:
                    pe.wait_ge(m_bcu, 4 * h + e)
                spread(h, e, mt)

            def state_weights(h, e):
                pe.wait_ge(m_bcu, 4 * h + 2 + e)
                if h and e == 0:
                    pe.wait_ge(m_y, h)
                spread(h, e, wint)

            def numerators(h, e):
                pe.wait_ge(m_chain, 2 * CHAIN * (h + 1))
                pe.wait_ge(m_pt, 2 * h + e + 1)
                pe.wait_ge(m_bcu, 4 * h + 3 + e)
                if e:
                    pe.wait_ge(m_hh, 6 * h + 3)
                for c in range(NT):
                    t = slice(c * P, (c + 1) * P)
                    stateless = c == (0 if e == 0 else NT - 1)
                    done = pe.matmul(place(c), w_dirs(h)[e][:, t], v1[:, c, h, :], start=True, stop=stateless)
                    if not stateless:
                        done = pe.matmul(place(c), qs[e * 64:(e + 1) * 64, t], state(e, c), start=False, stop=True)
                done.then_inc(m_num, 1)

            def output(h):
                pe.wait_ge(m_hn, h + 1)
                pe.wait_ge(m_bcu, min(4 * h + 6, 4 * MH))
                for c in range(NT):
                    done = pe.transpose(ps[1][:, c * P:(c + 1) * P], h_tok[:, c, :], ident[:])
                done.then_inc(m_tr, 1)

            for e in range(2):
                stabilisers(0, e)
            for h in range(MH):
                hb = slice((h % 2) * 64, (h % 2) * 64 + 64)
                if h:
                    pe.wait_ge(m_pt, 2 * h)
                for c in range(NT):
                    t = slice(c * P, (c + 1) * P)
                    done = pe.matmul(ps[0][:, t], kt[hb, h // 2, t], qt[hb, h // 2, t], start=True, stop=True)
                done.then_inc(m_sc, 1)
                if h:
                    output(h - 1)
                pe.wait_ge(m_kw, 2 * h + 2)
                if h:
                    pe.wait_ge(m_hh, 6 * h)
                for c in range(NT):
                    done = pe.matmul(place(c), kw[:, c, :, :].rearrange("p e d -> p (e d)"), v1[:, c, h, :], start=True, stop=True)
                done.then_inc(m_u, 1)
                for e in range(2):
                    state_weights(h, e)
                for e in range(2):
                    if h + 1 < MH:
                        stabilisers(h + 1, e)
                    numerators(h, e)
            output(MH - 1)

        @block.gpsimd
        def _(pool):
            for h in range(MH):
                for e, w in enumerate(w_dirs(h)):
                    pool.wait_ge(m_bcu, 4 * h + e + 1)
                    pool.affine_select(out=chunks(w), in_=chunks(w), compare_op=ALU.is_ge, fill=-NEG, base=0,
                                       pattern=[[0, NT], [1 - 2 * e, P]], channel_multiplier=2 * e - 1).then_inc(m_sel, 1)

        @block.scalar
        def _(act):
            def weights(h):
                for e, w in enumerate(w_dirs(h)):
                    act.wait_ge(m_sel, 2 * h + e + 1)
                    act.activation(w, w, ACT.Exp, scale=-1.0).then_inc(m_w, 1)

            weights(0)
            for h in range(MH):
                if h + 1 < MH:
                    weights(h + 1)
                act.wait_ge(m_mv, h + 1)
                act.activation(hrs, hmv[:, :, 1], ACT.Sqrt, bias=eps[:]).then_inc(m_sd, 1)
                if h == MH - 1:
                    split_hi(act, gout2, 0, 0)
                act.wait_ge(m_y, h + 1)
                act.activation(xh[:, h, :], so[:, h, :], ACT.Copy).then_inc(m_hi, 1)

        @block.vector
        def _(dve):
            def exponents(h, e):
                dve.wait_ge(m_bc, 4 * h + e + 1)
                dve.tensor_tensor(chunks(w_dirs(h)[e]), chunks(ps[1][:]), colt[:, 0, :, e, h:h + 1].to_broadcast([P, NT, P]),
                                  ALU.subtract).then_inc(m_bcu, 1)

            def weighted_keys(h):
                for e in range(2):
                    dve.tensor_tensor(kw[:, :, e, :], k_tok[:, :, h * MDK:(h + 1) * MDK],
                                      colt[:, 1, :, e, h:h + 1].to_broadcast([P, NT, MDK]), ALU.mult).then_inc(m_kw, 1)

            def state_queries(h, e):
                hb = slice((h % 2) * 64, (h % 2) * 64 + 64)
                dve.wait_ge(m_bc, 4 * h + e + 3)
                dve.tensor_tensor(qs[e * 64:(e + 1) * 64, :], qt[hb, h // 2, :], ps[1][hb, :], ALU.mult).then_inc(m_bcu, 1)

            def states(h):
                dve.wait_ge(m_u, h + 1)
                done = 2 * CHAIN * h
                for n in range(CHAIN):
                    for e in range(2):
                        f = slice(e * 64, (e + 1) * 64)
                        c, to = (n, n + 1) if e == 0 else (NT - 1 - n, NT - 2 - n)
                        if n == 0:
                            dve.tensor_copy(state(e, to), place(c)[f]).then_inc(m_chain, 1)
                        else:
                            dve.wait_ge(m_chain, done - 1)
                            dve.scalar_tensor_tensor(state(e, to), state(e, c), decay[f, h, c:c + 1], place(c)[f],
                                                     ALU.mult, ALU.add).then_inc(m_chain, 1)
                        done += 1

            def weighted_scores(h):
                for e, w in enumerate(w_dirs(h)):
                    dve.wait_ge(m_w, 2 * h + e + 1)
                    if e == 0:
                        dve.wait_ge(m_sc, h + 1)
                    dve.tensor_tensor(w, ps[0][:], w, ALU.mult).then_inc(m_pt, 1)

            def quotient(h, e):
                dve.wait_ge(m_num, 2 * h + e + 1)
                for b, (c0, c1) in enumerate(BANK_CHUNKS):
                    part = BANKS[b][:, 0:(c1 - c0) * W1].rearrange("p (c d) -> p c d", d=W1)
                    dve.tensor_tensor(den_t[:, e, c0:c1].rearrange("p (c o) -> p c o", o=1), part[:, :, MDV:W1],
                                      colt[:, 2, c0:c1, e, h:h + 1], ALU.max).then_inc(m_den, 1)
                for b, (c0, c1) in enumerate(BANK_CHUNKS):
                    part = BANKS[b][:, 0:(c1 - c0) * W1].rearrange("p (c d) -> p c d", d=W1)
                    d = den_t[:, e, c0:c1].rearrange("p (c o) -> p c o", o=1)
                    dve.wait_ge(m_den, 12 * h + 6 * e + b + 1)
                    dve.scalar_tensor_tensor(d, part[:, :, MDV:W1], -1.0, d, ALU.mult, ALU.max).then_inc(m_den, 1)
                dve.wait_ge(m_den, 12 * h + 6 * e + 6)
                dve.reciprocal(den_t[:, e, :], den_t[:, e, :]).then_inc(m_rden, 1)
                dve.wait_ge(m_rden, 2 * h + e + 1)
                for b, (c0, c1) in enumerate(BANK_CHUNKS):
                    part = BANKS[b][:, 0:(c1 - c0) * W1].rearrange("p (c d) -> p c d", d=W1)[:, :, 0:MDV]
                    r = den_t[:, e, c0:c1].rearrange("p (c o) -> p c o", o=1).to_broadcast([P, c1 - c0, MDV])
                    dst = h_tok if e == 0 else chunks(w_dirs(h)[0])
                    dve.tensor_tensor(dst[:, c0:c1, :], part, r, ALU.mult).then_inc(m_hh, 1)

            def statistics(h):
                dve.wait_ge(m_hh, 6 * h + 6)
                dve.tensor_tensor(h_tok, h_tok, chunks(w_dirs(h)[0]), ALU.add).then_inc(m_stat, 1)
                dve.wait_ge(m_stat, 2 * h + 1)
                for c in range(NT):
                    done = dve.bn_stats(hst[:, c, :], h_tok[:, c, :])
                done.then_inc(m_stat, 1)
                dve.wait_ge(m_stat, 2 * h + 2)
                for c in range(NT):
                    done = dve.bn_aggr(hmv[:, c, :], hst[:, c, :])
                done.then_inc(m_mv, 1)

            def normalise(h):
                dve.wait_ge(m_sd, h + 1)
                dve.reciprocal(hrs, hrs).then_inc(m_rs, 1)
                dve.wait_ge(m_rs, h + 1)
                for c in range(NT):
                    done = dve.tensor_scalar(h_tok[:, c, :], h_tok[:, c, :], hmv[:, c, 0:1], hrs[:, c:c + 1], ALU.subtract, ALU.mult)
                done.then_inc(m_hn, 1)

            def output(h):
                dve.wait_ge(m_tr, h + 1)
                dve.scalar_tensor_tensor(so[:, h, :], ps[1][:], col("mnorm", h), so[:, h, :], ALU.mult, ALU.mult).then_inc(m_y, 1)

            def low(h):
                dve.wait_ge(m_hi, h + 1)
                dve.tensor_tensor(xl[:, h, :], so[:, h, :], xh[:, h, :].bitcast(F32), ALU.subtract).then_inc(m_lo, 1)

            exponents(0, 0)
            exponents(0, 1)
            for h in range(MH):
                if h:
                    normalise(h - 1)
                weighted_scores(h)
                if h:
                    dve.wait_ge(m_tr, h)
                weighted_keys(h)
                if h:
                    output(h - 1)
                states(h)
                state_queries(h, 0)
                if h:
                    low(h - 1)
                state_queries(h, 1)
                for e in range(2):
                    if h + 1 < MH:
                        exponents(h + 1, e)
                    quotient(h, e)
                statistics(h)
            normalise(MH - 1)
            split_lo(dve, gout2, 0, 0)
            output(MH - 1)
            low(MH - 1)
    mix_scope.close()

    scaled = sem("scaled")
    scaled_n = [0]

    def gated_dve(dve, g, gate, bias=None):
        base = scaled_n[0]
        scaled_n[0] += g.n if bias else 0

        def rest(i, k):
            j = 2 * i + k
            blk = x[:, bass.ds(j, 1), :].rearrange("p a n -> p (a n)")
            if bias:
                dve.tensor_scalar(blk, blk, ALPHA_2, bias(j), ALU.mult, ALU.add).then_inc(scaled, 1)
                dve.wait_ge(scaled, base + j + 1)
            dve.wait_ge(mm_done, g.base + j + 3)
            dve.scalar_tensor_tensor(blk, ps[(g.base + k) % 2][:], mod[:, gate, bass.ds(j, 1)], blk, ALU.mult, ALU.add).then_inc(acc_free, 1)
        ahead(dve, g, split_lo, rest)

    with nc.Block(no_gpsimd_drain=True) as block:
        @block.sync
        def _(sp):
            load_all(sp, gout2, after(gout2))

        @block.scalar
        def _(act):
            split_act(act, gout2)

        @block.vector
        def _(dve):
            gated_dve(dve, gout2, 2, lambda j: 0.0)

        @block.tensor
        def _(pe):
            product_pe(pe, gout2, DB, xh, xl)
    layer_norm("ln1", x, DB, lambda b: col("ln1_g", b), lambda b: col("ln1_b", b), x, split=False)
    layer_norm("mod2", x, DB, lambda b: mod[:, 4, b:b + 1], lambda b: mod[:, 3, b:b + 1], None)

    ff_scope = ExitStack()
    hh2 = sb("hh2", [P, DB, S], F32R, at=ff_scope)
    hl2 = sb("hl2", [P, DB, S], F32R, at=ff_scope)
    r_t = sb("r_t", [P, S], at=ff_scope)
    s_t = sb("s_t", [P, 2, S], at=ff_scope)
    sq_ready, s_hi, s_lo = sem("sq_ready"), sem("s_hi"), sem("s_lo")
    ff_runs = [(plan[f"ff1_{n}"], plan[f"ff2_{n}"], lo_b, hi_b) for n, (lo_b, hi_b) in enumerate(GROUPS_FF2)]
    with nc.Block(no_gpsimd_drain=True) as block:
        @block.sync
        def _(sp):
            for up, down, lo_b, hi_b in ff_runs:
                load_all(sp, up, down)
                load_all(sp, down, after(down))

        @block.tensor
        def _(pe):
            for up, down, lo_b, hi_b in ff_runs:
                def ready(b):
                    if b == 0:
                        pe.wait_ge(s_lo, hi_b - 1)
                    if b == hi_b - lo_b - 1:
                        pe.wait_ge(s_lo, hi_b)
                product_pe(pe, up, DB, xh, xl)
                product_pe(pe, down, hi_b - lo_b, hh2, hl2, ready)

        @block.scalar
        def _(act):
            for up, down, lo_b, hi_b in ff_runs:
                def rest(i, k):
                    j = 2 * i + k
                    act.wait_ge(mm_done, up.base + j + 3)
                    act.wait_ge(acc_free, up.base + j + 2)
                    act.activation(r_t[:], ps[(up.base + k) % 2][:], ACT.Relu, bias=col("b_ff1", j + lo_b)).then_inc(acc_free, 1)
                    act.wait_ge(sq_ready, j + (lo_b + 1))
                    act.activation(hh2[:, bass.ds(j, 1), :].rearrange("p a n -> p (a n)"), s_t[:, k, :], ACT.Copy).then_inc(s_hi, 1)
                ahead(act, up, split_hi, rest)
                split_act(act, down)

        @block.vector
        def _(dve):
            for n, (up, down, lo_b, hi_b) in enumerate(ff_runs):
                def rest(i, k):
                    j = 2 * i + k
                    dve.wait_ge(acc_free, up.base + j + 3)
                    dve.tensor_tensor(s_t[:, k, :], r_t[:], r_t[:], ALU.mult).then_inc(sq_ready, 1)
                    dve.wait_ge(s_hi, j + (lo_b + 1))
                    dve.tensor_tensor(hl2[:, bass.ds(j, 1), :].rearrange("p a n -> p (a n)"), s_t[:, k, :],
                                      hh2[:, bass.ds(j, 1), :].bitcast(F32).rearrange("p a n -> p (a n)"), ALU.subtract).then_inc(s_lo, 1)
                ahead(dve, up, split_lo, rest)
                gated_dve(dve, down, 5, (lambda j: gb2[:, bass.ds(j, 1)]) if n == 0 else None)
    ff_scope.close()
    layer_norm("ln2", x, DB, lambda b: col("ln2_g", b), lambda b: col("ln2_b", b), x, split=False)

    stored = sem("stored")
    with nc.Block(no_gpsimd_drain=True) as block:
        @block.sync
        def _(sp):
            for b in range(DB):
                sp.dma_start(out[:, b, :], x[:, b, :]).then_inc(stored, 16)
            sp.wait_ge(stored, 16 * DB)
    ctx.close()


def unit_layout(w):
    k, n = w.shape
    return np.ascontiguousarray(w.reshape(k // P, P, n // P, P).transpose(2, 1, 0, 3).reshape(n // P, P, k))


def feature_columns(v):
    return np.ascontiguousarray(np.reshape(v, (-1, P)).T)


def layouts(a):
    a = {k: np.asarray(v) for k, v in a.items()}
    io = {"x": np.ascontiguousarray(a["x"][0].T.reshape(DB, P, S).transpose(1, 0, 2))}
    table = {}

    def put(name, v):
        table[name] = feature_columns(v)

    def even(v):
        val, gate, bgate, rec = np.split(v, 4, axis=-1)
        parts = [np.split(t, AB, axis=-1) for t in (gate, val, rec, bgate)]
        return np.concatenate([parts[k][j] for j in range(AB) for k in range(4)], axis=-1)

    put("b_in", even(a["even_b_in"][0]))
    put("conv_w", a["even_conv_w"][0].T.reshape(AB, P, CONV_TAPS).transpose(0, 2, 1))
    put("conv_b", a["even_conv_b"])
    put("cnorm_g", a["even_cnorm_g"])
    put("cnorm_b", a["even_cnorm_b"])
    put("lru_w", a["even_lru_conv_w"][0].T.reshape(AB, P, LRU_TAPS).transpose(0, 2, 1))
    put("lru_b", a["even_lru_conv_b"])
    put("b_a", a["even_b_a"])
    put("b_x", a["even_b_x"])
    put("lam", a["even_lru_lambda"])
    for n in ("mix", "ffn"):
        put(n + "_g", a[n + "_ln_g"])
        put(n + "_b", a[n + "_ln_b"])
    put("subln_g", a["odd_subln_g"])
    for n in ("q1", "k1", "q2", "k2"):
        put("l" + n, np.pad(a["odd_lambda_" + n][0], (0, P - HEAD_DIM)))
    put("b_ada", a["b_ada_2"])
    gate_rows = np.zeros((4, 32), np.float32)
    gate_rows[:, :MH] = a["b_gate_2"][0].reshape(4, MH)[[0, 2, 1, 3]]
    put("b_gate", gate_rows)
    put("mnorm", a["mlstm_norm_w_2"])
    for n in ("ln1_g", "ln1_b", "b_ff1", "b_ff2", "ln2_g", "ln2_b"):
        put(n, a[n + "_2"])
    assert all(table[n].shape[1] == c for n, (_, c) in COLS.items()), {n: table[n].shape for n in table}
    io["cols"] = np.ascontiguousarray(np.concatenate([table[n] for n in COLS], axis=1))
    io["ident"] = np.eye(P, dtype=np.float32)
    io["w_in0"] = unit_layout(even(a["even_w_in"][0]))
    io["w_out0"] = unit_layout(np.roll(a["even_w_out"][0], D // 2, axis=0))
    for n, w in (("w_a", "even_w_a"), ("w_x", "even_w_x")):
        io[n] = np.ascontiguousarray(a[w][0].reshape(AB, 2, 64, 64).transpose(1, 2, 0, 3))
    for layer in range(2):
        io[f"w_gate{layer}"] = unit_layout(a["ffn_w_gate"][layer])
        io[f"w_up{layer}"] = unit_layout(a["ffn_w_up"][layer])
        io[f"w_down{layer}"] = unit_layout(a["ffn_w_down"][layer])
    more_layouts(a, io)
    return io


def more_layouts(a, io):
    qkv = a["odd_w_qkv"][0].reshape(D, 3, HEADS, P).transpose(0, 2, 1, 3).reshape(D, 3 * D)
    io["w_qkv"] = np.concatenate([unit_layout(np.ascontiguousarray(qkv)), unit_layout(a["odd_w_out"][0])])
    inv = np.float32(ROPE_THETA) ** (-np.arange(0, HEAD_DIM, 2, dtype=np.float32) / np.float32(HEAD_DIM))
    ang = np.tile(inv[:, None] * np.arange(S, dtype=np.float32)[None, :], (4, 1))
    sign = np.where(np.arange(P) % HEAD_DIM < HEAD_DIM // 2, -1.0, 1.0)[:, None]
    io["cos"] = np.cos(ang.astype(np.float64)).astype(np.float32)
    io["sin"] = (sign * np.sin(ang.astype(np.float64))).astype(np.float32)
    wq, wk, wv, wo, wf, wg = np.split(a["w_in_2"][0], np.cumsum([256, 256, 512, 512, 512]), axis=1)
    gate_cols = np.zeros((D, 4, 32), np.float32)
    gate_cols[:, :, :MH] = wg.reshape(D, 4, MH)[:, [0, 2, 1, 3]]
    io["w_in2"] = unit_layout(np.concatenate([wf, wq, wk, wv, wo, gate_cols.reshape(D, P)], axis=1))
    io["w_out2"] = unit_layout(a["w_out_2"][0])
    io["w_ff1"] = unit_layout(a["w_ff1_2"][0])
    io["w_ff2"] = unit_layout(a["w_ff2_2"][0])
    io["w_ada"] = np.ascontiguousarray(a["w_ada_2"][0].T).reshape(NMOD * DB, P, D)
    io["c_rows"] = np.ascontiguousarray(np.broadcast_to(a["c_2"].reshape(1, D), (P, D)))
    turn = 2.0 * np.pi * (np.outer(np.arange(S), np.arange(S)) % S) / S
    token = np.stack([unit_layout(np.cos(turn) * S ** -0.5), unit_layout(-np.sin(turn) * S ** -0.5)], axis=1)
    io["dft"] = np.ascontiguousarray(token[:NT // 2].reshape(NT, P, S).astype(np.float32))
    turn = 2.0 * np.pi * (np.outer(np.arange(P), np.arange(P)) % P) / P
    io["dft_channel"] = (np.concatenate([np.cos(turn), np.sin(turn)], axis=1) * P ** -0.5).astype(np.float32)


def kernel(**inputs):
    import concourse.bacc as bacc
    from concourse.bass_utils import run_bass_kernel_spmd as run

    nc = bacc.Bacc("TRN2", target_bir_lowering=False, num_devices=1)
    arrays = layouts(inputs)
    io = {n: nc.dram_tensor(f"in_{n}", v.shape, mybir.dt.from_np(v.dtype), kind="ExternalInput").ap() for n, v in arrays.items()}
    out = nc.dram_tensor("out", (P, DB, S), F32, kind="ExternalOutput").ap()
    program(nc, io, out)
    got = run(nc, [{f"in_{n}": v for n, v in arrays.items()}], core_ids=[0]).results[0]["out"]
    return np.ascontiguousarray(got.transpose(1, 0, 2).reshape(D, S).T)[None]
```
